# Optimizing a Trainium2 kernel written in Bass

```python
import math
import jax, jax.numpy as jnp
from jax import lax
import numpy as np

D_MODEL = 1024
BATCH = 1
SEQ = 512
DEPTH = 2

SB_HEAD_DIM = 64
SB_HEADS = D_MODEL // 128
SB_WIDTH = SB_HEADS * SB_HEAD_DIM
SB_BLOCK = 128
RET_QK_DIM = 64
RET_V_DIM = 128
RET_HEADS = D_MODEL // 256
RET_QK_WIDTH = RET_HEADS * RET_QK_DIM
RET_WIDTH = RET_HEADS * RET_V_DIM
RET_CHUNK = 64
ROPE_BASE = 10000.0
GDN_HEAD_DIM = 128
GDN_HEADS = D_MODEL // 256
GDN_WIDTH = GDN_HEADS * GDN_HEAD_DIM
GDN_QKV_WIDTH = 3 * GDN_WIDTH
GDN_CONV = 4
GDN_CHUNK = 64
N_BRANCH = 3
EPS = 1e-6
IN_SIZES = (SB_WIDTH, SB_WIDTH, SB_WIDTH, SB_WIDTH,
            RET_QK_WIDTH, RET_QK_WIDTH, RET_WIDTH, RET_WIDTH,
            GDN_QKV_WIDTH, GDN_WIDTH, GDN_HEADS, GDN_HEADS,
            N_BRANCH * D_MODEL)
IN_WIDTH = sum(IN_SIZES)

kernel_name = 'hybrid_stickbreak_retention_gdn_block'

def _rmsnorm(x, gain):
    xf = x.astype(jnp.float32)
    y = xf * lax.rsqrt(jnp.mean(xf * xf, axis=-1, keepdims=True) + EPS)
    return (y * gain.astype(jnp.float32)).astype(x.dtype)

def _head_layernorm(x):
    mu = jnp.mean(x, axis=-1, keepdims=True)
    xc = x - mu
    return xc * lax.rsqrt(jnp.mean(xc * xc, axis=-1, keepdims=True) + EPS)

def _l2norm(x):
    return x * lax.rsqrt(jnp.sum(x * x, axis=-1, keepdims=True) + EPS)

def _split_heads(x, n_heads):
    b, t, w = x.shape
    return x.reshape(b, t, n_heads, w // n_heads).transpose(0, 2, 1, 3)

def _merge_heads(x):
    b, h, t, d = x.shape
    return x.transpose(0, 2, 1, 3).reshape(b, t, h * d)

def _to_chunks(x, c):
    b, h, t = x.shape[:3]
    x = x.reshape((b, h, t // c, c) + x.shape[3:])
    return jnp.moveaxis(x, 2, 0)

def _from_chunks(x):
    n, b, h, c, d = x.shape
    return jnp.moveaxis(x, 0, 2).reshape(b, h, n * c, d)

def _rotary(x, pos):
    half = x.shape[-1] // 2
    inv_freq = ROPE_BASE ** (-jnp.arange(half, dtype=jnp.float32) / half)
    ang = pos.astype(jnp.float32)[:, None] * inv_freq[None, :]
    cos, sin = jnp.cos(ang), jnp.sin(ang)
    x1, x2 = x[..., :half], x[..., half:]
    return jnp.concatenate([x1 * cos - x2 * sin, x1 * sin + x2 * cos], axis=-1)

def _causal_conv(x, w):
    k, c = w.shape
    return lax.conv_general_dilated(
        x, w[:, None, :].astype(x.dtype), window_strides=(1,), padding=[(k - 1, 0)],
        dimension_numbers=('NWC', 'WIO', 'NWC'), feature_group_count=c)

def _stick_breaking(q, k, v):
    b, h, t, d = q.shape
    nb = t // SB_BLOCK
    qb = jnp.moveaxis((q * d ** -0.5).reshape(b, h, nb, SB_BLOCK, d), 2, 0)
    key_pos = jnp.arange(t)

    def block(args):
        q_blk, blk = args
        z = jnp.einsum('bhqd,bhkd->bhqk', q_blk, k)
        q_pos = blk * SB_BLOCK + jnp.arange(SB_BLOCK)
        valid = key_pos[None, :] < q_pos[:, None]
        log_keep = jnp.where(valid, jax.nn.log_sigmoid(-z), 0.0)
        after = lax.cumsum(log_keep, axis=3, reverse=True) - log_keep
        w = jnp.where(valid, jnp.exp(jax.nn.log_sigmoid(z) + after), 0.0)
        return jnp.einsum('bhqk,bhkd->bhqd', w, v)

    o = lax.map(block, (qb, jnp.arange(nb)))
    return jnp.moveaxis(o, 0, 2).reshape(b, h, t, d)

def _retention(q, k, v):
    c = RET_CHUNK
    b, h, _, dk = q.shape
    dv = v.shape[-1]
    log_gamma = jnp.log(1.0 - 2.0 ** (-5.0 - jnp.arange(h, dtype=jnp.float32)))
    pos = jnp.arange(c, dtype=jnp.float32)
    diff = pos[:, None] - pos[None, :]
    intra_decay = jnp.where(diff >= 0.0,
                            jnp.exp(log_gamma[:, None, None] * jnp.maximum(diff, 0.0)), 0.0)
    q_decay = jnp.exp(log_gamma[:, None] * (pos + 1.0))[:, :, None]
    k_decay = jnp.exp(log_gamma[:, None] * (c - 1.0 - pos))[:, :, None]
    chunk_decay = jnp.exp(log_gamma * c)[:, None, None]
    qc, kc, vc = _to_chunks(q, c), _to_chunks(k, c), _to_chunks(v, c)
    scores = jnp.einsum('nbhid,nbhjd->nbhij', qc, kc) * intra_decay
    intra = jnp.einsum('nbhij,nbhjv->nbhiv', scores, vc)

    def step(r, inp):
        qd_i, kd_i, v_i = inp
        o = jnp.einsum('bhck,bhkv->bhcv', qd_i, r)
        r = r * chunk_decay + jnp.einsum('bhck,bhcv->bhkv', kd_i, v_i)
        return r, o

    r0 = jnp.zeros((b, h, dk, dv), jnp.float32)
    _, inter = lax.scan(step, r0, (qc * q_decay, kc * k_decay, vc))
    return _from_chunks(intra + inter)

def _gated_delta_rule(q, k, v, g, beta):
    c = GDN_CHUNK
    b, h, _, dk = q.shape
    dv = v.shape[-1]
    qc, kc, vc = _to_chunks(q, c), _to_chunks(k, c), _to_chunks(v, c)
    gc = jnp.cumsum(_to_chunks(g, c), axis=-1)
    bc = _to_chunks(beta, c)[..., None]
    idx = jnp.arange(c)
    incl = idx[:, None] >= idx[None, :]
    strict = idx[:, None] > idx[None, :]
    decay = jnp.exp(jnp.where(incl, gc[..., :, None] - gc[..., None, :], -jnp.inf))
    kb = kc * bc
    l_mat = jnp.where(strict, jnp.einsum('nbhid,nbhjd->nbhij', kb, kc) * decay, 0.0)
    rhs = jnp.concatenate([vc * bc, kb * jnp.exp(gc)[..., None]], axis=-1)
    sol = lax.linalg.triangular_solve(l_mat, rhs, left_side=True, lower=True,
                                      unit_diagonal=True)
    u, w = sol[..., :dv], sol[..., dv:]
    scores = jnp.einsum('nbhid,nbhjd->nbhij', qc, kc) * decay
    q_dec = qc * jnp.exp(gc)[..., None]
    k_dec = kc * jnp.exp(gc[..., -1:] - gc)[..., None]
    last = jnp.exp(gc[..., -1])[..., None, None]

    def step(s, inp):
        sc_i, u_i, w_i, qd_i, kd_i, last_i = inp
        v_new = u_i - jnp.einsum('bhck,bhkv->bhcv', w_i, s)
        o = jnp.einsum('bhck,bhkv->bhcv', qd_i, s) + jnp.einsum('bhij,bhjv->bhiv', sc_i, v_new)
        s = s * last_i + jnp.einsum('bhck,bhcv->bhkv', kd_i, v_new)
        return s, o

    s0 = jnp.zeros((b, h, dk, dv), jnp.float32)
    _, o = lax.scan(step, s0, (scores, u, w, q_dec, k_dec, last))
    return _from_chunks(o)

def _hybrid_mixer(hn, w_in, conv_w, a_log, dt_bias, gdn_norm_g, w_sb, w_ret, w_gdn, w_out):
    b, t, _ = hn.shape
    dt = hn.dtype
    f32 = jnp.float32
    proj = jnp.einsum('btd,dn->btn', hn, w_in)
    split_at = np.cumsum(IN_SIZES)[:-1].tolist()
    (sb_q, sb_k, sb_v, sb_z, ret_q, ret_k, ret_v, ret_z,
     gdn_qkv, gdn_z, gdn_b, gdn_a, gate_logits) = jnp.split(proj, split_at, axis=-1)

    o_sb = _stick_breaking(_split_heads(sb_q, SB_HEADS).astype(f32),
                           _split_heads(sb_k, SB_HEADS).astype(f32),
                           _split_heads(sb_v, SB_HEADS).astype(f32))
    y_sb = _merge_heads(o_sb).astype(dt) * jax.nn.silu(sb_z)

    pos = jnp.arange(t)
    rq = _rotary(_split_heads(ret_q, RET_HEADS).astype(f32), pos)
    rk = _rotary(_split_heads(ret_k, RET_HEADS).astype(f32), pos) * RET_QK_DIM ** -0.5
    o_ret = _head_layernorm(_retention(rq, rk, _split_heads(ret_v, RET_HEADS).astype(f32)))
    y_ret = _merge_heads(o_ret).astype(dt) * jax.nn.silu(ret_z)

    qkv = jax.nn.silu(_causal_conv(gdn_qkv, conv_w))
    gq, gk, gv = jnp.split(qkv, 3, axis=-1)
    gq = _l2norm(_split_heads(gq, GDN_HEADS).astype(f32)) * GDN_HEAD_DIM ** -0.5
    gk = _l2norm(_split_heads(gk, GDN_HEADS).astype(f32))
    gv = _split_heads(gv, GDN_HEADS).astype(f32)
    beta = jax.nn.sigmoid(gdn_b.astype(f32)).transpose(0, 2, 1)
    g = (-jnp.exp(a_log.astype(f32))
         * jax.nn.softplus(gdn_a.astype(f32) + dt_bias.astype(f32))).transpose(0, 2, 1)
    o_gdn = _rmsnorm(_gated_delta_rule(gq, gk, gv, g, beta), gdn_norm_g)
    y_gdn = _merge_heads(o_gdn).astype(dt) * jax.nn.silu(gdn_z)

    gates = jax.nn.sigmoid(gate_logits.astype(f32)).astype(dt).reshape(b, t, N_BRANCH, D_MODEL)
    merged = (gates[:, :, 0] * jnp.einsum('btw,wd->btd', y_sb, w_sb)
              + gates[:, :, 1] * jnp.einsum('btw,wd->btd', y_ret, w_ret)
              + gates[:, :, 2] * jnp.einsum('btw,wd->btd', y_gdn, w_gdn))
    return jnp.einsum('btd,de->bte', merged, w_out)

def setup_inputs(seed: int = 0) -> dict:
    key = jax.random.key(seed)
    ks = jax.random.split(key, 12)
    f32 = jnp.float32
    x = jax.random.normal(ks[0], (BATCH, SEQ, D_MODEL), f32)
    norm_g = 1.0 + 0.02 * jax.random.normal(ks[1], (DEPTH, D_MODEL), f32)
    w_in = jax.random.normal(ks[2], (DEPTH, D_MODEL, IN_WIDTH), f32) * D_MODEL ** -0.5
    conv_w = jax.random.normal(ks[3], (DEPTH, GDN_CONV, GDN_QKV_WIDTH), f32) * GDN_CONV ** -0.5
    a_log = jnp.log(jax.random.uniform(ks[4], (DEPTH, GDN_HEADS), f32, 1.0, 16.0))
    dt0 = jnp.exp(jax.random.uniform(ks[5], (DEPTH, GDN_HEADS), f32,
                                     math.log(1e-3), math.log(1e-1)))
    dt_bias = dt0 + jnp.log(-jnp.expm1(-dt0))
    gdn_norm_g = 1.0 + 0.02 * jax.random.normal(ks[6], (DEPTH, GDN_HEAD_DIM), f32)
    w_sb = jax.random.normal(ks[7], (DEPTH, SB_WIDTH, D_MODEL), f32) * SB_WIDTH ** -0.5
    w_ret = jax.random.normal(ks[8], (DEPTH, RET_WIDTH, D_MODEL), f32) * RET_WIDTH ** -0.5
    w_gdn = jax.random.normal(ks[9], (DEPTH, GDN_WIDTH, D_MODEL), f32) * GDN_WIDTH ** -0.5
    w_out = jax.random.normal(ks[10], (DEPTH, D_MODEL, D_MODEL), f32) * D_MODEL ** -0.5
    final_g = 1.0 + 0.02 * jax.random.normal(ks[11], (D_MODEL,), f32)
    return {'x': x, 'norm_g': norm_g, 'w_in': w_in, 'conv_w': conv_w, 'a_log': a_log,
            'dt_bias': dt_bias, 'gdn_norm_g': gdn_norm_g, 'w_sb': w_sb, 'w_ret': w_ret,
            'w_gdn': w_gdn, 'w_out': w_out, 'final_g': final_g}

def reference(x, norm_g, w_in, conv_w, a_log, dt_bias, gdn_norm_g, w_sb, w_ret, w_gdn,
              w_out, final_g):
    for layer in range(DEPTH):
        hn = _rmsnorm(x, norm_g[layer])
        x = x + _hybrid_mixer(hn, w_in[layer], conv_w[layer], a_log[layer], dt_bias[layer],
                              gdn_norm_g[layer], w_sb[layer], w_ret[layer], w_gdn[layer],
                              w_out[layer])
    return _rmsnorm(x, final_g)


_drawn_inputs = setup_inputs


def setup_inputs(seed=0):
    import zlib

    import numpy as np

    out = dict(_drawn_inputs(seed))
    spreads = {}
    factors = {'gdn_norm_g': 6.562, 'final_g': 2.824}
    for name, (base, spread) in spreads.items():
        noise = np.random.default_rng([zlib.crc32(name.encode()), seed]).standard_normal(out[name].shape)
        drawn = base * np.exp(spread * noise) if base else spread * noise
        out[name] = __import__('jax').numpy.asarray(drawn.astype(out[name].dtype))
    for name, factor in factors.items():
        out[name] = (out[name] * factor).astype(out[name].dtype)
    return out
```

```python
import math

import numpy as np
import concourse.bass as bass
from concourse import mybir
from contextlib import ExitStack

F32 = mybir.dt.float32
F32R = mybir.dt.float32r
ALU = mybir.AluOpType
ACT = mybir.ActivationFunctionType

P = 128
D = 1024
T = 512
DEPTH = 2
KB = D // P
TB = T // P
SBH, SBD = 8, 64
RH = 4
GH = 4
EPS = 1e-6
TILE = 1024
RAW = 2
OFF = dict(sbq=0, sbk=512, sbv=1024, sbz=1536, rq=2048, rk=2304, rv=2560, rz=3072,
           gqkv=3584, gz=5120, gab=5632, gate=5640)
LEVELS = 7
LN_EXP = "natural_log_exp_and_others"
NEG = -1e30


def weight_plan():
    plan = [("sbq", i) for i in range(4)] + [("sbk", i) for i in range(4)]
    plan += [("sbv", i) for i in range(4)] + [("sbz", i) for i in range(4)]
    plan += [("rq", i) for i in range(2)] + [("rk", i) for i in range(2)]
    plan += [("rv", i) for i in range(4)] + [("rz", i) for i in range(4)]

    def branch(b):
        out = []
        for g in range(4):
            out += [("gate", 8 * b + 2 * g), ("gate", 8 * b + 2 * g + 1), ("branch", 4 * b + g)]
        return out

    plan += branch(0)
    plan += [("gqkv", i) for i in range(12)] + [("gz", i) for i in range(4)]
    plan += branch(1) + branch(2)
    plan += [("wout", i) for i in range(8)]
    return plan


PLAN = weight_plan()
NTILES = len(PLAN)
FIRST = {what: next(i for i, (w, _) in enumerate(PLAN) if w == what) for what, _ in PLAN}
SB_OUT, RET_OUT, GDN_OUT = (next(i for i, x in enumerate(PLAN) if x == ("gate", 8 * b)) for b in range(3))
ON_VECTOR = ("sbz", "rz", "gz", "branch")


def block_table():
    first, taken, counts = [], [], {"act": 0, "dve": 0, "x": 0}
    for what, _ in PLAN:
        first.append(len(taken))
        for _ in range(2 if what == "branch" else 1):
            who = "x" if what == "wout" else "dve" if what in ON_VECTOR else "act"
            counts[who] += 1
            taken.append((who, counts[who]))
    return first, taken, counts


BLOCK, TAKEN, COUNTS = block_table()

UNITS = [[(3, 0), (2, 128)], [(1, 0)], [(0, 0)]]
WIDTH = {kb: T - P * kb for kb in range(TB)}
SP_AT = {3: 0, 2: 128, 1: 384, 0: 768}
UNIT_AT = [0, 384, 768]
UNIT_W = [384, 384, 512]

CONST = ["triu", "ident", "ntril", "nones", "ones", "rot", "negsb", "neggdn", "m1t"]
CC = {n: P * i for i, n in enumerate(CONST)}
C_LEVEL = P * len(CONST)
C_DIFF = C_LEVEL + P * LEVELS
C_COS = C_DIFF + T
C_SIN = C_COS + T
C_END = C_SIN + T
PAR = dict(norm=0, conv=8, gain=56, dtb=57, alog=73)
PAR_END = 89


def constants():
    i = np.arange(P)
    r, c = i[:, None], i[None, :]
    out = np.zeros((P, C_END), np.float32)

    def put(name, a):
        out[:, CC[name]:CC[name] + P] = a

    put("triu", r <= c)
    put("ident", r == c)
    put("ntril", -(r >= c).astype(np.float32))
    put("nones", -1.0)
    put("ones", 1.0)
    src = np.where(c % 64 < 32, c + 32, c - 32)
    put("rot", np.where(r == src, np.where(c % 64 < 32, -1.0, 1.0), 0.0))
    put("negsb", np.where(r >= c, NEG, 0.0))
    put("neggdn", np.where(r > c, NEG, 0.0))

    def level(s):
        return ((r // (2 * s) == c // (2 * s)) & ((r // s) % 2 == 1) & ((c // s) % 2 == 0)).astype(np.float32)

    put("m1t", level(1).T)
    for n in range(LEVELS):
        out[:, C_LEVEL + P * n:C_LEVEL + P * (n + 1)] = level(1 << n)
    t = np.arange(T)[None, :]
    out[:, C_DIFF:C_DIFF + T] = np.where(t >= r, t - r, 1e9)
    freq = (np.float32(10000.0) ** (-(np.arange(32, dtype=np.float32)) / np.float32(32)))
    ang = t.astype(np.float32) * freq[(i % 32)][:, None]
    out[:, C_COS:C_COS + T] = np.cos(ang.astype(np.float32))
    out[:, C_SIN:C_SIN + T] = np.sin(ang.astype(np.float32))
    return out


def trunk(nc, xin, wt, wab, par, fin, cst, out):
    ctx = ExitStack()
    sigs = []
    nc.disable_value_cache = True

    class Signal:

        def __init__(self, name, per_layer):
            self.sem = ctx.enter_context(nc.semaphore(name))
            self.name, self.per_layer, self.n = name, per_layer, 0
            sigs.append(self)

        def __call__(self, l, n):
            return self.sem, l * self.per_layer + n

        def up(self, by=1):
            self.n += by
            return self.sem, by

    with ctx:
        def sb(name, shape, dt=F32):
            return ctx.enter_context(nc.sbuf_tensor(name, shape, dt))

        x = sb("x", [P, KB, T])
        hnh = sb("hnh", [P, KB, T], F32R)
        hnl = sb("hnl", [P, KB, T], F32R)
        wraw = sb("wraw", [P, RAW, TILE])
        whi = sb("whi", [P, 2, TILE], F32R)
        wlo = sb("wlo", [P, 2, TILE], F32R)
        con = sb("con", [P, C_END])
        conr = sb("conr", [P, 3, P], F32R)
        prm = sb("prm", [P, PAR_END])
        fing = sb("fing", [P, KB])
        eps = sb("eps", [P, 1])
        mrg = sb("mrg", [P, KB, T])
        yh = sb("yh", [P, 4, T], F32R)
        yl = sb("yl", [P, 4, T], F32R)
        zA = sb("zA", [P, 4, T])
        zB = sb("zB", [P, 4, T])
        tg = sb("tg", [P, 2, T])
        abw = sb("abw", [P, KB * 8])
        abh = sb("abh", [P, KB, 8], F32R)
        abl = sb("abl", [P, KB, 8], F32R)
        sm = sb("sm", [P, 16, 16])
        gel = sb("gel", [P, GH, TB])
        arena = sb("arena", [P, 16896])
        pj = [ctx.enter_context(nc.psum_tensor(f"pj{i}", [P, T], F32)) for i in range(2)]
        mx = [ctx.enter_context(nc.psum_tensor(f"mx{i}", [P, T], F32)) for i in range(6)]

        def area(at, *shape):
            n = int(np.prod(shape))
            v = arena[:, at:at + n]
            if len(shape) == 2:
                v = v.rearrange("p (a b) -> p a b", a=shape[0])
            if len(shape) == 3:
                v = v.rearrange("p (a b c) -> p a b c", a=shape[0], b=shape[1])
            return v

        def const(name):
            return con[:, CC[name]:CC[name] + P]

        ident = const("ident")
        ident_r, negsb_r, neggdn_r = (conr[:, i, :] for i in range(3))
        diff = con[:, C_DIFF:C_DIFF + T]
        cos, sin = con[:, C_COS:C_COS + T], con[:, C_SIN:C_SIN + T]

        sq = area(0, KB, T)
        rstd = area(4096, T)
        sbq, sbk = area(0, 4, T), area(2048, 4, T)
        vpad = area(4096, TB, SBH, P)
        sbe, sbsp, sbw = area(8192, 2, T), area(9216, 2, 1280), area(11776, 2, T)
        rraw, rv = area(12800, 4, T), area(14848, TB, T)
        rrot, rdec, rsc = area(0, 4, T), area(2048, 2, T), area(3072, 2, 1280)
        ro, rsq, rrs, rtmp = area(5632, 2, T), area(6656, 2, T), area(7680, 2, T), area(8704, 2, T)
        gq, gk, gv = area(0, GH, T), area(2048, GH, T), area(4096, GH, T)
        kbg, gX, gXT = area(6144, GH, T), area(8192, GH, T), area(10240, GH, T)
        gLT, gsc = area(12288, GH, T), area(14336, GH, T)
        gS = area(16384, GH, P)
        cin, cacc = area(8192, 2, 516), area(10240, 2, T)
        gqkv = area(0, 12, T)
        ed = zB

        def blk(ap):
            return ap.rearrange("p (a b) -> p a b", a=TB)

        def S(name, n):
            return Signal(name, n)

        consts_in = ctx.enter_context(nc.semaphore("consts_in"))
        consts_up = ctx.enter_context(nc.semaphore("consts_up"))
        w_in = [ctx.enter_context(nc.semaphore(f"w_in{i}")) for i in range(RAW)]
        out_done = ctx.enter_context(nc.semaphore("out_done"))
        x_new = S("x_new", 16)
        w_hi = S("w_hi", NTILES)
        w_lo = S("w_lo", NTILES)
        blocks = S("blocks", 2 * NTILES)
        act_took = S("act_took", COUNTS["act"])
        dve_took = S("dve_took", COUNTS["dve"])
        params_in = S("params_in", 32)
        norm_sq, norm_sum, norm_ln, norm_rs = S("norm_sq", 8), S("norm_sum", 1), S("norm_ln", 1), S("norm_rs", 1)
        norm_t, hn_hi, hn_lo = S("norm_t", 8), S("hn_hi", 8), S("hn_lo", 8)
        ab_hi, ab_lo = S("ab_hi", 1), S("ab_lo", 1)
        sb_zero = S("sb_zero", 1)
        silu_a, silu_b = S("silu_a", 2), S("silu_b", 1)
        NU = SBH * 3
        sb_z, sb_e, sb_l, sb_min, sb_sp = S("sb_z", NU), S("sb_e", NU), S("sb_l", NU), S("sb_min", NU), S("sb_sp", NU)
        sb_s, sb_w, sb_o, sb_oo = S("sb_s", NU), S("sb_w", NU), S("sb_o", NU), None
        y_ready, y_hi, y_lo = S("y_ready", 12), S("y_hi", 12), S("y_lo", 12)
        rr, rt1, rt2, rrd = S("rr", 4), S("rt1", 4), S("rt2", 4), S("rrd", 4)
        r_dec, r_scores, r_sc, r_o = S("r_dec", RH), S("r_scores", RH * 3), S("r_sc", RH * 3), S("r_o", RH)
        r_os, r_mu, r_xc, r_sq = S("r_os", RH), S("r_mu", RH), S("r_xc", RH), S("r_sq", RH)
        r_var, r_ln, r_rs, r_y = S("r_var", RH), S("r_ln", RH), S("r_rs", RH), S("r_y", RH)
        mrg_acc = S("mrg_acc", 16)
        g_pad = S("g_pad", 1)
        g_cv, g_silu = S("g_cv", 48), S("g_silu", 12)
        g_ab, g_s1, g_s2, g_s3, g_gc = S("g_ab", 1), S("g_s1", 3), S("g_s2", 4), S("g_s3", 4), S("g_gc", 1)
        g_s4, g_s5 = S("g_s4", 1), S("g_s5", 2)
        g_sq, g_ss, g_ln, g_rs, g_nrm = S("g_sq", 8), S("g_ss", 8), S("g_ln", 8), S("g_rs", 8), S("g_nrm", 8)
        g_x, g_E, g_gl, g_kd0, g_kds = S("g_x", GH), S("g_E", GH), S("g_gl", GH), S("g_kd0", GH), S("g_kds", GH)
        g_xm, g_dec = S("g_xm", GH), S("g_dec", GH)
        g_bb, g_kk, g_qk, g_kt, g_vt = S("g_bb", GH), S("g_kk", GH), S("g_qk", GH), S("g_kt", GH), S("g_vt", GH)
        g_prep = S("g_prep", GH * 8)
        g_P, g_Pm = S("g_P", LEVELS * GH), S("g_Pm", LEVELS * GH)
        g_AB = S("g_AB", (LEVELS - 1) * GH)
        g_X = S("g_X", (LEVELS - 1) * GH)
        g_XT = S("g_XT", (LEVELS + 1) * GH)
        g_wt, g_wts = S("g_wt", GH), S("g_wts", GH)
        g_v, g_vn, g_o, g_s, g_s0, g_su = S("g_v", TB), S("g_vn", TB), S("g_o", TB), S("g_s", TB - 1), S("g_s0", TB - 2), S("g_su", TB - 1)
        n_sq, n_ss, n_ln, n_rs, n_t = S("n_sq", GH), S("n_ss", GH), S("n_ln", GH), S("n_rs", GH), S("n_t", GH)
        m_hi, m_lo = S("m_hi", 8), S("m_lo", 8)

        def by(who):
            return {"act": act_took, "dve": dve_took, "x": x_new}[who]

        block = ctx.enter_context(nc.Block())

        @block.sync
        def _(sp):
            sp.dma_start(x[:, :, :], xin).then_inc(x_new.sem, 16)
            sp.dma_start(con[:, :], cst).then_inc(consts_in, 16)
            sp.dma_start(fing[:, :], fin).then_inc(consts_in, 16)
            for i in range(RAW):
                sp.dma_start(wraw[:, i, :], wt[0, i, :, :]).then_inc(w_in[i], 16)
            with sp.Fori(1, DEPTH * NTILES // RAW) as r:
                for i in range(RAW):
                    sp.wait_ge(w_lo.sem, RAW * r + (i - RAW + 1))
                    sp.dma_start(wraw[:, i, :], wt[r, i, :, :]).then_inc(w_in[i], 16)
            for kb in range(KB):
                sp.wait_ge(*norm_t(DEPTH, kb + 1))
                sp.dma_start(out[:, kb, :], sq[:, kb, :]).then_inc(out_done, 16)
            sp.wait_ge(out_done, 16 * KB)

        @block.gpsimd
        def _(pool):
            def split(g, i):
                pool.wait_ge(w_hi.sem, g + 1)
                nc.gpsimd.tensor_tensor(wlo[:, i, :], wraw[:, i, :], whi[:, i, :], ALU.subtract).then_inc(w_lo.sem, 1)

            for i in range(2):
                split(i, i)
            with pool.Fori(1, DEPTH * NTILES // 2) as r:
                for i in range(2):
                    pool.wait_ge(blocks.sem, 4 * r + (2 * i - 2))
                    split(2 * r + i, i)

        @block.scalar
        def _(act):
            def cp(dst, src, scale=1.0):
                return act.activation(dst, src, ACT.Copy, scale=scale)

            act.wait_ge(consts_in, 32)
            for i, n in enumerate(("ident", "negsb", "neggdn")):
                cp(conr[:, i, :], const(n)).then_inc(consts_up, 1)

            def norm_sums(l):
                act.wait_ge(*x_new(l, 16))
                for kb in range(KB):
                    act.activation(sq[:, kb, :], x[:, kb, :], ACT.Square).then_inc(*norm_sq.up())
                act.wait_ge(*norm_sum(l, 1))
                act.activation(rstd, mx[0][:, :], ACT.Ln, bias=eps[:, :], scale=1.0 / D).then_inc(*norm_ln.up())
                act.wait_ge(*norm_ln(l, 1))
                act.activation(rstd, rstd, ACT.Exp, scale=-0.5).then_inc(*norm_rs.up())

            with act.Fori(0, DEPTH) as l:
                def hi(t):
                    if t >= 2:
                        act.wait_ge(*blocks(l, 2 * (t - 1)))
                    act.wait_ge(w_in[t % RAW], l * (16 * (NTILES // RAW)) + 16 * (t // RAW + 1))
                    cp(whi[:, t % 2, :], wraw[:, t % RAW, :]).then_inc(*w_hi.up())

                def ahead(t):
                    if t + 2 < NTILES:
                        hi(t + 2)

                def came(t, b=0):
                    act.wait_ge(*blocks(l, 2 * t + 2 if PLAN[t][0] != "branch" else 2 * t + 1 + b))
                    return pj[(BLOCK[t] + b) % 2]

                act.wait_ge(*x_new(l, 16))
                act.dma_start(prm[:, :], par[l, :, :]).then_inc(*params_in.up(16))
                act.dma_start(abw[:, :], wab[l, :, :]).then_inc(*params_in.up(16))
                hi(0)
                hi(1)
                act.preload_act_table_set(LN_EXP)
                norm_sums(l)
                for kb in range(KB):
                    act.wait_ge(*norm_t(l, kb + 1))
                    cp(hnh[:, kb, :], sq[:, kb, :]).then_inc(*hn_hi.up())
                cp(abh[:, :, :], abw[:, :].rearrange("p (k c) -> p k c", k=KB)).then_inc(*ab_hi.up())

                for t in range(0, 16):
                    what, i = PLAN[t]
                    if what != "sbz":
                        bank = came(t)
                        if what == "sbq":
                            if t == 0:
                                act.wait_ge(*hn_lo(l, 8))
                            cp(sbq[:, i, :], bank[:, :], scale=SBD ** -0.5).then_inc(*act_took.up())
                        elif what == "sbk":
                            cp(sbk[:, i, :], bank[:, :]).then_inc(*act_took.up())
                        else:
                            if i == 0:
                                act.wait_ge(*sb_zero(l, 1))
                            v = blk(bank[:, :])
                            cp(vpad[:, :, 2 * i, 0:64], v[:, :, 0:64])
                            cp(vpad[:, :, 2 * i + 1, 64:128], v[:, :, 64:128]).then_inc(*act_took.up())
                    ahead(t)

                def take(t):
                    what, i = PLAN[t]
                    if what in ("rq", "rk"):
                        j = i + (2 if what == "rk" else 0)
                        cp(rraw[:, j, :], came(t)[:, :], scale=0.125 if what == "rk" else 1.0).then_inc(*act_took.up())
                    elif what == "rv":
                        cp(rv[:, :, i * P:(i + 1) * P], blk(came(t)[:, :])).then_inc(*act_took.up())
                    elif what == "gate":
                        if i >= 10:
                            act.wait_ge(*mrg_acc(l, i - 9))
                        elif i >= 2:
                            n = BLOCK[SB_OUT + 3 * ((i - 2) // 2) + 2] + i % 2
                            act.wait_ge(*dve_took(l, TAKEN[n][1]))
                        act.activation(tg[:, i % 2, :], came(t)[:, :], ACT.Tanh, scale=0.5).then_inc(*act_took.up())
                    ahead(t)

                act.wait_ge(*dve_took(l, 4))
                act.activation(zA[:, :, :], zA[:, :, :], ACT.Silu).then_inc(*silu_a.up())
                act.preload_act_table_set(LN_EXP)

                def sb_softplus(u):
                    j = u % 3
                    e = sbe[:, u % 2, 0:UNIT_W[j]]
                    act.wait_ge(*sb_min(l, u + 1))
                    act.activation(e, e, ACT.Exp).then_inc(*sb_e.up())
                    act.wait_ge(*sb_e(l, u + 1))
                    act.activation(e, e, ACT.Ln, bias=1.0).then_inc(*sb_l.up())

                def sb_weights(u):
                    j = u % 3
                    act.wait_ge(*sb_s(l, u + 1))
                    if u >= 2:
                        act.wait_ge(*sb_o(l, u - 1))
                    act.activation(sbw[:, u % 2, 0:UNIT_W[j]], mx[u % 5][:, 0:UNIT_W[j]], ACT.Exp).then_inc(*sb_w.up())

                for u in range(NU + 1):
                    if u < NU:
                        sb_softplus(u)
                    if u >= 1:
                        sb_weights(u - 1)
                    if u % 2 == 1:
                        take(16 + u // 2)

                def y_split(b, i, src, n):
                    act.wait_ge(*y_ready(l, n + 1))
                    cp(yh[:, i, :], src).then_inc(*y_hi.up())

                for c in range(4):
                    y_split(0, c, zA[:, c, :], c)

                act.wait_ge(*dve_took(l, 8))
                act.activation(zB[:, :, :], zB[:, :, :], ACT.Silu).then_inc(*silu_b.up())
                for h in range(RH):
                    act.preload_act_table_set(LN_EXP)
                    if h >= 2:
                        act.wait_ge(*r_sc(l, 3 * (h - 1)))
                    if h == 0:
                        act.wait_ge(*sb_s(l, NU))
                    act.activation(rdec[:, h % 2, :], diff, ACT.Exp,
                                   scale=math.log(1.0 - 2.0 ** (-5.0 - h))).then_inc(*r_dec.up())
                    take(SB_OUT + 3 * h)
                    take(SB_OUT + 3 * h + 1)
                    act.preload_act_table_set(LN_EXP)
                    act.wait_ge(*r_o(l, h + 1))
                    if h >= 2:
                        act.wait_ge(*r_y(l, h - 1))
                    cp(ro[:, h % 2, :], mx[3 + h % 2][:, :]).then_inc(*r_os.up())
                    act.wait_ge(*r_xc(l, h + 1))
                    act.activation(rsq[:, h % 2, :], ro[:, h % 2, :], ACT.Square).then_inc(*r_sq.up())
                    act.wait_ge(*r_var(l, h + 1))
                    act.activation(rrs[:, h % 2, :], mx[5][:, :], ACT.Ln, bias=eps[:, :], scale=1.0 / P).then_inc(*r_ln.up())
                    act.wait_ge(*r_ln(l, h + 1))
                    act.activation(rrs[:, h % 2, :], rrs[:, h % 2, :], ACT.Exp, scale=-0.5).then_inc(*r_rs.up())
                    ahead(SB_OUT + 3 * h + 2)
                act.wait_ge(*blocks(l, 2 * (SB_OUT + 12)))
                for c in range(4):
                    y_split(1, c, zB[:, c, :], 4 + c)

                for t in range(FIRST["gqkv"], FIRST["gqkv"] + 12):
                    i = t - FIRST["gqkv"]
                    bank = came(t)
                    if i == 0:
                        act.wait_ge(*g_pad(l, 1))
                    if i >= 2:
                        act.wait_ge(*g_cv(l, 4 * (i - 1)))
                    cp(cin[:, i % 2, 3:3 + T], bank[:, :]).then_inc(*act_took.up())
                    ahead(t)
                    if i >= 1:
                        act.wait_ge(*g_cv(l, 4 * i))
                        act.activation(gqkv[:, i - 1, :], cacc[:, (i - 1) % 2, :], ACT.Silu).then_inc(*g_silu.up())
                act.wait_ge(*g_cv(l, 48))
                act.activation(gqkv[:, 11, :], cacc[:, 1, :], ACT.Silu).then_inc(*g_silu.up())
                act.preload_act_table_set(LN_EXP)
                act.wait_ge(*g_s1(l, 3))
                act.activation(sm[:, 3, :], sm[:, 1, :], ACT.Exp).then_inc(*g_s2.up())
                act.activation(sm[:, 4, :], sm[:, 2, :], ACT.Exp).then_inc(*g_s2.up())
                act.activation(sm[:, 5, :], prm[:, PAR["alog"]:PAR["alog"] + 16], ACT.Exp).then_inc(*g_s2.up())
                act.wait_ge(*g_s2(l, 1))
                act.activation(sm[:, 3, :], sm[:, 3, :], ACT.Ln, bias=1.0).then_inc(*g_s2.up())
                act.wait_ge(*g_s5(l, 1))
                act.activation(sm[:, 9, :], mx[1][:, 0:16], ACT.Exp).then_inc(*g_s4.up())
                for t in range(FIRST["gz"], FIRST["gz"] + 4):
                    ahead(t)
                for n in range(8):
                    act.wait_ge(*g_silu(l, n + 1))
                    if n >= 2:
                        act.wait_ge(*g_ss(l, n - 1))
                    act.activation(ed[:, n % 2, :], gqkv[:, n, :], ACT.Square).then_inc(*g_sq.up())
                    act.wait_ge(*g_ss(l, n + 1))
                    if n >= 2:
                        act.wait_ge(*g_nrm(l, n - 1))
                    act.activation(ed[:, 2 + n % 2, :], mx[2 + n % 2][:, :], ACT.Ln, bias=eps[:, :]).then_inc(*g_ln.up())
                    act.wait_ge(*g_ln(l, n + 1))
                    act.activation(ed[:, 2 + n % 2, :], ed[:, 2 + n % 2, :], ACT.Exp, scale=-0.5).then_inc(*g_rs.up())
                act.wait_ge(*g_nrm(l, 8))
                for h in range(GH):
                    act.wait_ge(*g_x(l, h + 1))
                    if h >= 2:
                        act.wait_ge(*g_prep(l, 8 * (h - 1)))
                    act.activation(ed[:, h % 2, :], mx[0][:, :], ACT.Exp).then_inc(*g_E.up())
                    act.wait_ge(*g_kd0(l, h + 1))
                    act.activation(sm[:, 11, 4 * h:4 * h + 4], sm[:, 12, 4 * h:4 * h + 4], ACT.Exp).then_inc(*g_kds.up())
                    act.wait_ge(*g_xm(l, h + 1))
                    for tb in range(TB):
                        a = act.activation(ed[:, 2 + h % 2, tb * P:(tb + 1) * P], mx[0][:, tb * P:(tb + 1) * P], ACT.Exp,
                                           bias=sm[:, 8, 4 * h + tb:4 * h + tb + 1])
                    a.then_inc(*g_dec.up())
                for lv in range(LEVELS):
                    for half in range(2):
                        f = 2 * lv + half
                        if f < 12:
                            take(RET_OUT + f) if PLAN[RET_OUT + f][0] == "gate" else ahead(RET_OUT + f)
                for h in range(GH):
                    act.wait_ge(*g_wt(l, h + 1))
                    cp(gLT[:, h, :], mx[2 + h % 2][:, :], scale=-1.0).then_inc(*g_wts.up())
                for tb in range(TB):
                    act.wait_ge(*g_v(l, tb + 1))
                    if tb >= 1:
                        act.wait_ge(*g_o(l, tb))
                        act.wait_ge(*g_s(l, tb))
                    cp(ed[:, 2, :], mx[0][:, :]).then_inc(*g_vn.up())
                act.wait_ge(*dve_took(l, TAKEN[BLOCK[FIRST["gz"] + 3]][1]))
                act.activation(zA[:, :, :], zA[:, :, :], ACT.Silu).then_inc(*silu_a.up())
                act.preload_act_table_set(LN_EXP)
                for h in range(GH):
                    act.wait_ge(*g_o(l, TB))
                    if h >= 2:
                        act.wait_ge(*n_ss(l, h - 1))
                    act.activation(ed[:, h % 2, :], mx[2 + h][:, :], ACT.Square).then_inc(*n_sq.up())
                    act.wait_ge(*n_ss(l, h + 1))
                    if h >= 2:
                        act.wait_ge(*n_t(l, h - 1))
                    if h == 0:
                        act.wait_ge(*g_o(l, TB))
                    act.activation(ed[:, 2 + h % 2, :], mx[h % 2][:, :], ACT.Ln, bias=eps[:, :], scale=1.0 / P).then_inc(*n_ln.up())
                    act.wait_ge(*n_ln(l, h + 1))
                    act.activation(ed[:, 2 + h % 2, :], ed[:, 2 + h % 2, :], ACT.Exp, scale=-0.5).then_inc(*n_rs.up())
                act.wait_ge(*blocks(l, 2 * (RET_OUT + 12)))
                for h in range(GH):
                    y_split(2, h, zA[:, h, :], 8 + h)
                for f in range(12):
                    take(GDN_OUT + f) if PLAN[GDN_OUT + f][0] == "gate" else ahead(GDN_OUT + f)
                act.wait_ge(*blocks(l, 2 * (GDN_OUT + 12)))
                for kb in range(KB):
                    act.wait_ge(*mrg_acc(l, 8 + kb + 1))
                    cp(hnh[:, kb, :], mrg[:, kb, :], scale=0.5).then_inc(*m_hi.up())
                for t in range(FIRST["wout"], NTILES):
                    ahead(t)

            act.preload_act_table_set(LN_EXP)
            norm_sums(DEPTH)

        @block.vector
        def _(dve):
            dve.memset(eps[:, :], EPS).then_inc(consts_up, 1)

            def norm_scale(l, g, kb):
                dve.scalar_tensor_tensor(out=sq[:, kb, :], in0=x[:, kb, :], scalar=g, in1=rstd,
                                         op0=ALU.mult, op1=ALU.mult).then_inc(*norm_t.up())

            with dve.Fori(0, DEPTH) as l:
                def came(t, b=0):
                    dve.wait_ge(*blocks(l, 2 * t + 2 if PLAN[t][0] != "branch" else 2 * t + 1 + b))
                    return pj[(BLOCK[t] + b) % 2]

                dve.wait_ge(*norm_rs(l, 1))
                dve.wait_ge(*params_in(l, 32))

                def hn_low(kb):
                    dve.wait_ge(*hn_hi(l, kb + 1))
                    dve.tensor_tensor(hnl[:, kb, :], sq[:, kb, :], hnh[:, kb, :], ALU.subtract).then_inc(*hn_lo.up())

                for kb in range(KB):
                    norm_scale(l, prm[:, PAR["norm"] + kb:PAR["norm"] + kb + 1], kb)
                    if kb >= 1:
                        hn_low(kb - 1)
                hn_low(KB - 1)
                dve.wait_ge(*hn_lo(l, 8))
                dve.memset(area(4096, 4096), 0.0).then_inc(*sb_zero.up())
                dve.wait_ge(*ab_hi(l, 1))
                dve.tensor_tensor(abl[:, :, :], abw[:, :].rearrange("p (k c) -> p k c", k=KB), abh[:, :, :],
                                  ALU.subtract).then_inc(*ab_lo.up())

                def take_z(t, dst):
                    bank = came(t)
                    dve.tensor_copy(dst[:, PLAN[t][1], :], bank[:, :]).then_inc(*dve_took.up())

                for t in range(12, 16):
                    take_z(t, zA)

                def sb_clamp(u):
                    j = u % 3
                    dve.wait_ge(*sb_z(l, u + 1))
                    if u >= 2:
                        dve.wait_ge(*sb_sp(l, u - 1))
                    dve.tensor_scalar(sbe[:, u % 2, 0:UNIT_W[j]], mx[u % 5][:, 0:UNIT_W[j]], 40.0, None, ALU.min)\
                       .then_inc(*sb_min.up())

                def sb_softplus(u):
                    j, h = u % 3, u // 3
                    dve.wait_ge(*sb_l(l, u + 1))
                    if h >= 2:
                        dve.wait_ge(*sb_s(l, 3 * (h - 1)))
                    dve.tensor_tensor(sbsp[:, h % 2, UNIT_AT[j]:UNIT_AT[j] + UNIT_W[j]], sbe[:, u % 2, 0:UNIT_W[j]],
                                      mx[u % 5][:, 0:UNIT_W[j]], ALU.max).then_inc(*sb_sp.up())

                def y_low(i, src, n):
                    dve.wait_ge(*y_hi(l, n + 1))
                    dve.tensor_tensor(yl[:, i, :], src, yh[:, i, :], ALU.subtract).then_inc(*y_lo.up())

                for u in range(NU + 1):
                    if u < NU:
                        sb_clamp(u)
                    if u >= 1:
                        sb_softplus(u - 1)
                    if u >= 8 and u % 6 == 2:
                        c = u // 6 - 1
                        dve.wait_ge(*sb_o(l, 6 * c + 6))
                        if c == 0:
                            dve.wait_ge(*silu_a(l, 1))
                        dve.tensor_tensor(zA[:, c, :], mx[5][:, :], zA[:, c, :], ALU.mult).then_inc(*y_ready.up())
                    if u % 2 == 1 and PLAN[16 + u // 2][0] == "rz":
                        take_z(16 + u // 2, zB)
                dve.wait_ge(*sb_o(l, NU))
                dve.tensor_tensor(zA[:, 3, :], mx[5][:, :], zA[:, 3, :], ALU.mult).then_inc(*y_ready.up())
                for c in range(4):
                    y_low(c, zA[:, c, :], c)

                def take_branch(t, b):
                    for i in range(2):
                        d = 2 * (PLAN[t][1] % 4) + i
                        bank = came(t, i)
                        dve.wait_ge(*act_took(l, TAKEN[BLOCK[t - 2 + i]][1]))
                        if b == 0:
                            dve.scalar_tensor_tensor(out=mrg[:, d, :], in0=tg[:, i, :], scalar=1.0, in1=bank[:, :],
                                                     op0=ALU.add, op1=ALU.mult).then_inc(*dve_took.up())
                            continue
                        dve.scalar_tensor_tensor(out=tg[:, i, :], in0=tg[:, i, :], scalar=1.0, in1=bank[:, :],
                                                 op0=ALU.add, op1=ALU.mult).then_inc(*dve_took.up())
                        dve.wait_ge(*dve_took(l, TAKEN[BLOCK[t] + i][1]))
                        dve.tensor_tensor(mrg[:, d, :], mrg[:, d, :], tg[:, i, :], ALU.add).then_inc(*mrg_acc.up())

                for i in range(4):
                    dve.wait_ge(*rr(l, i + 1))
                    if i >= 1:
                        dve.wait_ge(*rrd(l, i))
                    dve.tensor_tensor(rtmp[:, 0, :], rraw[:, i, :], cos, ALU.mult).then_inc(*rt1.up())
                    dve.tensor_tensor(rtmp[:, 1, :], mx[i][:, :], sin, ALU.mult).then_inc(*rt2.up())
                    dve.wait_ge(*rt1(l, i + 1))
                    dve.wait_ge(*rt2(l, i + 1))
                    dve.tensor_tensor(rrot[:, i, :], rtmp[:, 0, :], rtmp[:, 1, :], ALU.add).then_inc(*rrd.up())
                for h in range(RH):
                    dve.wait_ge(*r_dec(l, h + 1))
                    if h >= 2:
                        dve.wait_ge(*r_o(l, h - 1))
                    for j in range(3):
                        dve.wait_ge(*r_scores(l, 3 * h + j + 1))
                        for kb, at in UNITS[j]:
                            w = WIDTH[kb]
                            d = dve.tensor_tensor(rsc[:, h % 2, UNIT_AT[j] + at:UNIT_AT[j] + at + w],
                                                  mx[j][:, at:at + w], rdec[:, h % 2, 0:w], ALU.mult)
                        d.then_inc(*r_sc.up())
                    dve.wait_ge(*r_mu(l, h + 1))
                    dve.wait_ge(*r_os(l, h + 1))
                    dve.scalar_tensor_tensor(out=ro[:, h % 2, :], in0=mx[5][:, :], scalar=-1.0 / P, in1=ro[:, h % 2, :],
                                             op0=ALU.mult, op1=ALU.add).then_inc(*r_xc.up())
                    take_branch(SB_OUT + 3 * h + 2, 0)
                    dve.wait_ge(*r_rs(l, h + 1))
                    dve.tensor_tensor(ro[:, h % 2, :], ro[:, h % 2, :], rrs[:, h % 2, :], ALU.mult).then_inc(*r_y.up())
                    dve.wait_ge(*r_y(l, h + 1))
                    if h == 0:
                        dve.wait_ge(*silu_b(l, 1))
                    dve.tensor_tensor(zB[:, h, :], ro[:, h % 2, :], zB[:, h, :], ALU.mult).then_inc(*y_ready.up())
                dve.wait_ge(*y_ready(l, 8))
                dve.memset(cin[:, :, 0:3], 0.0).then_inc(*g_pad.up())
                for c in range(4):
                    y_low(c, zB[:, c, :], 4 + c)

                ab = mx[0][:, 0:32].rearrange("p (t c) -> p t c", t=TB)

                def heads(ap):
                    return ap.rearrange("p (h t) -> p t h", h=GH)

                dve.wait_ge(*g_ab(l, 1))
                dve.tensor_tensor(heads(sm[:, 0, :]), ab[:, :, 4:8],
                                  heads(prm[:, PAR["dtb"]:PAR["dtb"] + 16]), ALU.add).then_inc(*g_s1.up())
                dve.tensor_scalar(heads(sm[:, 2, :]), ab[:, :, 0:4], -1.0, 80.0, ALU.mult, ALU.min).then_inc(*g_s1.up())
                dve.wait_ge(*g_s1(l, 1))
                dve.tensor_scalar(sm[:, 1, :], sm[:, 0, :], 40.0, None, ALU.min).then_inc(*g_s1.up())

                for i in range(12):
                    dve.wait_ge(*act_took(l, TAKEN[BLOCK[FIRST["gqkv"] + i]][1]))
                    if i >= 2:
                        dve.wait_ge(*g_silu(l, i - 1))
                    for j in range(4):
                        w = prm[:, PAR["conv"] + 4 * i + j:PAR["conv"] + 4 * i + j + 1]
                        if j == 0:
                            dve.tensor_scalar(cacc[:, i % 2, :], cin[:, i % 2, 0:T], w, None, ALU.mult).then_inc(*g_cv.up())
                        else:
                            dve.wait_ge(*g_cv(l, 4 * i + j))
                            dve.scalar_tensor_tensor(out=cacc[:, i % 2, :], in0=cin[:, i % 2, j:j + T], scalar=w,
                                                     in1=cacc[:, i % 2, :], op0=ALU.mult, op1=ALU.add).then_inc(*g_cv.up())
                dve.wait_ge(*g_s2(l, 4))
                dve.tensor_tensor(sm[:, 6, :], sm[:, 3, :], sm[:, 0, :], ALU.max).then_inc(*g_s3.up())
                dve.tensor_scalar(sm[:, 4, :], sm[:, 4, :], 1.0, None, ALU.add).then_inc(*g_s3.up())
                dve.wait_ge(*g_s3(l, 1))
                dve.scalar_tensor_tensor(out=sm[:, 6, :], in0=sm[:, 6, :], scalar=-1.0, in1=sm[:, 5, :],
                                         op0=ALU.mult, op1=ALU.mult).then_inc(*g_s3.up())
                dve.wait_ge(*g_s3(l, 2))
                dve.reciprocal(sm[:, 7, :], sm[:, 4, :]).then_inc(*g_s3.up())
                dve.wait_ge(*g_gc(l, 1))
                dve.tensor_scalar(sm[:, 8, :], mx[1][:, 0:16], -1.0, None, ALU.mult).then_inc(*g_s5.up())
                dve.wait_ge(*g_s4(l, 1))
                dve.tensor_tensor(sm[:, 10, :], sm[:, 7, :], sm[:, 9, :], ALU.mult).then_inc(*g_s5.up())
                for t in range(FIRST["gz"], FIRST["gz"] + 4):
                    if t == FIRST["gz"]:
                        dve.wait_ge(*y_lo(l, 4))
                    take_z(t, zA)
                for n in range(8):
                    dve.wait_ge(*g_rs(l, n + 1))
                    dve.scalar_tensor_tensor(out=gqkv[:, n, :], in0=gqkv[:, n, :], scalar=P ** -0.5 if n < 4 else 1.0,
                                             in1=ed[:, 2 + n % 2, :], op0=ALU.mult, op1=ALU.mult).then_inc(*g_nrm.up())

                def wide(ap):
                    return ap.unsqueeze(2).broadcast_to((P, TB, P))

                for h in range(GH):
                    col = slice(4 * h, 4 * h + 4)
                    E, dec = ed[:, h % 2, :], ed[:, 2 + h % 2, :]
                    dve.wait_ge(*g_x(l, h + 1))
                    dve.wait_ge(*g_E(l, h + 1))
                    dve.tensor_copy(sm[:, 13, col], blk(mx[0][:, :])[:, :, P - 1]).then_inc(*g_gl.up())
                    dve.wait_ge(*g_gl(l, h + 1))
                    dve.tensor_tensor(sm[:, 12, col], sm[:, 13, col], sm[:, 8, col], ALU.add).then_inc(*g_kd0.up())
                    dve.tensor_copy(gel[:, h, :], blk(E)[:, :, P - 1]).then_inc(*g_prep.up())
                    dve.wait_ge(*g_kt(l, h + 1))
                    dve.tensor_tensor(blk(kbg[:, h, :]), blk(mx[4][:, :]), wide(sm[:, 10, col]), ALU.mult).then_inc(*g_prep.up())
                    dve.wait_ge(*g_qk(l, h + 1))
                    dve.wait_ge(*g_kds(l, h + 1))
                    dve.tensor_tensor(blk(gk[:, h, :]), blk(mx[4][:, :]), wide(sm[:, 11, col]), ALU.mult).then_inc(*g_prep.up())
                    dve.wait_ge(*g_vt(l, h + 1))
                    dve.tensor_tensor(blk(gv[:, h, :]), blk(mx[5][:, :]), wide(sm[:, 7, col]), ALU.mult).then_inc(*g_prep.up())
                    dve.tensor_tensor(gq[:, h, :], gq[:, h, :], E, ALU.mult).then_inc(*g_prep.up())
                    dve.wait_ge(*g_dec(l, h + 1))
                    dve.tensor_tensor(gLT[:, h, :], mx[2][:, :], dec, ALU.mult).then_inc(*g_prep.up())
                    dve.tensor_tensor(gsc[:, h, :], mx[3][:, :], dec, ALU.mult).then_inc(*g_prep.up())
                    dve.wait_ge(*g_prep(l, 8 * h + 6))
                    dve.wait_ge(*g_bb(l, h + 1))
                    dve.tensor_tensor(gLT[:, h, :], gLT[:, h, :], mx[1][:, :], ALU.mult).then_inc(*g_prep.up())

                def rep(ap):
                    return ap.unsqueeze(1).broadcast_to((P, TB, P))

                identb = rep(ident)
                for lv in range(LEVELS):
                    mask = rep(con[:, C_LEVEL + P * lv:C_LEVEL + P * (lv + 1)])
                    for pair in range(2):
                        for h in (2 * pair, 2 * pair + 1):
                            dve.wait_ge(*g_P(l, GH * lv + h + 1))
                            if h >= 2:
                                if lv:
                                    dve.wait_ge(*g_AB(l, GH * (lv - 1) + h - 1))
                                else:
                                    dve.wait_ge(*g_X(l, h - 1))
                            dve.tensor_tensor(blk(ed[:, h % 2, :]), blk(mx[3 * (h % 2)][:, :]), mask, ALU.mult).then_inc(*g_Pm.up())
                            if lv == 0:
                                dve.wait_ge(*g_Pm(l, h + 1))
                                dve.tensor_tensor(blk(gX[:, h, :]), identb, blk(ed[:, h % 2, :]), ALU.subtract).then_inc(*g_X.up())
                                dve.tensor_tensor(blk(gXT[:, h, :]), blk(gLT[:, h, :]), rep(const("m1t")), ALU.mult).then_inc(*g_XT.up())
                                dve.wait_ge(*g_XT(l, 2 * h + 1))
                                dve.tensor_tensor(blk(gXT[:, h, :]), identb, blk(gXT[:, h, :]), ALU.subtract).then_inc(*g_XT.up())
                        if lv:
                            for h in (2 * pair, 2 * pair + 1):
                                dve.wait_ge(*g_AB(l, GH * (lv - 1) + h + 1))
                                if lv < LEVELS - 1:
                                    dve.tensor_tensor(gX[:, h, :], gX[:, h, :], mx[3 * (h % 2) + 1][:, :], ALU.subtract).then_inc(*g_X.up())
                                dve.tensor_tensor(gXT[:, h, :], gXT[:, h, :], mx[3 * (h % 2) + 2][:, :], ALU.subtract).then_inc(*g_XT.up())
                        f = 2 * lv + pair
                        if f < 12 and PLAN[RET_OUT + f][0] == "branch":
                            take_branch(RET_OUT + f, 1)
                for tb in range(TB - 1):
                    dve.wait_ge(*g_s(l, tb + 1))
                    if tb == 0:
                        dve.tensor_copy(gS[:, :, :], blk(mx[1][:, :])).then_inc(*g_su.up())
                    else:
                        dve.tensor_tensor(gS[:, :, :], gS[:, :, :], gel[:, :, tb].unsqueeze(2).broadcast_to((P, GH, P)),
                                          ALU.mult).then_inc(*g_s0.up())
                        dve.wait_ge(*g_s0(l, tb))
                        dve.tensor_tensor(gS[:, :, :], gS[:, :, :], blk(mx[1][:, :]), ALU.add).then_inc(*g_su.up())
                for h in range(GH):
                    dve.wait_ge(*n_rs(l, h + 1))
                    dve.scalar_tensor_tensor(out=gX[:, h, :], in0=mx[2 + h][:, :], scalar=prm[:, PAR["gain"]:PAR["gain"] + 1],
                                             in1=ed[:, 2 + h % 2, :], op0=ALU.mult, op1=ALU.mult).then_inc(*n_t.up())
                    dve.wait_ge(*n_t(l, h + 1))
                    if h == 0:
                        dve.wait_ge(*silu_a(l, 2))
                    dve.tensor_tensor(zA[:, h, :], gX[:, h, :], zA[:, h, :], ALU.mult).then_inc(*y_ready.up())
                for h in range(GH):
                    y_low(h, zA[:, h, :], 8 + h)
                for g in range(4):
                    take_branch(GDN_OUT + 3 * g + 2, 2)
                for kb in range(KB):
                    dve.wait_ge(*m_hi(l, kb + 1))
                    dve.scalar_tensor_tensor(out=hnl[:, kb, :], in0=mrg[:, kb, :], scalar=0.5, in1=hnh[:, kb, :],
                                             op0=ALU.mult, op1=ALU.subtract).then_inc(*m_lo.up())
                for d in range(KB):
                    bank = came(FIRST["wout"] + d)
                    dve.tensor_tensor(x[:, d, :], x[:, d, :], bank[:, :], ALU.add).then_inc(*x_new.up(2))

            dve.wait_ge(*norm_rs(DEPTH, 1))
            dve.wait_ge(consts_in, 32)
            for kb in range(KB):
                norm_scale(DEPTH, fing[:, kb:kb + 1], kb)

        @block.tensor
        def _(pe):
            def mm(o, w, a, start, stop):
                return pe.matmul(o, w, a, start=start, stop=stop, skip_group_check=True)

            def mm3(o, w, a, start, stop):
                mm(o, w[0], a[0], start, False)
                mm(o, w[0], a[1], False, False)
                return mm(o, w[1], a[0], False, stop)

            def norm_sum_of(l):
                for kb in range(KB):
                    pe.wait_ge(*norm_sq(l, kb + 1))
                    m = mm(mx[0][:, :], const("ones"), sq[:, kb, :], kb == 0, kb == KB - 1)
                m.then_inc(*norm_sum.up())

            pe.wait_ge(consts_in, 32)
            pe.wait_ge(consts_up, 4)
            with pe.Fori(0, DEPTH) as l:
                def wpair(t, a, b, kn, n):
                    s = t % 2
                    return [w[:, s, :].rearrange("p (k n) -> p k n", k=kn)[:, a, b:b + n] for w in (whi, wlo)]

                def hn(kb, c0=0, n=T):
                    return [hnh[:, kb, c0:c0 + n], hnl[:, kb, c0:c0 + n]]

                def free(n):
                    if n >= 2:
                        who, k = TAKEN[n - 2]
                        pe.wait_ge(*by(who)(l, 2 * k + 16 if who == "x" else k))

                def tile(t):
                    what, i = PLAN[t]
                    n = BLOCK[t]
                    pe.wait_ge(*w_hi(l, t + 1))
                    pe.wait_ge(*w_lo(l, t + 1))
                    if what == "branch":
                        for b in range(2):
                            free(n + b)
                            for c in range(4):
                                m = mm3(pj[(n + b) % 2][:, :], wpair(t, c, P * b, 4, P), [yh[:, c, :], yl[:, c, :]], c == 0, c == 3)
                            m.then_inc(*blocks.up())
                        return
                    free(n)
                    bank = pj[n % 2]
                    if what in ("sbv", "rv"):
                        for tb in range(TB):
                            for kb in range(KB):
                                m = mm3(bank[:, tb * P:(tb + 1) * P], hn(kb, tb * P, P), wpair(t, kb, 0, KB, P), kb == 0, kb == KB - 1)
                    else:
                        for kb in range(KB):
                            if t == 0:
                                pe.wait_ge(*hn_lo(l, kb + 1))
                            if t == FIRST["wout"]:
                                pe.wait_ge(*m_lo(l, kb + 1))
                            m = mm3(bank[:, :], wpair(t, kb, 0, KB, P), hn(kb), kb == 0, kb == KB - 1)
                    m.then_inc(*blocks.up(2))

                norm_sum_of(l)
                for t in range(16):
                    tile(t)

                def sb_scores(u):
                    h, j = divmod(u, 3)
                    c, po = h // 2, SBD * (h % 2)
                    if u == 0:
                        pe.wait_ge(*act_took(l, TAKEN[BLOCK[11]][1]))
                    if u >= 5:
                        pe.wait_ge(*sb_w(l, u - 4))
                    bank = mx[u % 5]
                    for n, (kb, at) in enumerate(UNITS[j]):
                        mm(bank[:, at:at + WIDTH[kb]], sbk[po:po + SBD, c, kb * P:(kb + 1) * P],
                           sbq[po:po + SBD, c, kb * P:T], n == 0, False)
                        m = mm(bank[:, at:at + P], ident_r, negsb_r, False, False)
                    m.then_inc(*sb_z.up())

                def sb_sums(u):
                    h, j = divmod(u, 3)
                    pe.wait_ge(*sb_sp(l, u + 1))
                    bank = mx[u % 5]
                    for kb, at in UNITS[j]:
                        for k2 in range(kb, TB):
                            lo = at + P * (k2 - kb)
                            m = mm(bank[:, lo:at + WIDTH[kb]], const("ntril") if k2 == kb else const("nones"),
                                   sbsp[:, h % 2, SP_AT[k2]:SP_AT[k2] + WIDTH[k2]], False, k2 == TB - 1)
                    m.then_inc(*sb_s.up())

                def sb_out(u):
                    h, j = divmod(u, 3)
                    pe.wait_ge(*sb_w(l, u + 1))
                    if u % 6 == 0 and u:
                        pe.wait_ge(*y_ready(l, u // 6))
                    for n, (kb, at) in enumerate(UNITS[j]):
                        m = mm(mx[5][:, kb * P:T], vpad[:, kb, h, :], sbw[:, u % 2, at:at + WIDTH[kb]],
                               u % 6 == 0 and n == 0, u % 6 == 5)
                    m.then_inc(*sb_o.up())

                for u in range(NU + 3):
                    if u < NU:
                        sb_scores(u)
                    if 1 <= u <= NU:
                        sb_sums(u - 1)
                    if u >= 2 and u - 2 < NU:
                        sb_out(u - 2)
                    if u % 2 == 1 and u < NU:
                        tile(16 + u // 2)

                for i in range(4):
                    if i == 0:
                        pe.wait_ge(*act_took(l, TAKEN[BLOCK[FIRST["rv"] + 3]][1]))
                        pe.wait_ge(*sb_w(l, NU))
                    mm(mx[i][:, :], const("rot"), rraw[:, i, :], True, True).then_inc(*rr.up())
                for h in range(RH):
                    c, po = h // 2, 64 * (h % 2)
                    pe.wait_ge(*rrd(l, 4))
                    for j in range(3):
                        if h:
                            pe.wait_ge(*r_sc(l, 3 * (h - 1) + j + 1))
                        for n, (kb, at) in enumerate(UNITS[j]):
                            m = mm(mx[j][:, at:at + WIDTH[kb]], rrot[po:po + 64, 2 + c, kb * P:(kb + 1) * P],
                                   rrot[po:po + 64, c, kb * P:T], n == 0, True)
                        m.then_inc(*r_scores.up())
                    if h == 0:
                        pe.wait_ge(*y_lo(l, 4))
                    tile(SB_OUT + 3 * h)
                    pe.wait_ge(*r_sc(l, 3 * h + 3))
                    if h >= 2:
                        pe.wait_ge(*r_os(l, h - 1))
                    for n, kb in enumerate(range(TB)):
                        m = mm(mx[3 + h % 2][:, kb * P:T], rv[:, kb, h * P:(h + 1) * P],
                               rsc[:, h % 2, SP_AT[kb]:SP_AT[kb] + WIDTH[kb]], kb == 0, kb == TB - 1)
                    m.then_inc(*r_o.up())
                    tile(SB_OUT + 3 * h + 1)
                    pe.wait_ge(*r_os(l, h + 1))
                    if h:
                        pe.wait_ge(*r_ln(l, h))
                    mm(mx[5][:, :], const("ones"), ro[:, h % 2, :], True, True).then_inc(*r_mu.up())
                    pe.wait_ge(*r_sq(l, h + 1))
                    mm(mx[5][:, :], const("ones"), rsq[:, h % 2, :], True, True).then_inc(*r_var.up())
                    tile(SB_OUT + 3 * h + 2)

                pe.wait_ge(*ab_lo(l, 1))
                for tb in range(TB):
                    for kb in range(KB):
                        m = mm3(mx[0][:, 8 * tb:8 * tb + 8], hn(kb, tb * P, P), [abh[:, kb, :], abl[:, kb, :]], kb == 0, kb == KB - 1)
                m.then_inc(*g_ab.up())
                for t in range(FIRST["gqkv"], FIRST["gqkv"] + 12):
                    tile(t)
                pe.wait_ge(*g_s3(l, 4))
                mm(mx[1][:, 0:16], const("triu"), sm[:, 6, :], True, True).then_inc(*g_gc.up())
                for t in range(FIRST["gz"], FIRST["gz"] + 4):
                    tile(t)
                for n in range(8):
                    pe.wait_ge(*g_sq(l, n + 1))
                    if n >= 2:
                        pe.wait_ge(*g_ln(l, n - 1))
                    mm(mx[2 + n % 2][:, :], const("ones"), ed[:, n % 2, :], True, True).then_inc(*g_ss.up())
                pe.wait_ge(*g_nrm(l, 8))
                pe.wait_ge(*g_s5(l, 2))
                for h in range(GH):
                    def four(bank, lhs, rhs):
                        for tb in range(TB):
                            m = mm(bank[:, tb * P:(tb + 1) * P], lhs(tb), rhs(tb), tb == 0, True)
                        return m

                    def tok(buf):
                        return lambda tb: buf[:, h, tb * P:(tb + 1) * P]

                    def spread(row):
                        return lambda tb: sm[:, row, 4 * h + tb:4 * h + tb + 1].broadcast_to((P, P))

                    if h:
                        pe.wait_ge(*g_dec(l, h))
                    four(mx[0], spread(6), lambda tb: const("triu")).then_inc(*g_x.up())
                    if h:
                        pe.wait_ge(*g_prep(l, 8 * h))
                    four(mx[1], spread(7), lambda tb: ident).then_inc(*g_bb.up())
                    four(mx[2], tok(gk), tok(gk)).then_inc(*g_kk.up())
                    for tb in range(TB):
                        m = pe.transpose(mx[4][:, tb * P:(tb + 1) * P], gk[:, h, tb * P:(tb + 1) * P], ident)
                    m.then_inc(*g_kt.up())
                    four(mx[3], tok(gk), tok(gq)).then_inc(*g_qk.up())
                    for tb in range(TB):
                        m = pe.transpose(mx[5][:, tb * P:(tb + 1) * P], gv[:, h, tb * P:(tb + 1) * P], ident)
                    m.then_inc(*g_vt.up())
                    pe.wait_ge(*g_gl(l, h + 1))
                    for tb in range(TB):
                        m = mm(mx[0][:, tb * P:(tb + 1) * P], ident_r, neggdn_r, False, True)
                    m.then_inc(*g_xm.up())

                pe.wait_ge(*g_prep(l, 8 * GH))
                for lv in range(LEVELS):
                    for pair in range(2):
                        for h in (2 * pair, 2 * pair + 1):
                            b = 3 * (h % 2)
                            if lv == 0:
                                if h >= 2:
                                    pe.wait_ge(*g_Pm(l, h - 1))
                                four(mx[b], tok(gLT), lambda tb: ident).then_inc(*g_P.up())
                            else:
                                pe.wait_ge(*g_X(l, GH * (lv - 1) + h + 1))
                                pe.wait_ge(*g_Pm(l, GH * lv + h - 1))
                                four(mx[b], tok(gLT), tok(gX)).then_inc(*g_P.up())
                        f = 2 * lv + pair
                        if f < 12:
                            if f == 0:
                                pe.wait_ge(*y_lo(l, 8))
                            tile(RET_OUT + f)
                        if lv:
                            for h in (2 * pair, 2 * pair + 1):
                                b = 3 * (h % 2)
                                pe.wait_ge(*g_Pm(l, GH * lv + h + 1))
                                pe.wait_ge(*g_XT(l, GH * lv + h + (3 if h < 2 else 1)))
                                if h >= 2:
                                    pe.wait_ge(*g_XT(l, GH * (lv + 1) + h - 1))
                                pm = (lambda tb, h=h: ed[:, h % 2, tb * P:(tb + 1) * P])
                                if lv < LEVELS - 1:
                                    four(mx[b + 1], tok(gXT), pm)
                                four(mx[b + 2], pm, tok(gXT)).then_inc(*g_AB.up())
                for h in range(GH):
                    pe.wait_ge(*g_XT(l, GH * (LEVELS + 1) if h == 0 else GH * (LEVELS + 1)))
                    if h >= 2:
                        pe.wait_ge(*g_wts(l, h - 1))
                    four(mx[2 + h % 2], tok(kbg), tok(gXT)).then_inc(*g_wt.up())
                pe.wait_ge(*g_wts(l, GH))
                for tb in range(TB):
                    s = slice(tb * P, (tb + 1) * P)
                    if tb:
                        pe.wait_ge(*g_vn(l, tb))
                        pe.wait_ge(*g_su(l, tb))
                    for h in range(GH):
                        hs = slice(h * P, (h + 1) * P)
                        m = mm(mx[0][:, hs], gXT[:, h, s], gv[:, h, s], True, tb == 0)
                        if tb:
                            m = mm(mx[0][:, hs], gLT[:, h, s], gS[:, h, :], False, True)
                    m.then_inc(*g_v.up())
                    if tb:
                        for h in range(GH):
                            mm(mx[2 + h][:, s], gS[:, h, :], gq[:, h, s], True, False)
                    pe.wait_ge(*g_vn(l, tb + 1))
                    for h in range(GH):
                        m = mm(mx[2 + h][:, s], ed[:, 2, h * P:(h + 1) * P], gsc[:, h, s], tb == 0, True)
                    m.then_inc(*g_o.up())
                    if tb < TB - 1:
                        for h in range(GH):
                            m = mm(mx[1][:, h * P:(h + 1) * P], gk[:, h, s], ed[:, 2, h * P:(h + 1) * P], True, True)
                        m.then_inc(*g_s.up())
                for h in range(GH):
                    pe.wait_ge(*n_sq(l, h + 1))
                    if h >= 2:
                        pe.wait_ge(*n_ln(l, h - 1))
                    mm(mx[h % 2][:, :], const("ones"), ed[:, h % 2, :], True, True).then_inc(*n_ss.up())
                pe.wait_ge(*y_lo(l, 12))
                for t in range(GDN_OUT, NTILES):
                    tile(t)
            norm_sum_of(DEPTH)

        for s in sigs:
            extra = {"norm_sq": KB, "norm_sum": 1, "norm_ln": 1, "norm_rs": 1, "norm_t": KB}.get(s.name, 0)
            want = {"w_lo": 0}.get(s.name, s.per_layer)
            assert s.n == want + extra, (s.name, s.n, s.per_layer)


def layout(inputs):
    a = {k: np.asarray(v) for k, v in inputs.items()}
    xin = np.ascontiguousarray(a["x"][0].T.reshape(KB, P, T).transpose(1, 0, 2))
    wt = np.empty((DEPTH, NTILES, P, TILE), np.float32)
    branches = (a["w_sb"], a["w_ret"], a["w_gdn"])
    for t, (what, i) in enumerate(PLAN):
        if what == "branch":
            src = branches[i // 4][:, :, 256 * (i % 4):256 * (i % 4) + 256]
        elif what == "wout":
            src = a["w_out"][:, :, P * i:P * (i + 1)]
        else:
            src = a["w_in"][:, :, OFF[what] + P * i:OFF[what] + P * (i + 1)]
        k = src.shape[1] // P
        wt[:, t] = src.reshape(DEPTH, k, P, -1).transpose(0, 2, 1, 3).reshape(DEPTH, P, TILE)
    wab = np.ascontiguousarray(a["w_in"][:, :, OFF["gab"]:OFF["gab"] + 8].reshape(DEPTH, KB, P, 8)
                               .transpose(0, 2, 1, 3).reshape(DEPTH, P, KB * 8))
    par = np.empty((DEPTH, P, PAR_END), np.float32)
    par[:, :, 0:8] = a["norm_g"].reshape(DEPTH, KB, P).transpose(0, 2, 1)
    par[:, :, 8:56] = a["conv_w"].reshape(DEPTH, 4, 12, P).transpose(0, 3, 2, 1).reshape(DEPTH, P, 48)
    par[:, :, 56] = a["gdn_norm_g"]
    par[:, :, 57:73] = np.repeat(a["dt_bias"], TB, axis=1)[:, None, :]
    par[:, :, 73:89] = np.repeat(a["a_log"], TB, axis=1)[:, None, :]
    return {"xin": xin, "wt": wt.reshape(DEPTH * NTILES // RAW, RAW, P, TILE), "wab": wab, "par": par,
            "fin": np.ascontiguousarray(a["final_g"].reshape(KB, P).T), "cst": constants()}


def kernel(**inputs):
    import concourse.bacc as _bacc
    from concourse.bass_utils import run_bass_kernel_spmd as _run

    arrays = layout(inputs)
    nc = _bacc.Bacc("TRN2", target_bir_lowering=False, num_devices=1)
    args = [nc.dram_tensor(n, v.shape, mybir.dt.float32, kind="ExternalInput").ap() for n, v in arrays.items()]
    args.append(nc.dram_tensor("out", (P, KB, T), mybir.dt.float32, kind="ExternalOutput").ap())
    trunk(nc, *args)
    r = _run(nc, [arrays], core_ids=[0])
    got = r.results[0]["out"]
    return np.ascontiguousarray(got.transpose(1, 0, 2).reshape(D, T).T)[None]
```

```python
import math

import numpy as np
import concourse.bass as bass
from concourse import mybir
from contextlib import ExitStack

F32 = mybir.dt.float32
F32R = mybir.dt.float32r
ALU = mybir.AluOpType
ACT = mybir.ActivationFunctionType

P = 128
D = 1024
T = 512
DEPTH = 2
KB = D // P
TB = T // P
SBH, SBD = 8, 64
RH = 4
GH = 4
EPS = 1e-6
TILE = 1024
RAW = 2
OFF = dict(sbq=0, sbk=512, sbv=1024, sbz=1536, rq=2048, rk=2304, rv=2560, rz=3072,
           gqkv=3584, gz=5120, gab=5632, gate=5640)
LEVELS = 7
LN_EXP = "natural_log_exp_and_others"
NEG = -1e30


def weight_plan():
    plan = [("sbq", i) for i in range(4)] + [("sbk", i) for i in range(4)]
    plan += [("sbv", i) for i in range(4)] + [("sbz", i) for i in range(4)]
    plan += [("rq", i) for i in range(2)] + [("rk", i) for i in range(2)]
    plan += [("rv", i) for i in range(4)] + [("rz", i) for i in range(4)]

    def branch(b):
        out = []
        for g in range(4):
            out += [("gate", 8 * b + 2 * g), ("gate", 8 * b + 2 * g + 1), ("branch", 4 * b + g)]
        return out

    plan += branch(0)
    plan += [("gqkv", i) for i in range(12)] + [("gz", i) for i in range(4)]
    plan += branch(1)
    plan += [("gate", 16 + i) for i in range(8)] + [("branch", 8 + i) for i in range(4)]
    plan += [("wout", i) for i in range(8)]
    return plan


PLAN = weight_plan()
NTILES = len(PLAN)
FIRST = {what: next(i for i, (w, _) in enumerate(PLAN) if w == what) for what, _ in PLAN}
SB_OUT, RET_OUT, GATES = (next(i for i, x in enumerate(PLAN) if x == ("gate", 8 * b)) for b in range(3))
GDN_OUT = GATES + 8
ON_VECTOR = ("sbz", "rz", "gz", "branch")


def block_table():
    first, taken, counts = [], [], {"act": 0, "dve": 0, "x": 0}
    for what, _ in PLAN:
        first.append(len(taken))
        for _ in range(2 if what == "branch" else 1):
            who = "x" if what == "wout" else "dve" if what in ON_VECTOR else "act"
            counts[who] += 1
            taken.append((who, counts[who]))
    return first, taken, counts


BLOCK, TAKEN, COUNTS = block_table()

UNITS = [[(3, 0), (2, 128)], [(1, 0)], [(0, 0)]]
WIDTH = {kb: T - P * kb for kb in range(TB)}
SP_AT = {3: 0, 2: 128, 1: 384, 0: 768}
UNIT_AT = [0, 384, 768]
UNIT_W = [384, 384, 512]

CONST = ["triu", "ident", "ntril", "nones", "rot", "negsb", "neggdn", "m1t"]
CC = {n: P * i for i, n in enumerate(CONST)}
C_LEVEL = P * len(CONST)
C_DIFF = C_LEVEL + P * LEVELS
C_COS = C_DIFF + T
C_SIN = C_COS + T
C_END = C_SIN + T
PAR = dict(norm=0, conv=8, gain=56, dtb=57, alog=73)
PAR_END = 89


def constants():
    i = np.arange(P)
    r, c = i[:, None], i[None, :]
    out = np.zeros((P, C_END), np.float32)

    def put(name, a):
        out[:, CC[name]:CC[name] + P] = a

    put("triu", r <= c)
    put("ident", r == c)
    put("ntril", -(r >= c).astype(np.float32))
    put("nones", -1.0)
    src = np.where(c % 64 < 32, c + 32, c - 32)
    put("rot", np.where(r == src, np.where(c % 64 < 32, -1.0, 1.0), 0.0))
    put("negsb", np.where(r >= c, NEG, 0.0))
    put("neggdn", np.where(r > c, NEG, 0.0))

    def level(s):
        return ((r // (2 * s) == c // (2 * s)) & ((r // s) % 2 == 1) & ((c // s) % 2 == 0)).astype(np.float32)

    put("m1t", level(1).T)
    for n in range(LEVELS):
        out[:, C_LEVEL + P * n:C_LEVEL + P * (n + 1)] = level(1 << n)
    t = np.arange(T)[None, :]
    out[:, C_DIFF:C_DIFF + T] = np.where(t >= r, t - r, 1e9)
    freq = (np.float32(10000.0) ** (-(np.arange(32, dtype=np.float32)) / np.float32(32)))
    ang = t.astype(np.float32) * freq[(i % 32)][:, None]
    out[:, C_COS:C_COS + T] = np.cos(ang.astype(np.float32))
    out[:, C_SIN:C_SIN + T] = np.sin(ang.astype(np.float32))
    return out


def trunk(nc, xin, wt, wab, par, fin, cst, out):
    ctx = ExitStack()
    sigs = []
    nc.disable_value_cache = True

    class Signal:

        def __init__(self, name, per_layer):
            self.sem = ctx.enter_context(nc.semaphore(name))
            self.name, self.per_layer, self.n = name, per_layer, 0
            sigs.append(self)

        def __call__(self, l, n):
            return self.sem, l * self.per_layer + n

        def up(self, by=1):
            self.n += by
            return self.sem, by

    with ctx:
        def sb(name, shape, dt=F32):
            return ctx.enter_context(nc.sbuf_tensor(name, shape, dt))

        x = sb("x", [P, KB, T])
        hnh = sb("hnh", [P, KB, T], F32R)
        hnl = sb("hnl", [P, KB, T], F32R)
        wraw = sb("wraw", [P, RAW, TILE])
        whi = sb("whi", [P, 2, TILE], F32R)
        wlo = sb("wlo", [P, 2, TILE], F32R)
        con = sb("con", [P, C_END])
        conr = sb("conr", [P, 3, P], F32R)
        prm = sb("prm", [P, PAR_END])
        fing = sb("fing", [P, KB])
        eps = sb("eps", [P, 1])
        mrg = sb("mrg", [P, KB, T])
        yh = sb("yh", [P, 4, T], F32R)
        yl = sb("yl", [P, 4, T], F32R)
        zA = sb("zA", [P, 4, T])
        zB = sb("zB", [P, 4, T])
        tg = sb("tg", [P, 2, T])
        abh = sb("abh", [P, KB * 8 + P - 8], F32R)
        abl = sb("abl", [P, KB * 8 + P - 8], F32R)
        sm = sb("sm", [P, 14, 16])
        gel = sb("gel", [P, GH, TB])
        arena = sb("arena", [P, 16896])
        pj = [ctx.enter_context(nc.psum_tensor(f"pj{i}", [P, T], F32)) for i in range(2)]
        mx = [ctx.enter_context(nc.psum_tensor(f"mx{i}", [P, T], F32)) for i in range(6)]

        def area(at, *shape):
            n = int(np.prod(shape))
            v = arena[:, at:at + n]
            if len(shape) == 2:
                v = v.rearrange("p (a b) -> p a b", a=shape[0])
            if len(shape) == 3:
                v = v.rearrange("p (a b c) -> p a b c", a=shape[0], b=shape[1])
            return v

        def const(name):
            return con[:, CC[name]:CC[name] + P]

        ident = const("ident")
        ident_r, negsb_r, neggdn_r = (conr[:, i, :] for i in range(3))
        diff = con[:, C_DIFF:C_DIFF + T]
        cos, sin = con[:, C_COS:C_COS + T], con[:, C_SIN:C_SIN + T]

        sq = area(0, KB, T)
        rstd = area(4096, T)
        sbq, sbk = area(0, 4, T), area(2048, 4, T)
        vpad = area(4096, TB, SBH, P)
        sbv, abt = area(9216, 4, T), area(11264, T)
        abw = area(11776, KB * 8)
        sbe, sbsp, sbw = area(8192, 2, T), area(9216, 2, 1280), area(11776, 2, T)
        rraw, rv = area(12800, 4, T), area(14848, TB, T)
        rrot, rdec, rsc = area(0, 4, T), area(2048, 2, T), area(3072, 2, 1280)
        ro, rsq, rrs, rtmp = area(5632, 2, T), area(6656, 2, T), area(7680, 2, T), area(8704, 2, T)
        gq, gk, gv = area(0, GH, T), area(2048, GH, T), area(4096, GH, T)
        kbg, gX, gXT = area(6144, GH, T), area(8192, GH, T), area(10240, GH, T)
        gLT, gsc = area(12288, GH, T), area(14336, GH, T)
        gS = area(16384, GH, P)
        gates = area(6144, KB, T)
        cin, cacc = area(8192, 2, 516), area(10240, 2, T)
        gqkv = area(0, 12, T)
        ed = zB

        def blk(ap):
            return ap.rearrange("p (a b) -> p a b", a=TB)

        def S(name, n):
            return Signal(name, n)

        consts_in = ctx.enter_context(nc.semaphore("consts_in"))
        consts_up = ctx.enter_context(nc.semaphore("consts_up"))
        w_in = [ctx.enter_context(nc.semaphore(f"w_in{i}")) for i in range(RAW)]
        out_done = ctx.enter_context(nc.semaphore("out_done"))
        x_new = S("x_new", 16)
        w_hi = S("w_hi", NTILES)
        w_lo = S("w_lo", NTILES)
        blocks = S("blocks", 2 * NTILES)
        act_took = S("act_took", COUNTS["act"])
        dve_took = S("dve_took", COUNTS["dve"])
        params_in = S("params_in", 32)
        norm_sq, norm_sum, norm_ln, norm_rs = S("norm_sq", 8), S("norm_sum", 1), S("norm_ln", 1), S("norm_rs", 1)
        norm_t, hn_hi, hn_lo, hn_lo_p = S("norm_t", 8), S("hn_hi", 8), S("hn_lo", 4), S("hn_lo_p", 4)
        ab_cm, ab_t, v_tr, v_tm = S("ab_cm", 1), S("ab_t", 1), S("v_tr", 4), S("v_tm", 4)
        rv_tr, rv_tm = S("rv_tr", 4), S("rv_tm", 4)
        ab_hi, ab_lo = S("ab_hi", 1), S("ab_lo", 1)
        sb_zero = S("sb_zero", 1)
        silu_a, silu_b = S("silu_a", 2), S("silu_b", 1)
        NU = SBH * 3
        sb_z, sb_e, sb_l, sb_min, sb_sp = S("sb_z", NU), S("sb_e", NU), S("sb_l", NU), S("sb_min", NU), S("sb_sp", NU)
        sb_s, sb_w, sb_o, sb_oo = S("sb_s", NU), S("sb_w", NU), S("sb_o", NU), None
        y_ready, y_hi, y_lo = S("y_ready", 12), S("y_hi", 12), S("y_lo", 12)
        rr, rt1, rt2, rrd = S("rr", 4), S("rt1", 4), S("rt2", 4), S("rrd", 4)
        r_dec, r_scores, r_sc, r_o = S("r_dec", RH), S("r_scores", RH * 3), S("r_sc", RH * 3), S("r_o", RH)
        r_os, r_mu, r_xc, r_sq = S("r_os", RH), S("r_mu", RH), S("r_xc", RH), S("r_sq", RH)
        r_var, r_ln, r_rs, r_y = S("r_var", RH), S("r_ln", RH), S("r_rs", RH), S("r_y", RH)
        mrg_acc = S("mrg_acc", 16)
        g_pad = S("g_pad", 1)
        g_cv, g_silu = S("g_cv", 48), S("g_silu", 12)
        g_ab, g_s1, g_s2, g_s3, g_gc = S("g_ab", 1), S("g_s1", 3), S("g_s2", 4), S("g_s3", 4), S("g_gc", 1)
        g_s4, g_s5 = S("g_s4", 1), S("g_s5", 2)
        g_sq, g_ss, g_ln, g_rs, g_nrm = S("g_sq", 8), S("g_ss", 8), S("g_ln", 8), S("g_rs", 8), S("g_nrm", 8)
        g_x, g_E, g_gl, g_kd0, g_kds = S("g_x", GH), S("g_E", GH), S("g_gl", GH), S("g_kd0", GH), S("g_kds", GH)
        g_xm, g_dec = S("g_xm", GH), S("g_dec", GH)
        g_bb, g_kk, g_qk, g_kt, g_vt = S("g_bb", GH), S("g_kk", GH), S("g_qk", GH), S("g_kt", GH), S("g_vt", GH)
        g_prep = S("g_prep", GH * 8)
        g_P, g_Pm = S("g_P", LEVELS * GH), S("g_Pm", LEVELS * GH)
        g_AB = S("g_AB", (LEVELS - 1) * GH)
        g_X = S("g_X", (LEVELS - 1) * GH)
        g_XT = S("g_XT", (LEVELS + 1) * GH)
        g_wt, g_wts = S("g_wt", GH), S("g_wts", GH)
        g_v, g_vn, g_o, g_s, g_s0, g_su = S("g_v", TB), S("g_vn", TB), S("g_o", TB), S("g_s", TB - 1), S("g_s0", TB - 2), S("g_su", TB - 1)
        n_sq, n_ss, n_ln, n_rs, n_t = S("n_sq", GH), S("n_ss", GH), S("n_ln", GH), S("n_rs", GH), S("n_t", GH)
        m_hi, m_lo = S("m_hi", 8), S("m_lo", 8)

        def by(who):
            return {"act": act_took, "dve": dve_took, "x": x_new}[who]

        block = ctx.enter_context(nc.Block())

        @block.sync
        def _(sp):
            sp.dma_start(x[:, :, :], xin).then_inc(x_new.sem, 16)
            sp.dma_start(con[:, :], cst).then_inc(consts_in, 16)
            sp.dma_start(fing[:, :], fin).then_inc(consts_in, 16)
            for i in range(RAW):
                sp.dma_start(wraw[:, i, :], wt[0, i, :, :]).then_inc(w_in[i], 16)
            with sp.Fori(1, DEPTH * NTILES // RAW) as r:
                for i in range(RAW):
                    sp.wait_ge(w_lo.sem, RAW * r + (i - RAW + 1))
                    sp.dma_start(wraw[:, i, :], wt[r, i, :, :]).then_inc(w_in[i], 16)
            for kb in range(KB):
                sp.wait_ge(*norm_t(DEPTH, kb + 1))
                sp.dma_start(out[:, kb, :], sq[:, kb, :]).then_inc(out_done, 16)
            sp.wait_ge(out_done, 16 * KB)

        @block.gpsimd
        def _(pool):
            with pool.Fori(0, DEPTH) as l:
                def split(t, i):
                    pool.wait_ge(*w_hi(l, t + 1))
                    nc.gpsimd.tensor_tensor(wlo[:, i, :], wraw[:, i, :], whi[:, i, :], ALU.subtract).then_inc(w_lo.sem, 1)

                split(0, 0)
                for kb in range(1, KB, 2):
                    pool.wait_ge(*hn_hi(l, kb + 1))
                    nc.gpsimd.tensor_tensor(hnl[:, kb, :], sq[:, kb, :], hnh[:, kb, :], ALU.subtract).then_inc(*hn_lo_p.up())
                split(1, 1)
                with pool.Fori(1, NTILES // 2) as r:
                    for i in range(2):
                        pool.wait_ge(*blocks(l, 4 * r + (2 * i - 2)))
                        split(2 * r + i, i)

        @block.scalar
        def _(act):
            def cp(dst, src, scale=1.0):
                return act.activation(dst, src, ACT.Copy, scale=scale)

            act.wait_ge(consts_in, 32)
            for i, n in enumerate(("ident", "negsb", "neggdn")):
                cp(conr[:, i, :], const(n)).then_inc(consts_up, 1)

            def square(kb):
                act.activation(sq[:, kb, :], x[:, kb, :], ACT.Square).then_inc(*norm_sq.up())

            def rms(l):
                act.wait_ge(*norm_sum(l, 1))
                act.activation(rstd, mx[0][:, :], ACT.Ln, bias=eps[:, :], scale=-1.0 / D).then_inc(*norm_ln.up())
                act.wait_ge(*norm_ln(l, 1))
                act.activation(rstd, rstd, ACT.Exp, scale=-0.5).then_inc(*norm_rs.up())

            act.wait_ge(*x_new(0, 16))
            for kb in range(KB):
                square(kb)

            with act.Fori(0, DEPTH) as l:
                def hi(t):
                    if t >= 2:
                        act.wait_ge(*blocks(l, 2 * (t - 1)))
                    act.wait_ge(w_in[t % RAW], l * (16 * (NTILES // RAW)) + 16 * (t // RAW + 1))
                    cp(whi[:, t % 2, :], wraw[:, t % RAW, :]).then_inc(*w_hi.up())

                def ahead(t):
                    if t + 2 < NTILES:
                        hi(t + 2)

                def came(t, b=0):
                    act.wait_ge(*blocks(l, 2 * t + 2 if PLAN[t][0] != "branch" else 2 * t + 1 + b))
                    return pj[(BLOCK[t] + b) % 2]

                act.wait_ge(*x_new(l, 16))
                act.dma_start(prm[:, :], par[l, :, :]).then_inc(*params_in.up(16))
                act.dma_start(abw, wab[l, :, :]).then_inc(*params_in.up(16))
                act.preload_act_table_set(LN_EXP)
                rms(l)
                hi(0)
                for kb in range(KB):
                    act.wait_ge(*norm_t(l, kb + 1))
                    cp(hnh[:, kb, :], sq[:, kb, :]).then_inc(*hn_hi.up())
                    if kb == 1:
                        hi(1)
                act.wait_ge(*params_in(l, 32))
                cp(abh[:, 0:KB * 8], abw).then_inc(*ab_hi.up())

                def small_first():
                    act.wait_ge(*g_s1(l, 3))
                    act.activation(sm[:, 3, :], sm[:, 1, :], ACT.Exp).then_inc(*g_s2.up())
                    act.activation(sm[:, 4, :], sm[:, 2, :], ACT.Exp).then_inc(*g_s2.up())
                    act.activation(sm[:, 5, :], prm[:, PAR["alog"]:PAR["alog"] + 16], ACT.Exp).then_inc(*g_s2.up())
                    act.wait_ge(*g_s2(l, 1))
                    act.activation(sm[:, 3, :], sm[:, 3, :], ACT.Ln, bias=1.0).then_inc(*g_s2.up())

                def small_last():
                    act.wait_ge(*g_s5(l, 1))
                    act.activation(sm[:, 9, :], mx[5][:, 0:16], ACT.Exp).then_inc(*g_s4.up())

                for t in range(0, 16):
                    what, i = PLAN[t]
                    if what != "sbz":
                        bank = came(t)
                        if what == "sbq":
                            if t == 0:
                                act.wait_ge(*hn_lo(l, 4))
                                act.wait_ge(*hn_lo_p(l, 4))
                            cp(sbq[:, i, :], bank[:, :], scale=SBD ** -0.5).then_inc(*act_took.up())
                        elif what == "sbk":
                            cp(sbk[:, i, :], bank[:, :]).then_inc(*act_took.up())
                        else:
                            cp(sbv[:, i, :], bank[:, :]).then_inc(*act_took.up())
                    ahead(t)
                    if t == 1:
                        act.wait_ge(*ab_cm(l, 1))
                        cp(abt, mx[4][:, :]).then_inc(*ab_t.up())
                    if t == 3:
                        small_first()
                    if t == 5:
                        small_last()
                    if t == 13:
                        act.wait_ge(*sb_zero(l, 1))
                        for i in range(4):
                            act.wait_ge(*v_tr(l, i + 1))
                            v = blk(mx[i][:, :])
                            cp(vpad[:, :, 2 * i, 0:64], v[:, :, 0:64])
                            cp(vpad[:, :, 2 * i + 1, 64:128], v[:, :, 64:128]).then_inc(*v_tm.up())

                def take(t):
                    what, i = PLAN[t]
                    if what in ("rq", "rk"):
                        j = i + (2 if what == "rk" else 0)
                        cp(rraw[:, j, :], came(t)[:, :], scale=0.125 if what == "rk" else 1.0).then_inc(*act_took.up())
                    elif what == "rv":
                        cp(rv[:, i, :], came(t)[:, :]).then_inc(*act_took.up())
                    elif what == "gate":
                        if i >= 16:
                            act.activation(gates[:, i - 16, :], came(t)[:, :], ACT.Tanh, scale=0.5).then_inc(*act_took.up())
                            ahead(t)
                            return
                        if i >= 10:
                            act.wait_ge(*mrg_acc(l, i - 9))
                        elif i >= 2:
                            n = BLOCK[SB_OUT + 3 * ((i - 2) // 2) + 2] + i % 2
                            act.wait_ge(*dve_took(l, TAKEN[n][1]))
                        act.activation(tg[:, i % 2, :], came(t)[:, :], ACT.Tanh, scale=0.5).then_inc(*act_took.up())
                    ahead(t)

                act.wait_ge(*dve_took(l, 4))
                act.activation(zA[:, :, :], zA[:, :, :], ACT.Silu).then_inc(*silu_a.up())
                act.preload_act_table_set(LN_EXP)

                def sb_softplus(u):
                    j = u % 3
                    e = sbe[:, u % 2, 0:UNIT_W[j]]
                    act.wait_ge(*sb_min(l, u + 1))
                    act.activation(e, e, ACT.Exp).then_inc(*sb_e.up())
                    act.wait_ge(*sb_e(l, u + 1))
                    act.activation(e, e, ACT.Ln, bias=1.0).then_inc(*sb_l.up())

                def sb_weights(u):
                    j = u % 3
                    act.wait_ge(*sb_s(l, u + 1))
                    if u >= 2:
                        act.wait_ge(*sb_o(l, u - 1))
                    act.activation(sbw[:, u % 2, 0:UNIT_W[j]], mx[u % 5][:, 0:UNIT_W[j]], ACT.Exp).then_inc(*sb_w.up())

                for u in range(NU + 2):
                    if u < NU:
                        sb_softplus(u)
                    if u >= 2:
                        sb_weights(u - 2)
                    if u >= 2 and u % 2 == 0:
                        take(16 + u // 2 - 1)

                def y_split(b, i, src, n):
                    act.wait_ge(*y_ready(l, n + 1))
                    cp(yh[:, i, :], src).then_inc(*y_hi.up())

                for c in range(4):
                    y_split(0, c, zA[:, c, :], c)

                act.wait_ge(*dve_took(l, 8))
                act.activation(zB[:, :, :], zB[:, :, :], ACT.Silu).then_inc(*silu_b.up())
                for h in range(RH):
                    act.wait_ge(*rv_tr(l, h + 1))
                    cp(rv[:, h, :], mx[h][:, :]).then_inc(*rv_tm.up())
                act.preload_act_table_set(LN_EXP)

                def decay(h):
                    act.activation(rdec[:, h % 2, :], diff, ACT.Exp,
                                   scale=math.log(1.0 - 2.0 ** (-5.0 - h))).then_inc(*r_dec.up())

                act.wait_ge(*sb_s(l, NU))
                decay(0)
                decay(1)
                for h in range(RH):
                    take(SB_OUT + 3 * h)
                    act.wait_ge(*r_o(l, h + 1))
                    if h >= 2:
                        act.wait_ge(*r_y(l, h - 1))
                    cp(ro[:, h % 2, :], mx[3 + h % 2][:, :]).then_inc(*r_os.up())
                    take(SB_OUT + 3 * h + 1)
                    act.wait_ge(*r_xc(l, h + 1))
                    act.activation(rsq[:, h % 2, :], ro[:, h % 2, :], ACT.Square).then_inc(*r_sq.up())
                    act.preload_act_table_set(LN_EXP)
                    if h + 2 < RH:
                        act.wait_ge(*r_sc(l, 3 * (h + 1)))
                        decay(h + 2)
                    act.wait_ge(*r_var(l, h + 1))
                    act.activation(rrs[:, h % 2, :], mx[5][:, :], ACT.Ln, bias=eps[:, :], scale=-1.0 / P).then_inc(*r_ln.up())
                    act.wait_ge(*r_ln(l, h + 1))
                    act.activation(rrs[:, h % 2, :], rrs[:, h % 2, :], ACT.Exp, scale=-0.5).then_inc(*r_rs.up())
                    ahead(SB_OUT + 3 * h + 2)
                act.wait_ge(*blocks(l, 2 * (SB_OUT + 12)))
                for c in range(4):
                    y_split(1, c, zB[:, c, :], 4 + c)

                for t in range(FIRST["gqkv"], FIRST["gqkv"] + 12):
                    i = t - FIRST["gqkv"]
                    bank = came(t)
                    if i == 0:
                        act.wait_ge(*g_pad(l, 1))
                    if i >= 2:
                        act.wait_ge(*g_cv(l, 4 * (i - 1)))
                    cp(cin[:, i % 2, 3:3 + T], bank[:, :]).then_inc(*act_took.up())
                    ahead(t)
                    if i >= 1:
                        act.wait_ge(*g_cv(l, 4 * i))
                        act.activation(gqkv[:, i - 1, :], cacc[:, (i - 1) % 2, :], ACT.Silu).then_inc(*g_silu.up())
                act.wait_ge(*g_cv(l, 48))
                act.activation(gqkv[:, 11, :], cacc[:, 1, :], ACT.Silu).then_inc(*g_silu.up())
                act.preload_act_table_set(LN_EXP)
                for n in range(8):
                    if n and n % 2 == 0:
                        ahead(FIRST["gz"] + n // 2 - 1)
                    act.wait_ge(*g_silu(l, n + 1))
                    if n >= 2:
                        act.wait_ge(*g_ss(l, n - 1))
                    act.activation(ed[:, n % 2, :], gqkv[:, n, :], ACT.Square).then_inc(*g_sq.up())
                    act.wait_ge(*g_ss(l, n + 1))
                    if n >= 2:
                        act.wait_ge(*g_nrm(l, n - 1))
                    act.activation(ed[:, 2 + n % 2, :], mx[2 + n % 2][:, :], ACT.Ln, bias=eps[:, :], scale=-1.0).then_inc(*g_ln.up())
                    act.wait_ge(*g_ln(l, n + 1))
                    act.activation(ed[:, 2 + n % 2, :], ed[:, 2 + n % 2, :], ACT.Exp, scale=-0.5).then_inc(*g_rs.up())
                ahead(FIRST["gz"] + 3)
                act.wait_ge(*g_nrm(l, 8))
                def rs(h):
                    act.wait_ge(*n_ss(l, h + 1))
                    if h >= 2:
                        act.wait_ge(*n_t(l, h - 1))
                    act.activation(ed[:, 2 + h % 2, :], mx[h % 2][:, :], ACT.Ln, bias=eps[:, :], scale=-1.0 / P).then_inc(*n_ln.up())
                    act.wait_ge(*n_ln(l, h + 1))
                    act.activation(ed[:, 2 + h % 2, :], ed[:, 2 + h % 2, :], ACT.Exp, scale=-0.5).then_inc(*n_rs.up())

                for h in range(GH):
                    act.wait_ge(*g_x(l, h + 1))
                    if h >= 2:
                        act.wait_ge(*g_prep(l, 8 * (h - 1)))
                    act.activation(ed[:, h % 2, :], mx[0][:, :], ACT.Exp).then_inc(*g_E.up())
                    act.wait_ge(*g_kd0(l, h + 1))
                    act.activation(sm[:, 11, 4 * h:4 * h + 4], sm[:, 12, 4 * h:4 * h + 4], ACT.Exp).then_inc(*g_kds.up())
                    act.wait_ge(*g_xm(l, h + 1))
                    for tb in range(TB):
                        a = act.activation(ed[:, 2 + h % 2, tb * P:(tb + 1) * P], mx[0][:, tb * P:(tb + 1) * P], ACT.Exp,
                                           bias=sm[:, 8, 4 * h + tb:4 * h + tb + 1])
                    a.then_inc(*g_dec.up())
                for lv in range(LEVELS):
                    for half in range(2):
                        f = 2 * lv + half
                        if f < 12:
                            take(RET_OUT + f) if PLAN[RET_OUT + f][0] == "gate" else ahead(RET_OUT + f)
                for h in range(GH):
                    act.wait_ge(*g_wt(l, h + 1))
                    cp(gLT[:, h, :], mx[2 + h % 2][:, :], scale=-1.0).then_inc(*g_wts.up())
                act.wait_ge(*dve_took(l, TAKEN[BLOCK[FIRST["gz"] + 3]][1]))
                act.activation(zA[:, :, :], zA[:, :, :], ACT.Silu).then_inc(*silu_a.up())
                for tb in range(TB):
                    act.wait_ge(*g_v(l, tb + 1))
                    if tb >= 1:
                        act.wait_ge(*g_o(l, tb))
                        act.wait_ge(*g_s(l, tb))
                    cp(ed[:, 2, :], mx[0][:, :]).then_inc(*g_vn.up())
                    take(GATES + tb)
                take(GATES + 4)
                act.preload_act_table_set(LN_EXP)
                for h in range(GH):
                    act.wait_ge(*g_o(l, TB))
                    if h >= 2:
                        act.wait_ge(*n_ss(l, h - 1))
                    act.activation(ed[:, h % 2, :], mx[2 + h][:, :], ACT.Square).then_inc(*n_sq.up())
                    if h >= 1:
                        rs(h - 1)
                rs(GH - 1)
                take(GATES + 5)
                take(GATES + 6)
                act.wait_ge(*blocks(l, 2 * (RET_OUT + 12)))
                for h in range(GH):
                    y_split(2, h, zA[:, h, :], 8 + h)
                take(GATES + 7)
                for g in range(4):
                    ahead(GDN_OUT + g)
                    for kb in (2 * g, 2 * g + 1):
                        act.wait_ge(*mrg_acc(l, 8 + kb + 1))
                        cp(hnh[:, kb, :], mrg[:, kb, :], scale=0.5).then_inc(*m_hi.up())
                for d in range(KB):
                    ahead(FIRST["wout"] + d)
                    act.wait_ge(*x_new(l, 16 + 2 * (d + 1)))
                    square(d)

            act.preload_act_table_set(LN_EXP)
            rms(DEPTH)

        @block.vector
        def _(dve):
            dve.memset(eps[:, :], EPS)
            dve.memset(abh[:, KB * 8:].bitcast(F32), 0.0)
            dve.memset(abl[:, KB * 8:].bitcast(F32), 0.0).then_inc(consts_up, 1)

            def norm_scale(l, g, kb):
                dve.scalar_tensor_tensor(out=sq[:, kb, :], in0=x[:, kb, :], scalar=g, in1=rstd,
                                         op0=ALU.mult, op1=ALU.mult).then_inc(*norm_t.up())

            with dve.Fori(0, DEPTH) as l:
                def came(t, b=0):
                    dve.wait_ge(*blocks(l, 2 * t + 2 if PLAN[t][0] != "branch" else 2 * t + 1 + b))
                    return pj[(BLOCK[t] + b) % 2]

                dve.wait_ge(*norm_rs(l, 1))
                dve.wait_ge(*params_in(l, 32))

                def hn_low(kb):
                    dve.wait_ge(*hn_hi(l, kb + 1))
                    dve.tensor_tensor(hnl[:, kb, :], sq[:, kb, :], hnh[:, kb, :], ALU.subtract).then_inc(*hn_lo.up())

                for kb in range(KB):
                    norm_scale(l, prm[:, PAR["norm"] + kb:PAR["norm"] + kb + 1], kb)
                    if kb % 2:
                        hn_low(kb - 1)
                dve.wait_ge(*hn_lo(l, 4))
                dve.wait_ge(*ab_hi(l, 1))
                dve.tensor_tensor(abl[:, 0:KB * 8], abw, abh[:, 0:KB * 8], ALU.subtract).then_inc(*ab_lo.up())
                dve.memset(area(4096, 4096), 0.0).then_inc(*sb_zero.up())

                ab = blk(mx[5][:, :])

                def heads(ap):
                    return ap.rearrange("p (h t) -> p t h", h=GH)

                dve.wait_ge(*g_ab(l, 1))
                dve.tensor_tensor(heads(sm[:, 0, :]), ab[:, :, 4:8],
                                  heads(prm[:, PAR["dtb"]:PAR["dtb"] + 16]), ALU.add).then_inc(*g_s1.up())
                dve.tensor_scalar(heads(sm[:, 2, :]), ab[:, :, 0:4], -1.0, 80.0, ALU.mult, ALU.min).then_inc(*g_s1.up())
                dve.wait_ge(*g_s1(l, 1))
                dve.tensor_scalar(sm[:, 1, :], sm[:, 0, :], 40.0, None, ALU.min).then_inc(*g_s1.up())
                dve.wait_ge(*g_s2(l, 4))
                dve.tensor_tensor(sm[:, 6, :], sm[:, 3, :], sm[:, 0, :], ALU.max).then_inc(*g_s3.up())
                dve.tensor_scalar(sm[:, 4, :], sm[:, 4, :], 1.0, None, ALU.add).then_inc(*g_s3.up())
                dve.wait_ge(*g_s3(l, 1))
                dve.scalar_tensor_tensor(out=sm[:, 6, :], in0=sm[:, 6, :], scalar=-1.0, in1=sm[:, 5, :],
                                         op0=ALU.mult, op1=ALU.mult).then_inc(*g_s3.up())
                dve.wait_ge(*g_s3(l, 2))
                dve.reciprocal(sm[:, 7, :], sm[:, 4, :]).then_inc(*g_s3.up())
                dve.wait_ge(*g_gc(l, 1))
                dve.tensor_scalar(sm[:, 8, :], mx[5][:, 0:16], -1.0, None, ALU.mult).then_inc(*g_s5.up())
                dve.wait_ge(*g_s4(l, 1))
                dve.tensor_tensor(sm[:, 10, :], sm[:, 7, :], sm[:, 9, :], ALU.mult).then_inc(*g_s5.up())

                def take_z(t, dst):
                    bank = came(t)
                    dve.tensor_copy(dst[:, PLAN[t][1], :], bank[:, :]).then_inc(*dve_took.up())

                for t in range(12, 16):
                    take_z(t, zA)

                def sb_clamp(u):
                    j = u % 3
                    dve.wait_ge(*sb_z(l, u + 1))
                    if u >= 2:
                        dve.wait_ge(*sb_sp(l, u - 1))
                    dve.tensor_scalar(sbe[:, u % 2, 0:UNIT_W[j]], mx[u % 5][:, 0:UNIT_W[j]], 40.0, None, ALU.min)\
                       .then_inc(*sb_min.up())

                def sb_softplus(u):
                    j, h = u % 3, u // 3
                    dve.wait_ge(*sb_l(l, u + 1))
                    if h >= 2:
                        dve.wait_ge(*sb_s(l, 3 * (h - 1)))
                    dve.tensor_tensor(sbsp[:, h % 2, UNIT_AT[j]:UNIT_AT[j] + UNIT_W[j]], sbe[:, u % 2, 0:UNIT_W[j]],
                                      mx[u % 5][:, 0:UNIT_W[j]], ALU.max).then_inc(*sb_sp.up())

                def y_low(i, src, n):
                    dve.wait_ge(*y_hi(l, n + 1))
                    dve.tensor_tensor(yl[:, i, :], src, yh[:, i, :], ALU.subtract).then_inc(*y_lo.up())

                for u in range(NU + 2):
                    if u < NU:
                        sb_clamp(u)
                    if 1 <= u <= NU:
                        sb_softplus(u - 1)
                    if u >= 9 and u % 6 == 3:
                        c = u // 6 - 1
                        dve.wait_ge(*sb_o(l, 6 * c + 6))
                        if c == 0:
                            dve.wait_ge(*silu_a(l, 1))
                        dve.tensor_tensor(zA[:, c, :], mx[5][:, :], zA[:, c, :], ALU.mult).then_inc(*y_ready.up())
                    if u >= 2 and u % 2 == 0 and PLAN[16 + u // 2 - 1][0] == "rz":
                        take_z(16 + u // 2 - 1, zB)
                dve.wait_ge(*sb_o(l, NU))
                dve.tensor_tensor(zA[:, 3, :], mx[5][:, :], zA[:, 3, :], ALU.mult).then_inc(*y_ready.up())
                for c in range(4):
                    y_low(c, zA[:, c, :], c)

                def take_branch(t, b):
                    for i in range(2):
                        d = 2 * (PLAN[t][1] % 4) + i
                        bank = came(t, i)
                        gate = gates[:, d, :] if b == 2 else tg[:, i, :]
                        dve.wait_ge(*act_took(l, TAKEN[BLOCK[GATES + d if b == 2 else t - 2 + i]][1]))
                        if b == 0:
                            dve.scalar_tensor_tensor(out=mrg[:, d, :], in0=tg[:, i, :], scalar=1.0, in1=bank[:, :],
                                                     op0=ALU.add, op1=ALU.mult).then_inc(*dve_took.up())
                            continue
                        dve.scalar_tensor_tensor(out=gate, in0=gate, scalar=1.0, in1=bank[:, :],
                                                 op0=ALU.add, op1=ALU.mult).then_inc(*dve_took.up())
                        dve.wait_ge(*dve_took(l, TAKEN[BLOCK[t] + i][1]))
                        dve.tensor_tensor(mrg[:, d, :], mrg[:, d, :], gate, ALU.add).then_inc(*mrg_acc.up())

                for i in range(4):
                    dve.wait_ge(*rr(l, i + 1))
                    if i >= 1:
                        dve.wait_ge(*rrd(l, i))
                    dve.tensor_tensor(rtmp[:, 0, :], rraw[:, i, :], cos, ALU.mult).then_inc(*rt1.up())
                    dve.tensor_tensor(rtmp[:, 1, :], mx[4 + i % 2][:, :], sin, ALU.mult).then_inc(*rt2.up())
                    dve.wait_ge(*rt1(l, i + 1))
                    dve.wait_ge(*rt2(l, i + 1))
                    dve.tensor_tensor(rrot[:, i, :], rtmp[:, 0, :], rtmp[:, 1, :], ALU.add).then_inc(*rrd.up())
                for h in range(RH):
                    dve.wait_ge(*r_dec(l, h + 1))
                    if h >= 2:
                        dve.wait_ge(*r_o(l, h - 1))
                    for j in range(3):
                        dve.wait_ge(*r_scores(l, 3 * h + j + 1))
                        for kb, at in UNITS[j]:
                            w = WIDTH[kb]
                            d = dve.tensor_tensor(rsc[:, h % 2, UNIT_AT[j] + at:UNIT_AT[j] + at + w],
                                                  mx[j][:, at:at + w], rdec[:, h % 2, 0:w], ALU.mult)
                        d.then_inc(*r_sc.up())
                    dve.wait_ge(*r_mu(l, h + 1))
                    dve.wait_ge(*r_os(l, h + 1))
                    dve.scalar_tensor_tensor(out=ro[:, h % 2, :], in0=mx[5][:, :], scalar=1.0 / P, in1=ro[:, h % 2, :],
                                             op0=ALU.mult, op1=ALU.add).then_inc(*r_xc.up())
                    take_branch(SB_OUT + 3 * h + 2, 0)
                    dve.wait_ge(*r_rs(l, h + 1))
                    dve.tensor_tensor(ro[:, h % 2, :], ro[:, h % 2, :], rrs[:, h % 2, :], ALU.mult).then_inc(*r_y.up())
                    dve.wait_ge(*r_y(l, h + 1))
                    if h == 0:
                        dve.wait_ge(*silu_b(l, 1))
                    dve.tensor_tensor(zB[:, h, :], ro[:, h % 2, :], zB[:, h, :], ALU.mult).then_inc(*y_ready.up())
                dve.wait_ge(*y_ready(l, 8))
                dve.memset(cin[:, :, 0:3], 0.0).then_inc(*g_pad.up())
                for c in range(4):
                    y_low(c, zB[:, c, :], 4 + c)

                for i in range(12):
                    dve.wait_ge(*act_took(l, TAKEN[BLOCK[FIRST["gqkv"] + i]][1]))
                    if i >= 2:
                        dve.wait_ge(*g_silu(l, i - 1))
                    for j in range(4):
                        w = prm[:, PAR["conv"] + 4 * i + j:PAR["conv"] + 4 * i + j + 1]
                        if j == 0:
                            dve.tensor_scalar(cacc[:, i % 2, :], cin[:, i % 2, 0:T], w, None, ALU.mult).then_inc(*g_cv.up())
                        else:
                            dve.wait_ge(*g_cv(l, 4 * i + j))
                            dve.scalar_tensor_tensor(out=cacc[:, i % 2, :], in0=cin[:, i % 2, j:j + T], scalar=w,
                                                     in1=cacc[:, i % 2, :], op0=ALU.mult, op1=ALU.add).then_inc(*g_cv.up())
                for n in range(8):
                    if n and n % 2 == 0:
                        take_z(FIRST["gz"] + n // 2 - 1, zA)
                    dve.wait_ge(*g_rs(l, n + 1))
                    dve.scalar_tensor_tensor(out=gqkv[:, n, :], in0=gqkv[:, n, :], scalar=P ** -0.5 if n < 4 else 1.0,
                                             in1=ed[:, 2 + n % 2, :], op0=ALU.mult, op1=ALU.mult).then_inc(*g_nrm.up())

                take_z(FIRST["gz"] + 3, zA)

                def wide(ap):
                    return ap.unsqueeze(2).broadcast_to((P, TB, P))

                for h in range(GH):
                    col = slice(4 * h, 4 * h + 4)
                    E, dec = ed[:, h % 2, :], ed[:, 2 + h % 2, :]
                    dve.wait_ge(*g_x(l, h + 1))
                    dve.wait_ge(*g_E(l, h + 1))
                    dve.tensor_copy(sm[:, 13, col], blk(mx[0][:, :])[:, :, P - 1]).then_inc(*g_gl.up())
                    dve.wait_ge(*g_gl(l, h + 1))
                    dve.tensor_tensor(sm[:, 12, col], sm[:, 13, col], sm[:, 8, col], ALU.add).then_inc(*g_kd0.up())
                    dve.tensor_copy(gel[:, h, :], blk(E)[:, :, P - 1]).then_inc(*g_prep.up())
                    dve.wait_ge(*g_kt(l, h + 1))
                    dve.tensor_tensor(blk(kbg[:, h, :]), blk(mx[4][:, :]), wide(sm[:, 10, col]), ALU.mult).then_inc(*g_prep.up())
                    dve.wait_ge(*g_qk(l, h + 1))
                    dve.wait_ge(*g_kds(l, h + 1))
                    dve.tensor_tensor(blk(gk[:, h, :]), blk(mx[4][:, :]), wide(sm[:, 11, col]), ALU.mult).then_inc(*g_prep.up())
                    dve.wait_ge(*g_vt(l, h + 1))
                    dve.tensor_tensor(blk(gv[:, h, :]), blk(mx[5][:, :]), wide(sm[:, 7, col]), ALU.mult).then_inc(*g_prep.up())
                    dve.tensor_tensor(gq[:, h, :], gq[:, h, :], E, ALU.mult).then_inc(*g_prep.up())
                    dve.wait_ge(*g_dec(l, h + 1))
                    dve.tensor_tensor(gLT[:, h, :], mx[2][:, :], dec, ALU.mult).then_inc(*g_prep.up())
                    dve.tensor_tensor(gsc[:, h, :], mx[3][:, :], dec, ALU.mult).then_inc(*g_prep.up())
                    dve.wait_ge(*g_prep(l, 8 * h + 6))
                    dve.wait_ge(*g_bb(l, h + 1))
                    dve.tensor_tensor(gLT[:, h, :], gLT[:, h, :], mx[1][:, :], ALU.mult).then_inc(*g_prep.up())

                def rep(ap):
                    return ap.unsqueeze(1).broadcast_to((P, TB, P))

                identb = rep(ident)
                for lv in range(LEVELS):
                    mask = rep(con[:, C_LEVEL + P * lv:C_LEVEL + P * (lv + 1)])
                    for pair in range(2):
                        for h in (2 * pair, 2 * pair + 1):
                            dve.wait_ge(*g_P(l, GH * lv + h + 1))
                            if h >= 2:
                                if lv:
                                    dve.wait_ge(*g_AB(l, GH * (lv - 1) + h - 1))
                                else:
                                    dve.wait_ge(*g_X(l, h - 1))
                            dve.tensor_tensor(blk(ed[:, h % 2, :]), blk(mx[3 * (h % 2)][:, :]), mask, ALU.mult).then_inc(*g_Pm.up())
                            if lv == 0:
                                dve.wait_ge(*g_Pm(l, h + 1))
                                dve.tensor_tensor(blk(gX[:, h, :]), identb, blk(ed[:, h % 2, :]), ALU.subtract).then_inc(*g_X.up())
                                dve.tensor_tensor(blk(gXT[:, h, :]), blk(gLT[:, h, :]), rep(const("m1t")), ALU.mult).then_inc(*g_XT.up())
                                dve.wait_ge(*g_XT(l, 2 * h + 1))
                                dve.tensor_tensor(blk(gXT[:, h, :]), identb, blk(gXT[:, h, :]), ALU.subtract).then_inc(*g_XT.up())
                        if lv:
                            for h in (2 * pair, 2 * pair + 1):
                                dve.wait_ge(*g_AB(l, GH * (lv - 1) + h + 1))
                                if lv < LEVELS - 1:
                                    dve.tensor_tensor(gX[:, h, :], gX[:, h, :], mx[3 * (h % 2) + 1][:, :], ALU.subtract).then_inc(*g_X.up())
                                dve.tensor_tensor(gXT[:, h, :], gXT[:, h, :], mx[3 * (h % 2) + 2][:, :], ALU.subtract).then_inc(*g_XT.up())
                        f = 2 * lv + pair
                        if f < 12 and PLAN[RET_OUT + f][0] == "branch":
                            take_branch(RET_OUT + f, 1)
                for tb in range(TB - 1):
                    dve.wait_ge(*g_s(l, tb + 1))
                    if tb == 0:
                        dve.tensor_copy(gS[:, :, :], blk(mx[1][:, :])).then_inc(*g_su.up())
                    else:
                        dve.tensor_tensor(gS[:, :, :], gS[:, :, :], gel[:, :, tb].unsqueeze(2).broadcast_to((P, GH, P)),
                                          ALU.mult).then_inc(*g_s0.up())
                        dve.wait_ge(*g_s0(l, tb))
                        dve.tensor_tensor(gS[:, :, :], gS[:, :, :], blk(mx[1][:, :]), ALU.add).then_inc(*g_su.up())
                for h in range(GH):
                    dve.wait_ge(*n_rs(l, h + 1))
                    dve.scalar_tensor_tensor(out=gXT[:, h, :], in0=mx[2 + h][:, :], scalar=prm[:, PAR["gain"]:PAR["gain"] + 1],
                                             in1=ed[:, 2 + h % 2, :], op0=ALU.mult, op1=ALU.mult).then_inc(*n_t.up())
                    dve.wait_ge(*n_t(l, h + 1))
                    if h == 0:
                        dve.wait_ge(*silu_a(l, 2))
                    dve.tensor_tensor(zA[:, h, :], gXT[:, h, :], zA[:, h, :], ALU.mult).then_inc(*y_ready.up())
                for h in range(GH):
                    y_low(h, zA[:, h, :], 8 + h)
                def merged_low(kb):
                    dve.wait_ge(*m_hi(l, kb + 1))
                    dve.scalar_tensor_tensor(out=hnl[:, kb, :], in0=mrg[:, kb, :], scalar=0.5, in1=hnh[:, kb, :],
                                             op0=ALU.mult, op1=ALU.subtract).then_inc(*m_lo.up())

                for g in range(4):
                    take_branch(GDN_OUT + g, 2)
                    if g:
                        merged_low(2 * g - 2)
                        merged_low(2 * g - 1)
                merged_low(6)
                merged_low(7)
                for d in range(KB):
                    bank = came(FIRST["wout"] + d)
                    dve.tensor_tensor(x[:, d, :], x[:, d, :], bank[:, :], ALU.add).then_inc(*x_new.up(2))

            dve.wait_ge(*norm_rs(DEPTH, 1))
            dve.wait_ge(consts_in, 32)
            for kb in range(KB):
                norm_scale(DEPTH, fing[:, kb:kb + 1], kb)

        @block.tensor
        def _(pe):
            def mm(o, w, a, start, stop):
                return pe.matmul(o, w, a, start=start, stop=stop, skip_group_check=True)

            def mm3(o, w, a, start, stop):
                mm(o, w[0], a[0], start, False)
                mm(o, w[0], a[1], False, False)
                return mm(o, w[1], a[0], False, stop)

            def square_sum(kb):
                m = mm(mx[0][:, :], const("nones"), sq[:, kb, :], kb == 0, kb == KB - 1)
                if kb == KB - 1:
                    m.then_inc(*norm_sum.up())

            pe.wait_ge(consts_in, 32)
            pe.wait_ge(consts_up, 4)
            for kb in range(KB):
                pe.wait_ge(*norm_sq(0, kb + 1))
                square_sum(kb)
            with pe.Fori(0, DEPTH) as l:
                def wpair(t, a, b, kn, n):
                    s = t % 2
                    return [w[:, s, :].rearrange("p (k n) -> p k n", k=kn)[:, a, b:b + n] for w in (whi, wlo)]

                def hn(kb, c0=0, n=T):
                    return [hnh[:, kb, c0:c0 + n], hnl[:, kb, c0:c0 + n]]

                def free(n):
                    if n >= 2:
                        who, k = TAKEN[n - 2]
                        pe.wait_ge(*by(who)(l, 2 * k + 16 if who == "x" else k))

                def half(t, b):
                    what, i = PLAN[t]
                    n = BLOCK[t]
                    if b == 0:
                        pe.wait_ge(*w_hi(l, t + 1))
                        pe.wait_ge(*w_lo(l, t + 1))
                    if what == "branch":
                        free(n + b)
                        for c in range(4):
                            m = mm3(pj[(n + b) % 2][:, :], wpair(t, c, P * b, 4, P), [yh[:, c, :], yl[:, c, :]], c == 0, c == 3)
                        m.then_inc(*blocks.up())
                        return
                    if b == 0:
                        free(n)
                    for kb in range(4 * b, 4 * b + 4):
                        if t == 0:
                            pe.wait_ge(*(hn_lo_p if kb % 2 else hn_lo)(l, kb // 2 + 1))
                        if t == FIRST["wout"]:
                            pe.wait_ge(*m_lo(l, kb + 1))
                        m = mm3(pj[n % 2][:, :], wpair(t, kb, 0, KB, P), hn(kb), kb == 0, kb == KB - 1)
                    if b == 1:
                        m.then_inc(*blocks.up(2))

                def tile(t):
                    half(t, 0)
                    half(t, 1)

                def four_turned(bank, src):
                    for tb in range(TB):
                        m = pe.transpose(bank[:, tb * P:(tb + 1) * P], src[:, tb * P:(tb + 1) * P], ident)
                    return m

                tile(0)
                pe.wait_ge(*ab_lo(l, 1))
                for kb in range(KB):
                    m = mm3(mx[4][:, :], [w[:, 8 * kb:8 * kb + P] for w in (abh, abl)], hn(kb), kb == 0, kb == KB - 1)
                m.then_inc(*ab_cm.up())
                tile(1)
                pe.wait_ge(*ab_t(l, 1))
                four_turned(mx[5], abt).then_inc(*g_ab.up())
                for t in range(2, 5):
                    tile(t)
                pe.wait_ge(*g_s3(l, 4))
                mm(mx[5][:, 0:16], const("triu"), sm[:, 6, :], True, True).then_inc(*g_gc.up())
                for t in range(5, 13):
                    tile(t)
                for i in range(4):
                    pe.wait_ge(*act_took(l, TAKEN[BLOCK[FIRST["sbv"] + i]][1]))
                    four_turned(mx[i], sbv[:, i, :]).then_inc(*v_tr.up())
                for t in range(13, 16):
                    tile(t)

                def sb_scores(u):
                    h, j = divmod(u, 3)
                    c, po = h // 2, SBD * (h % 2)
                    if u == 0:
                        pe.wait_ge(*v_tm(l, 4))
                    if u >= 5:
                        pe.wait_ge(*sb_w(l, u - 4))
                    bank = mx[u % 5]
                    for n, (kb, at) in enumerate(UNITS[j]):
                        mm(bank[:, at:at + WIDTH[kb]], sbk[po:po + SBD, c, kb * P:(kb + 1) * P],
                           sbq[po:po + SBD, c, kb * P:T], n == 0, False)
                        m = mm(bank[:, at:at + P], ident_r, negsb_r, False, False)
                    m.then_inc(*sb_z.up())

                def sb_sums(u):
                    h, j = divmod(u, 3)
                    pe.wait_ge(*sb_sp(l, u + 1))
                    bank = mx[u % 5]
                    for kb, at in UNITS[j]:
                        for k2 in range(kb, TB):
                            lo = at + P * (k2 - kb)
                            m = mm(bank[:, lo:at + WIDTH[kb]], const("ntril") if k2 == kb else const("nones"),
                                   sbsp[:, h % 2, SP_AT[k2]:SP_AT[k2] + WIDTH[k2]], False, k2 == TB - 1)
                    m.then_inc(*sb_s.up())

                def sb_out(u):
                    h, j = divmod(u, 3)
                    pe.wait_ge(*sb_w(l, u + 1))
                    if u % 6 == 0 and u:
                        pe.wait_ge(*y_ready(l, u // 6))
                    for n, (kb, at) in enumerate(UNITS[j]):
                        m = mm(mx[5][:, kb * P:T], vpad[:, kb, h, :], sbw[:, u % 2, at:at + WIDTH[kb]],
                               u % 6 == 0 and n == 0, u % 6 == 5)
                    m.then_inc(*sb_o.up())

                for u in range(NU + 3):
                    if u < NU:
                        sb_scores(u)
                        half(16 + u // 2, u % 2)
                    if 2 <= u < NU + 2:
                        sb_sums(u - 2)
                    if u >= 3:
                        sb_out(u - 3)

                pe.wait_ge(*act_took(l, TAKEN[BLOCK[FIRST["rv"] + 3]][1]))
                pe.wait_ge(*sb_w(l, NU))
                for h in range(RH):
                    four_turned(mx[h], rv[:, h, :]).then_inc(*rv_tr.up())
                pe.wait_ge(*y_ready(l, 4))
                for i in range(4):
                    if i >= 2:
                        pe.wait_ge(*rt2(l, i - 1))
                    mm(mx[4 + i % 2][:, :], const("rot"), rraw[:, i, :], True, True).then_inc(*rr.up())
                    if i == 1:
                        pe.wait_ge(*y_lo(l, 4))
                        half(SB_OUT, 0)
                for h in range(RH):
                    c, po = h // 2, 64 * (h % 2)
                    t = SB_OUT + 3 * h
                    pe.wait_ge(*rrd(l, 4))
                    for j in range(3):
                        pe.wait_ge(*(r_sc(l, 3 * (h - 1) + j + 1) if h else rv_tm(l, j + 1)))
                        for n, (kb, at) in enumerate(UNITS[j]):
                            m = mm(mx[j][:, at:at + WIDTH[kb]], rrot[po:po + 64, 2 + c, kb * P:(kb + 1) * P],
                                   rrot[po:po + 64, c, kb * P:T], n == 0, True)
                        m.then_inc(*r_scores.up())
                    if h:
                        half(t, 0)
                    half(t, 1)
                    pe.wait_ge(*r_sc(l, 3 * h + 3))
                    if h == 0:
                        pe.wait_ge(*rv_tm(l, 4))
                    if h >= 2:
                        pe.wait_ge(*r_os(l, h - 1))
                    for kb in range(TB):
                        m = mm(mx[3 + h % 2][:, kb * P:T], rv[:, h, kb * P:(kb + 1) * P],
                               rsc[:, h % 2, SP_AT[kb]:SP_AT[kb] + WIDTH[kb]], kb == 0, kb == TB - 1)
                    m.then_inc(*r_o.up())
                    tile(t + 1)
                    pe.wait_ge(*r_os(l, h + 1))
                    if h:
                        pe.wait_ge(*r_ln(l, h))
                    mm(mx[5][:, :], const("nones"), ro[:, h % 2, :], True, True).then_inc(*r_mu.up())
                    half(t + 2, 0)
                    pe.wait_ge(*r_sq(l, h + 1))
                    mm(mx[5][:, :], const("nones"), rsq[:, h % 2, :], True, True).then_inc(*r_var.up())
                    half(t + 2, 1)

                for t in range(FIRST["gqkv"], FIRST["gqkv"] + 12):
                    tile(t)
                for n in range(8):
                    pe.wait_ge(*g_sq(l, n + 1))
                    if n >= 2:
                        pe.wait_ge(*g_ln(l, n - 1))
                    mm(mx[2 + n % 2][:, :], const("nones"), ed[:, n % 2, :], True, True).then_inc(*g_ss.up())
                    half(FIRST["gz"] + n // 2, n % 2)
                pe.wait_ge(*g_nrm(l, 8))
                pe.wait_ge(*g_s5(l, 2))
                for h in range(GH):
                    def four(bank, lhs, rhs):
                        for tb in range(TB):
                            m = mm(bank[:, tb * P:(tb + 1) * P], lhs(tb), rhs(tb), tb == 0, True)
                        return m

                    def tok(buf):
                        return lambda tb: buf[:, h, tb * P:(tb + 1) * P]

                    def spread(row):
                        return lambda tb: sm[:, row, 4 * h + tb:4 * h + tb + 1].broadcast_to((P, P))

                    if h:
                        pe.wait_ge(*g_dec(l, h))
                    four(mx[0], spread(6), lambda tb: const("triu")).then_inc(*g_x.up())
                    if h:
                        pe.wait_ge(*g_prep(l, 8 * h))
                    four(mx[1], spread(7), lambda tb: ident).then_inc(*g_bb.up())
                    four(mx[2], tok(gk), tok(gk)).then_inc(*g_kk.up())
                    for tb in range(TB):
                        m = pe.transpose(mx[4][:, tb * P:(tb + 1) * P], gk[:, h, tb * P:(tb + 1) * P], ident)
                    m.then_inc(*g_kt.up())
                    four(mx[3], tok(gk), tok(gq)).then_inc(*g_qk.up())
                    for tb in range(TB):
                        m = pe.transpose(mx[5][:, tb * P:(tb + 1) * P], gv[:, h, tb * P:(tb + 1) * P], ident)
                    m.then_inc(*g_vt.up())
                    pe.wait_ge(*g_gl(l, h + 1))
                    for tb in range(TB):
                        m = mm(mx[0][:, tb * P:(tb + 1) * P], ident_r, neggdn_r, False, True)
                    m.then_inc(*g_xm.up())

                pe.wait_ge(*g_prep(l, 8 * GH))
                for lv in range(LEVELS):
                    for pair in range(2):
                        for h in (2 * pair, 2 * pair + 1):
                            b = 3 * (h % 2)
                            if lv == 0:
                                if h >= 2:
                                    pe.wait_ge(*g_Pm(l, h - 1))
                                four(mx[b], tok(gLT), lambda tb: ident).then_inc(*g_P.up())
                            else:
                                pe.wait_ge(*g_X(l, GH * (lv - 1) + h + 1))
                                pe.wait_ge(*g_Pm(l, GH * lv + h - 1))
                                four(mx[b], tok(gLT), tok(gX)).then_inc(*g_P.up())
                        f = 2 * lv + pair
                        if f < 12:
                            if f == 0:
                                pe.wait_ge(*y_lo(l, 8))
                            tile(RET_OUT + f)
                        if lv:
                            for h in (2 * pair, 2 * pair + 1):
                                b = 3 * (h % 2)
                                pe.wait_ge(*g_Pm(l, GH * lv + h + 1))
                                pe.wait_ge(*g_XT(l, GH * lv + h + (3 if h < 2 else 1)))
                                if h >= 2:
                                    pe.wait_ge(*g_XT(l, GH * (lv + 1) + h - 1))
                                pm = (lambda tb, h=h: ed[:, h % 2, tb * P:(tb + 1) * P])
                                if lv < LEVELS - 1:
                                    four(mx[b + 1], tok(gXT), pm)
                                four(mx[b + 2], pm, tok(gXT)).then_inc(*g_AB.up())
                for h in range(GH):
                    pe.wait_ge(*g_XT(l, GH * (LEVELS + 1) if h == 0 else GH * (LEVELS + 1)))
                    if h >= 2:
                        pe.wait_ge(*g_wts(l, h - 1))
                    four(mx[2 + h % 2], tok(kbg), tok(gXT)).then_inc(*g_wt.up())
                pe.wait_ge(*g_wts(l, GH))
                for tb in range(TB):
                    s = slice(tb * P, (tb + 1) * P)
                    if tb:
                        pe.wait_ge(*g_vn(l, tb))
                        pe.wait_ge(*g_su(l, tb))
                    for h in range(GH):
                        hs = slice(h * P, (h + 1) * P)
                        m = mm(mx[0][:, hs], gXT[:, h, s], gv[:, h, s], True, tb == 0)
                        if tb:
                            m = mm(mx[0][:, hs], gLT[:, h, s], gS[:, h, :], False, True)
                    m.then_inc(*g_v.up())
                    half(GATES + tb, 0)
                    if tb:
                        for h in range(GH):
                            mm(mx[2 + h][:, s], gS[:, h, :], gq[:, h, s], True, False)
                    pe.wait_ge(*g_vn(l, tb + 1))
                    if tb < TB - 1:
                        for h in range(GH):
                            m = mm(mx[1][:, h * P:(h + 1) * P], gk[:, h, s], ed[:, 2, h * P:(h + 1) * P], True, True)
                        m.then_inc(*g_s.up())
                    for h in range(GH):
                        m = mm(mx[2 + h][:, s], ed[:, 2, h * P:(h + 1) * P], gsc[:, h, s], tb == 0, True)
                    m.then_inc(*g_o.up())
                    half(GATES + tb, 1)
                tile(GATES + 4)
                for h in range(GH):
                    pe.wait_ge(*n_sq(l, h + 1))
                    if h >= 2:
                        pe.wait_ge(*n_ln(l, h - 1))
                    mm(mx[h % 2][:, :], const("nones"), ed[:, h % 2, :], True, True).then_inc(*n_ss.up())
                    half(GATES + 5 + h // 2, h % 2)
                tile(GATES + 7)
                pe.wait_ge(*y_lo(l, 12))
                for t in range(GDN_OUT, FIRST["wout"]):
                    tile(t)
                for d in range(KB):
                    tile(FIRST["wout"] + d)
                    if d >= 2:
                        pe.wait_ge(*norm_sq(l, KB + d - 1))
                        square_sum(d - 2)
                for d in (KB - 2, KB - 1):
                    pe.wait_ge(*norm_sq(l, KB + d + 1))
                    square_sum(d)

        for s in sigs:
            extra = {"norm_sq": KB, "norm_sum": 1, "norm_ln": 1, "norm_rs": 1, "norm_t": KB}.get(s.name, 0)
            want = {"w_lo": 0}.get(s.name, s.per_layer)
            assert s.n == want + extra, (s.name, s.n, s.per_layer)


def layout(inputs):
    a = {k: np.asarray(v) for k, v in inputs.items()}
    xin = np.ascontiguousarray(a["x"][0].T.reshape(KB, P, T).transpose(1, 0, 2))
    wt = np.empty((DEPTH, NTILES, P, TILE), np.float32)
    branches = (a["w_sb"], a["w_ret"], a["w_gdn"])
    for t, (what, i) in enumerate(PLAN):
        if what == "branch":
            src = branches[i // 4][:, :, 256 * (i % 4):256 * (i % 4) + 256]
        elif what == "wout":
            src = a["w_out"][:, :, P * i:P * (i + 1)]
        else:
            src = a["w_in"][:, :, OFF[what] + P * i:OFF[what] + P * (i + 1)]
        k = src.shape[1] // P
        wt[:, t] = src.reshape(DEPTH, k, P, -1).transpose(0, 2, 1, 3).reshape(DEPTH, P, TILE)
    wab = np.ascontiguousarray(a["w_in"][:, :, OFF["gab"]:OFF["gab"] + 8].reshape(DEPTH, KB, P, 8)
                               .transpose(0, 2, 1, 3).reshape(DEPTH, P, KB * 8))
    par = np.empty((DEPTH, P, PAR_END), np.float32)
    par[:, :, 0:8] = a["norm_g"].reshape(DEPTH, KB, P).transpose(0, 2, 1)
    par[:, :, 8:56] = a["conv_w"].reshape(DEPTH, 4, 12, P).transpose(0, 3, 2, 1).reshape(DEPTH, P, 48)
    par[:, :, 56] = a["gdn_norm_g"]
    par[:, :, 57:73] = np.repeat(a["dt_bias"], TB, axis=1)[:, None, :]
    par[:, :, 73:89] = np.repeat(a["a_log"], TB, axis=1)[:, None, :]
    return {"xin": xin, "wt": wt.reshape(DEPTH * NTILES // RAW, RAW, P, TILE), "wab": wab, "par": par,
            "fin": np.ascontiguousarray(a["final_g"].reshape(KB, P).T), "cst": constants()}


def kernel(**inputs):
    import concourse.bacc as _bacc
    from concourse.bass_utils import run_bass_kernel_spmd as _run

    arrays = layout(inputs)
    nc = _bacc.Bacc("TRN2", target_bir_lowering=False, num_devices=1)
    args = [nc.dram_tensor(n, v.shape, mybir.dt.float32, kind="ExternalInput").ap() for n, v in arrays.items()]
    args.append(nc.dram_tensor("out", (P, KB, T), mybir.dt.float32, kind="ExternalOutput").ap())
    trunk(nc, *args)
    r = _run(nc, [arrays], core_ids=[0])
    got = r.results[0]["out"]
    return np.ascontiguousarray(got.transpose(1, 0, 2).reshape(D, T).T)[None]
```

```python
import math

import numpy as np
import concourse.bass as bass
from concourse import mybir
from contextlib import ExitStack

F32 = mybir.dt.float32
F32R = mybir.dt.float32r
ALU = mybir.AluOpType
ACT = mybir.ActivationFunctionType

P = 128
D = 1024
T = 512
DEPTH = 2
KB = D // P
TB = T // P
SBH, SBD = 8, 64
RH = 4
GH = 4
EPS = 1e-6
WIDE = 5
TILE = 1024
RAW = 2
OFF = dict(sbq=0, sbk=512, sbv=1024, sbz=1536, rq=2048, rk=2304, rv=2560, rz=3072,
           gqkv=3584, gz=5120, gab=5632, gate=5640)
QK_SPLIT = 6
LEVELS = 7
LN_EXP = "natural_log_exp_and_others"
NEG = -1e30


def weight_plan():
    plan = [("sbq", i) for i in range(4)] + [("sbk", i) for i in range(4)]
    plan += [("sbv", i) for i in range(4)] + [("rv", i) for i in range(4)]
    plan += [("sbz", i) for i in range(4)]
    plan += [("rq", i) for i in range(2)] + [("rk", i) for i in range(2)]
    plan += [("rz", i) for i in range(4)]

    def branch(b):
        out = []
        for g in range(4):
            out += [("gate", 8 * b + 2 * g), ("gate", 8 * b + 2 * g + 1), ("branch", 4 * b + g)]
        return out

    plan += branch(0)
    plan += [("gqkv", i) for i in range(12)] + [("gz", i) for i in range(4)]
    plan += branch(1)
    plan += [("gate", 16 + i) for i in range(8)] + [("branch", 8 + i) for i in range(4)]
    plan += [("wout", i) for i in range(8)]
    return plan


PLAN = weight_plan()
NTILES = len(PLAN)
FIRST = {what: next(i for i, (w, _) in enumerate(PLAN) if w == what) for what, _ in PLAN}
SB_OUT, RET_OUT, GATES = (next(i for i, x in enumerate(PLAN) if x == ("gate", 8 * b)) for b in range(3))
GDN_OUT = GATES + 8
VECTOR_LOW = (0, 3, 6)
TOKEN_MAJOR = {"sbv": (0, 1, 2, 3), "rv": (4, 5, 2, 3)}
ON_VECTOR = ("sbz", "rz", "gz", "branch")


def block_table():
    first, taken, counts = [], [], {"act": 0, "dve": 0, "x": 0}
    for what, _ in PLAN:
        first.append(len(taken))
        for _ in range(0 if what in TOKEN_MAJOR else 2 if what == "branch" else 1):
            who = "x" if what == "wout" else "dve" if what in ON_VECTOR else "act"
            counts[who] += 1
            taken.append((who, counts[who]))
    return first, taken, counts


BLOCK, TAKEN, COUNTS = block_table()

UNITS = [[(3, 0), (2, 128)], [(1, 0)], [(0, 0)]]
WIDTH = {kb: T - P * kb for kb in range(TB)}
SC_AT = {3: 0, 2: 128, 1: 384, 0: 768}
SP_AT = [SC_AT, {3: 1280, 2: 1408, 1: 1664, 0: 768}]
UNIT_AT = [0, 384, 768]
UNIT_W = [384, 384, 512]



HALVES = [(2, 1), (1, 1), (1, 2), (1, 2), (1, 2), (1, 2), (2, 1)]


def inverse_plan():
    fill = [(RET_OUT + f, b) for f in range(2, 12) for b in range(2)]
    halves = HALVES
    steps = []
    for lv in range(LEVELS):
        for pair in range(2):
            heads = (2 * pair, 2 * pair + 1)
            mine = [("half",) + fill.pop(0) for _ in range(halves[lv][pair])]
            if lv == 0:
                steps += mine
                continue
            steps += [("P", lv, h) for h in heads]
            steps.append(mine.pop(0))
            lt, ht = (lv, (0, 1)) if pair else (lv - 1, (2, 3))
            if lt == WIDE:
                steps += [("turn", lt, h) for h in ht]
            steps += mine
            steps += [("AB", lv, h) for h in heads]
    assert not fill
    return steps


INVERSE = inverse_plan()
WT_BANK = [0, 3, 1, 4]

CONST = ["triu", "ident", "nones", "m1t", "negsb", "neggdn"]
STAGED = ["ntril"]
CC = {n: P * i for i, n in enumerate(CONST + STAGED)}
C_STAGED = P * len(CONST)
C_LEVEL = P * (len(CONST) + len(STAGED))
C_COS = C_LEVEL + P * (LEVELS - 1)
C_SIN = C_COS + T
C_DIFF = C_SIN + T
C_END = C_DIFF + T
PAR = dict(norm=0, conv=8, gain=56, dtb=57, alog=73)
PAR_END = 89


def constants():
    i = np.arange(P)
    r, c = i[:, None], i[None, :]
    out = np.zeros((P, C_END), np.float32)

    def put(name, a):
        out[:, CC[name]:CC[name] + P] = a

    put("triu", r <= c)
    put("ident", r == c)
    put("ntril", -(r >= c).astype(np.float32))
    put("nones", -1.0)
    put("negsb", np.where(r >= c, NEG, 0.0))
    put("neggdn", np.where(r > c, NEG, 0.0))

    def level(s):
        return ((r // (2 * s) == c // (2 * s)) & ((r // s) % 2 == 1) & ((c // s) % 2 == 0)).astype(np.float32)

    put("m1t", level(1).T)
    for n in range(1, LEVELS):
        out[:, C_LEVEL + P * (n - 1):C_LEVEL + P * n] = level(1 << n)
    t = np.arange(T)[None, :]
    out[:, C_DIFF:C_DIFF + T] = np.where(t >= r, t - r, 1e9)
    freq = (np.float32(10000.0) ** (-(np.arange(32, dtype=np.float32)) / np.float32(32)))
    ang = t.astype(np.float32) * freq[(i % 32)][:, None]
    out[:, C_COS:C_COS + T] = np.cos(ang.astype(np.float32))
    out[:, C_SIN:C_SIN + T] = np.sin(ang.astype(np.float32))
    return out


def trunk(nc, xin, wt, wab, par, fin, cst, out):
    ctx = ExitStack()
    sigs = []
    nc.disable_value_cache = True

    class Signal:

        def __init__(self, name, per_layer):
            self.sem = ctx.enter_context(nc.semaphore(name))
            self.name, self.per_layer, self.n = name, per_layer, 0
            sigs.append(self)

        def __call__(self, l, n):
            assert n >= 1, self.name
            return self.sem, l * self.per_layer + n

        def up(self, by=1):
            self.n += by
            return self.sem, by

    with ctx:
        def sb(name, shape, dt=F32):
            return ctx.enter_context(nc.sbuf_tensor(name, shape, dt))

        x = sb("x", [P, KB, T])
        hnh = sb("hnh", [P, KB, T], F32R)
        hnl = sb("hnl", [P, KB, T], F32R)
        wraw = sb("wraw", [P, RAW, TILE])
        whi = sb("whi", [P, 2, TILE], F32R)
        wlo = sb("wlo", [P, 2, TILE], F32R)
        con = sb("con", [P, C_DIFF - P * len(STAGED)])
        conr = sb("conr", [P, 2, P], F32R)
        prm = sb("prm", [P, PAR_END])
        fing = sb("fing", [P, KB])
        eps = sb("eps", [P, 1])
        mrg = sb("mrg", [P, KB, T])
        yh = sb("yh", [P, 4, T], F32R)
        yl = sb("yl", [P, 4, T], F32R)
        zA = sb("zA", [P, 4, T])
        zB = sb("zB", [P, 4, T])
        tg = sb("tg", [P, 2, T])
        abh = sb("abh", [P, KB * 8 + P - 8], F32R)
        abl = sb("abl", [P, KB * 8 + P - 8], F32R)
        sm = sb("sm", [P, 14, 16])
        part = sb("part", [P, 2, T], F32R)
        gel = sb("gel", [P, GH, TB])
        arena = sb("arena", [P, 16896])
        pj = [ctx.enter_context(nc.psum_tensor(f"pj{i}", [P, T], F32)) for i in range(2)]
        mx = [ctx.enter_context(nc.psum_tensor(f"mx{i}", [P, T], F32)) for i in range(6)]

        def area(at, *shape):
            n = int(np.prod(shape))
            v = arena[:, at:at + n]
            if len(shape) == 2:
                v = v.rearrange("p (a b) -> p a b", a=shape[0])
            if len(shape) == 3:
                v = v.rearrange("p (a b c) -> p a b c", a=shape[0], b=shape[1])
            return v

        def const(name):
            return con[:, CC[name]:CC[name] + P]

        ident = const("ident")
        ntril_r, nones_r = (conr[:, i, :] for i in range(2))

        def late(at, n):
            at += C_STAGED - C_LEVEL
            return con[:, at:at + n]

        cos, sin = late(C_COS, T), late(C_SIN, T)
        diff = mrg[:, KB - 1, :]
        staged = zA[:, 0, 0:P * len(STAGED)]

        sq = area(0, KB, T)
        rstd, ssq = area(4096, T), area(4608, T)
        sbq, sbk = area(0, 4, T), area(2048, 4, T)
        vpad = area(4096, TB, SBH, P)
        sby, abt = area(9216, 4, T), area(11264, T)
        abw = area(11776, KB * 8)
        sbe, sbw = area(8192, 2, T), area(11776, 2, T)
        sp_parts = [v[:, :, :].rearrange("p a b -> p (a b)") for v in (yh, yl)]
        rrot, rv, rsw = area(12800, 4, T), area(14848, TB, T), mrg
        rdec, rsc = area(2048, 2, T), area(3072, 2, 1280)
        ro, rsq, rrs = area(5632, 2, T), area(6656, 2, T), area(7680, 2, T)
        gq, gk, gv = area(0, GH, T), area(2048, GH, T), area(4096, GH, T)
        kbg, gX, gXT = area(6144, GH, T), area(8192, GH, T), area(10240, GH, T)
        gLT, gsc = area(12288, GH, T), area(14336, GH, T)
        gS = area(16384, GH, P)
        gates = area(6144, KB, T)
        cin, cacc = area(8192, 2, 516), area(10240, 2, T)
        gqkv = area(0, 12, T)
        ed = zB

        def blk(ap):
            return ap.rearrange("p (a b) -> p a b", a=TB)

        def subs(ap, lv, odd):
            return ap.rearrange("p (b o s) -> p b o s", o=2, s=1 << lv)[:, :, odd, :]

        def S(name, n):
            return Signal(name, n)

        x_in = [ctx.enter_context(nc.semaphore(f"x_in{i}")) for i in range(4)]
        late_consts_in = ctx.enter_context(nc.semaphore("late_consts_in"))
        consts_in = ctx.enter_context(nc.semaphore("consts_in"))
        consts_up = ctx.enter_context(nc.semaphore("consts_up"))
        w_in = [ctx.enter_context(nc.semaphore(f"w_in{i}")) for i in range(RAW)]
        out_done = ctx.enter_context(nc.semaphore("out_done"))
        x_new = S("x_new", 8)
        w_hi = S("w_hi", NTILES)
        w_lo = S("w_lo", NTILES)
        blocks = S("blocks", 2 * NTILES)
        act_took = S("act_took", COUNTS["act"])
        dve_took = S("dve_took", COUNTS["dve"])
        params_in = S("params_in", 32)
        norm_sq, norm_sum, norm_ln, norm_rs = S("norm_sq", 8), S("norm_sum", 1), S("norm_ln", 1), S("norm_rs", 1)
        norm_add = S("norm_add", KB - 2)
        norm_t, hn_hi, hn_lo, hn_lo_p = S("norm_t", 8), S("hn_hi", 8), S("hn_lo", 3), S("hn_lo_p", 5)
        ab_cm, ab_t, v_tm = S("ab_cm", 1), S("ab_t", 1), S("v_tm", 4)
        rv_sum, rv_mean, rv_tm, sb_y = S("rv_sum", 4), S("rv_mean", 4), S("rv_tm", 4), S("sb_y", 4)
        diff_in = S("diff_in", 16)
        ab_hi, ab_lo = S("ab_hi", 1), S("ab_lo", 1)
        sb_zero = S("sb_zero", 1)
        silu_a, silu_b = S("silu_a", 2), S("silu_b", 1)
        NU = SBH * 3
        sb_z, sb_e, sb_l, sb_min, sb_sp = S("sb_z", NU), S("sb_e", NU), S("sb_l", NU), S("sb_min", NU), S("sb_sp", NU)
        sb_mask, sb_m, sb_hi = S("sb_mask", NU), S("sb_m", NU), S("sb_hi", NU)
        sb_s, sb_w, sb_o = S("sb_s", NU), S("sb_w", NU), S("sb_o", NU)
        y_ready, y_hi, y_lo = S("y_ready", 12), S("y_hi", 12), S("y_lo", 12)
        r_swap, rt1, rt2, rrd = S("r_swap", 4), S("rt1", 4), S("rt2", 4), S("rrd", 4)
        r_dec, r_scores, r_sc, r_o = S("r_dec", RH), S("r_scores", RH * 3), S("r_sc", RH * 3), S("r_o", RH)
        r_sq, r_sq_lo = S("r_sq", RH), S("r_sq_lo", RH)
        r_var, r_ln, r_rs, r_y = S("r_var", RH), S("r_ln", RH), S("r_rs", RH), S("r_y", RH)
        mrg_acc = S("mrg_acc", 16)
        g_pad = S("g_pad", 1)
        g_cv, g_silu = S("g_cv", 48), S("g_silu", 12)
        g_ab, g_s1, g_s2, g_s3, g_gc = S("g_ab", 1), S("g_s1", 3), S("g_s2", 4), S("g_s3", 4), S("g_gc", 1)
        g_s4, g_s5 = S("g_s4", 1), S("g_s5", 2)
        g_sq, g_ss, g_ln, g_rs, g_nrm = S("g_sq", 8), S("g_ss", 8), S("g_ln", 8), S("g_rs", 8), S("g_nrm", 8)
        g_x, g_E, g_gl, g_kd0, g_kds = S("g_x", GH), S("g_E", GH), S("g_gl", GH), S("g_kd0", GH), S("g_kds", GH)
        g_xm, g_dec = S("g_xm", GH), S("g_dec", GH)
        g_bb, g_kk, g_qk, g_kt, g_vt = S("g_bb", GH), S("g_kk", GH), S("g_qk", GH), S("g_kt", GH), S("g_vt", GH)
        g_prep = S("g_prep", GH * 8)
        g_P, g_Pm = S("g_P", (LEVELS - 1) * GH), S("g_Pm", (LEVELS - 1) * GH)
        g_AB = S("g_AB", (LEVELS - 1) * GH)
        g_X, g_T = S("g_X", (LEVELS - 1) * GH), S("g_T", GH)
        g_XT = S("g_XT", (LEVELS + 1) * GH)
        g_wt, g_wts = S("g_wt", GH), S("g_wts", GH)
        g_v, g_vn, g_o, g_s, g_s0, g_su = S("g_v", TB), S("g_vn", TB), S("g_o", TB), S("g_s", TB - 1), S("g_s0", TB - 2), S("g_su", TB - 1)
        n_sq, n_ss, n_ln, n_rs, n_t = S("n_sq", GH), S("n_ss", GH), S("n_ln", GH), S("n_rs", GH), S("n_t", GH)
        g_sq_lo, n_sq_lo = S("g_sq_lo", QK_SPLIT), S("n_sq_lo", GH)
        g_tanh, tg_tanh = S("g_tanh", 4), S("tg_tanh", 1)
        m_hi, m_lo = S("m_hi", 8), S("m_lo", 8)

        def by(who):
            return {"act": act_took, "dve": dve_took, "x": x_new}[who]

        block = ctx.enter_context(nc.Block())

        @block.sync
        def _(sp):
            for i in range(4):
                sp.dma_start(x[:, 2 * i:2 * i + 2, :], xin[:, 2 * i:2 * i + 2, :]).then_inc(x_in[i], 16)
            sp.dma_start(con[:, 0:C_STAGED], cst[:, 0:C_STAGED]).then_inc(consts_in, 16)
            sp.dma_start(staged, cst[:, C_STAGED:C_LEVEL]).then_inc(consts_in, 16)
            for i in range(RAW):
                sp.dma_start(wraw[:, i, :], wt[0, i, :, :]).then_inc(w_in[i], 16)
            sp.wait_ge(w_lo.sem, 1)
            sp.dma_start(con[:, C_STAGED:], cst[:, C_LEVEL:C_DIFF]).then_inc(late_consts_in, 16)
            sp.dma_start(fing[:, :], fin).then_inc(late_consts_in, 16)
            with sp.Fori(1, DEPTH * NTILES // RAW) as r:
                for i in range(RAW):
                    sp.wait_ge(w_lo.sem, RAW * r + (i - RAW + 1))
                    sp.dma_start(wraw[:, i, :], wt[r, i, :, :]).then_inc(w_in[i], 16)
            for kb in range(KB):
                sp.wait_ge(*norm_t(DEPTH, kb + 1))
                sp.dma_start(out[:, kb, :], sq[:, kb, :]).then_inc(out_done, 16)
            sp.wait_ge(out_done, 16 * KB)

        @block.gpsimd
        def _(pool):
            with pool.Fori(0, DEPTH) as l:
                def split(t, i):
                    pool.wait_ge(*w_hi(l, t + 1))
                    nc.gpsimd.tensor_tensor(wlo[:, i, :], wraw[:, i, :], whi[:, i, :], ALU.subtract).then_inc(w_lo.sem, 1)

                split(0, 0)
                pool.wait_ge(*params_in(l, 32))
                pool.wait_ge(*ab_hi(l, 1))
                nc.gpsimd.tensor_tensor(abl[:, 0:KB * 8], abw, abh[:, 0:KB * 8], ALU.subtract).then_inc(*ab_lo.up())
                for kb in range(KB):
                    if kb not in VECTOR_LOW:
                        pool.wait_ge(*hn_hi(l, kb + 1))
                        nc.gpsimd.tensor_tensor(hnl[:, kb, :], sq[:, kb, :], hnh[:, kb, :], ALU.subtract).then_inc(*hn_lo_p.up())
                split(1, 1)
                with pool.Fori(1, NTILES // 2) as r:
                    for i in range(2):
                        pool.wait_ge(*blocks(l, 4 * r + (2 * i - 2)))
                        split(2 * r + i, i)

        @block.scalar
        def _(act):
            def cp(dst, src, scale=1.0):
                return act.activation(dst, src, ACT.Copy, scale=scale)

            def square(kb):
                act.activation(sq[:, kb, :], x[:, kb, :], ACT.Square).then_inc(*norm_sq.up())

            def rms(l):
                act.wait_ge(*norm_sum(l, 1))
                act.activation(rstd, mx[0][:, :], ACT.Ln, bias=eps[:, :], scale=-1.0 / D).then_inc(*norm_ln.up())
                act.wait_ge(*norm_ln(l, 1))
                act.activation(rstd, rstd, ACT.Exp, scale=-0.5).then_inc(*norm_rs.up())

            for kb in range(KB):
                if kb % 2 == 0:
                    act.wait_ge(x_in[kb // 2], 16)
                square(kb)
            act.wait_ge(consts_in, 32)
            for i, n in enumerate(("ntril", "nones")):
                src = zA[:, 0, CC[n] - C_STAGED:CC[n] - C_STAGED + P] if n in STAGED else const(n)
                cp(conr[:, i, :], src).then_inc(consts_up, 1)

            act.preload_act_table_set(LN_EXP)
            with act.Fori(0, DEPTH) as l:
                def hi(t):
                    if t >= 2:
                        act.wait_ge(*blocks(l, 2 * (t - 1)))
                    act.wait_ge(w_in[t % RAW], l * (16 * (NTILES // RAW)) + 16 * (t // RAW + 1))
                    cp(whi[:, t % 2, :], wraw[:, t % RAW, :]).then_inc(*w_hi.up())

                def ahead(t):
                    if t + 2 < NTILES:
                        hi(t + 2)

                def came(t, b=0):
                    act.wait_ge(*blocks(l, 2 * t + 2 if PLAN[t][0] != "branch" else 2 * t + 1 + b))
                    return pj[(BLOCK[t] + b) % 2]

                act.dma_start(prm[:, :], par[l, :, :]).then_inc(*params_in.up(16))
                act.dma_start(abw, wab[l, :, :]).then_inc(*params_in.up(16))
                act.dma_start(diff, cst[:, C_DIFF:C_END]).then_inc(*diff_in.up(16))
                hi(0)
                rms(l)
                act.wait_ge(*params_in(l, 32))
                cp(abh[:, 0:KB * 8], abw).then_inc(*ab_hi.up())
                hi(1)
                for kb in range(KB):
                    act.wait_ge(*norm_t(l, kb + 1))
                    cp(hnh[:, kb, :], sq[:, kb, :]).then_inc(*hn_hi.up())
                def small_first():
                    act.wait_ge(*g_s1(l, 3))
                    act.activation(sm[:, 3, :], sm[:, 1, :], ACT.Exp).then_inc(*g_s2.up())
                    act.activation(sm[:, 4, :], sm[:, 2, :], ACT.Exp).then_inc(*g_s2.up())
                    act.activation(sm[:, 5, :], prm[:, PAR["alog"]:PAR["alog"] + 16], ACT.Exp).then_inc(*g_s2.up())
                    act.wait_ge(*g_s2(l, 1))
                    act.activation(sm[:, 3, :], sm[:, 3, :], ACT.Ln, bias=1.0).then_inc(*g_s2.up())

                def small_last():
                    act.wait_ge(*g_s5(l, 1))
                    act.activation(sm[:, 9, :], mx[5][:, 0:16], ACT.Exp).then_inc(*g_s4.up())

                for t in range(0, 16):
                    what, i = PLAN[t]
                    if what not in TOKEN_MAJOR:
                        bank = came(t)
                        if what == "sbq":
                            if t == 0:
                                act.wait_ge(*hn_lo(l, 3))
                                act.wait_ge(*hn_lo_p(l, 5))
                            cp(sbq[:, i, :], bank[:, :], scale=SBD ** -0.5).then_inc(*act_took.up())
                        else:
                            cp(sbk[:, i, :], bank[:, :]).then_inc(*act_took.up())
                    ahead(t)
                    if t == 1:
                        act.wait_ge(*ab_cm(l, 1))
                        cp(abt, mx[4][:, :]).then_inc(*ab_t.up())
                    if t == 3:
                        small_first()
                    if t == 5:
                        small_last()
                    if t == FIRST["sbv"] + 3:
                        act.wait_ge(*sb_zero(l, 1))
                        for tb in range(TB):
                            act.wait_ge(*blocks(l, 2 * t + 1 + tb // 2))
                            v = mx[TOKEN_MAJOR["sbv"][tb]][:, :].rearrange("p (c e d) -> p c e d", e=2, d=SBD)
                            dst = vpad[:, tb, :, :].rearrange("p (c e) d -> p c e d", e=2)
                            cp(dst[:, :, 0, 0:SBD], v[:, :, 0, :])
                            cp(dst[:, :, 1, SBD:P], v[:, :, 1, :]).then_inc(*v_tm.up())

                def take(t):
                    what, i = PLAN[t]
                    if what in ("rq", "rk"):
                        j = i + (2 if what == "rk" else 0)
                        bank, scale = came(t), 0.125 if what == "rk" else 1.0
                        for p in range(0, P, 32):
                            q = p + 32 if p % 64 == 0 else p - 32
                            c = act.activation(rsw[p:p + 32, j, :], bank[q:q + 32, :], ACT.Copy,
                                               scale=-scale if p % 64 == 0 else scale)
                        c.then_inc(*r_swap.up())
                        cp(rrot[:, j, :], bank[:, :], scale=scale).then_inc(*act_took.up())
                    elif what == "gate":
                        if i >= 16:
                            cp(gates[:, i - 16, :], came(t)[:, :]).then_inc(*act_took.up())
                            ahead(t)
                            return
                        if i >= 10:
                            act.wait_ge(*mrg_acc(l, i - 9))
                        elif i >= 2:
                            n = BLOCK[SB_OUT + 3 * ((i - 2) // 2) + 2] + i % 2
                            act.wait_ge(*dve_took(l, TAKEN[n][1]))
                        act.activation(tg[:, i % 2, :], came(t)[:, :], ACT.Tanh, scale=0.5).then_inc(*act_took.up())
                    ahead(t)

                def sb_softplus(u):
                    j = u % 3
                    e = sbe[:, u % 2, 0:UNIT_W[j]]
                    act.wait_ge(*sb_min(l, u + 1))
                    act.activation(e, e, ACT.Exp).then_inc(*sb_e.up())
                    act.wait_ge(*sb_e(l, u + 1))
                    act.activation(e, e, ACT.Ln, bias=1.0).then_inc(*sb_l.up())

                def sb_weights(u):
                    j = u % 3
                    act.wait_ge(*sb_s(l, u + 1))
                    if u >= 2:
                        act.wait_ge(*sb_o(l, u - 1))
                    act.activation(sbw[:, u % 2, 0:UNIT_W[j]], mx[u % 5][:, 0:UNIT_W[j]], ACT.Exp).then_inc(*sb_w.up())

                def y_split(i, src, n):
                    act.wait_ge(*y_ready(l, n + 1))
                    cp(yh[:, i, :], src).then_inc(*y_hi.up())

                for u in range(NU + 2):
                    if u < NU:
                        sb_softplus(u)
                    if u >= 2:
                        sb_weights(u - 2)
                    if u >= 2 and u % 2 == 0:
                        take(16 + u // 2 - 1)

                def decay(h):
                    act.activation(rdec[:, h % 2, :], diff, ACT.Exp,
                                   scale=math.log(1.0 - 2.0 ** (-5.0 - h))).then_inc(*r_dec.up())

                act.wait_ge(*sb_s(l, NU))
                act.wait_ge(*diff_in(l, 16))
                decay(0)
                decay(1)
                act.wait_ge(*dve_took(l, 8))
                act.activation(zA[:, :, :], zA[:, :, :], ACT.Silu).then_inc(*silu_a.up())
                act.activation(zB[:, :, :], zB[:, :, :], ACT.Silu).then_inc(*silu_b.up())
                take(SB_OUT)
                for c in range(4):
                    y_split(c, zA[:, c, :], c)
                for h in range(RH):
                    if h:
                        take(SB_OUT + 3 * h)
                    act.wait_ge(*r_o(l, h + 1))
                    if h:
                        act.wait_ge(*r_var(l, h))
                    act.activation(part[:, 0, :], mx[3 + h % 2][:, :], ACT.Square)
                    act.activation(rsq[:, h % 2, :], mx[3 + h % 2][:, :], ACT.Square).then_inc(*r_sq.up())
                    take(SB_OUT + 3 * h + 1)
                    act.preload_act_table_set(LN_EXP)
                    if h + 2 < RH:
                        act.wait_ge(*r_sc(l, 3 * (h + 1)))
                        decay(h + 2)
                    act.wait_ge(*r_var(l, h + 1))
                    if h >= 2:
                        act.wait_ge(*r_y(l, h - 1))
                    act.activation(rrs[:, h % 2, :], mx[5][:, :], ACT.Ln, bias=eps[:, :], scale=-1.0 / P).then_inc(*r_ln.up())
                    act.wait_ge(*r_ln(l, h + 1))
                    act.activation(rrs[:, h % 2, :], rrs[:, h % 2, :], ACT.Exp, scale=-0.5).then_inc(*r_rs.up())
                    ahead(SB_OUT + 3 * h + 2)
                act.wait_ge(*blocks(l, 2 * (SB_OUT + 12)))
                for c in range(4):
                    y_split(c, zB[:, c, :], 4 + c)

                for t in range(FIRST["gqkv"], FIRST["gqkv"] + 12):
                    i = t - FIRST["gqkv"]
                    bank = came(t)
                    if i == 0:
                        act.wait_ge(*g_pad(l, 1))
                    if i >= 2:
                        act.wait_ge(*g_cv(l, 4 * (i - 1)))
                    cp(cin[:, i % 2, 3:3 + T], bank[:, :]).then_inc(*act_took.up())
                    ahead(t)
                    if i >= 1:
                        act.wait_ge(*g_cv(l, 4 * i))
                        act.activation(gqkv[:, i - 1, :], cacc[:, (i - 1) % 2, :], ACT.Silu).then_inc(*g_silu.up())
                    if 1 <= i <= 8:
                        n = i - 1
                        act.wait_ge(*g_silu(l, n + 1))
                        if n < QK_SPLIT:
                            if n:
                                act.wait_ge(*g_ss(l, n))
                            act.activation(part[:, 0, :], gqkv[:, n, :], ACT.Square)
                        act.activation(ed[:, n % 4, :], gqkv[:, n, :], ACT.Square).then_inc(*g_sq.up())
                act.wait_ge(*g_cv(l, 48))
                act.activation(gqkv[:, 11, :], cacc[:, 1, :], ACT.Silu).then_inc(*g_silu.up())
                act.preload_act_table_set(LN_EXP)
                for n in range(8):
                    if n and n % 2 == 0:
                        ahead(FIRST["gz"] + n // 2 - 1)
                    act.wait_ge(*g_ss(l, n + 1))
                    if n >= 2:
                        act.wait_ge(*g_nrm(l, n - 1))
                    act.activation(ed[:, n % 2, :], mx[n % 6][:, :], ACT.Ln, bias=eps[:, :], scale=-1.0).then_inc(*g_ln.up())
                    act.wait_ge(*g_ln(l, n + 1))
                    act.activation(ed[:, n % 2, :], ed[:, n % 2, :], ACT.Exp, scale=-0.5).then_inc(*g_rs.up())
                ahead(FIRST["gz"] + 3)
                act.wait_ge(*g_nrm(l, 8))
                def rs(h):
                    act.wait_ge(*n_ss(l, h + 1))
                    if h >= 2:
                        act.wait_ge(*n_t(l, h - 1))
                    act.activation(ed[:, 2 + h % 2, :], mx[h % 2][:, :], ACT.Ln, bias=eps[:, :], scale=-1.0 / P).then_inc(*n_ln.up())
                    act.wait_ge(*n_ln(l, h + 1))
                    act.activation(ed[:, 2 + h % 2, :], ed[:, 2 + h % 2, :], ACT.Exp, scale=-0.5).then_inc(*n_rs.up())

                for h in range(GH):
                    act.wait_ge(*g_x(l, h + 1))
                    if h >= 2:
                        act.wait_ge(*g_prep(l, 8 * (h - 1)))
                    act.activation(ed[:, h % 2, :], mx[0][:, :], ACT.Exp).then_inc(*g_E.up())
                    act.wait_ge(*g_kd0(l, h + 1))
                    act.activation(sm[:, 11, 4 * h:4 * h + 4], sm[:, 12, 4 * h:4 * h + 4], ACT.Exp).then_inc(*g_kds.up())
                    act.wait_ge(*g_xm(l, h + 1))
                    for tb in range(TB):
                        a = act.activation(ed[:, 2 + h % 2, tb * P:(tb + 1) * P], mx[0][:, tb * P:(tb + 1) * P], ACT.Exp,
                                           bias=sm[:, 8, 4 * h + tb:4 * h + tb + 1])
                    a.then_inc(*g_dec.up())
                    if h == 2:
                        ahead(RET_OUT)
                        cp(tg[:, 0, :], came(RET_OUT)[:, :]).then_inc(*act_took.up())
                cp(tg[:, 1, :], came(RET_OUT + 1)[:, :]).then_inc(*act_took.up())
                ahead(RET_OUT + 1)
                act.wait_ge(*dve_took(l, TAKEN[BLOCK[FIRST["gz"] + 3]][1]))
                act.wait_ge(*act_took(l, TAKEN[BLOCK[RET_OUT + 1]][1]))
                act.activation(tg[:, :, :], tg[:, :, :], ACT.Tanh, scale=0.5).then_inc(*tg_tanh.up())
                for step, n, h in INVERSE:
                    if step == "half" and h == 1:
                        take(n)
                    elif step == "turn":
                        act.wait_ge(*g_T(l, h + 1))
                        cp(gX[:, h, :], mx[3 * (h % 2) + 1][:, :]).then_inc(*g_X.up())
                    elif (step, n, h) == ("P", LEVELS - 1, 0):
                        act.activation(zA[:, :, :], zA[:, :, :], ACT.Silu).then_inc(*silu_a.up())
                for h in range(GH):
                    act.wait_ge(*g_wt(l, h + 1))
                    cp(gLT[:, h, :], mx[WT_BANK[h]][:, :], scale=-1.0).then_inc(*g_wts.up())
                for tb in range(TB):
                    act.wait_ge(*g_v(l, tb + 1))
                    if tb >= 1:
                        act.wait_ge(*g_o(l, tb))
                        act.wait_ge(*g_s(l, tb))
                    cp(ed[:, 2, :], mx[0][:, :]).then_inc(*g_vn.up())
                    if tb == 0:
                        act.preload_act_table_set(LN_EXP)
                    take(GATES + tb)

                def n_square(h):
                    act.wait_ge(*g_o(l, TB))
                    if h >= 2:
                        act.wait_ge(*n_sq_lo(l, h - 1))
                    act.activation(yh[:, h, :], mx[2 + h][:, :], ACT.Square)
                    act.activation(ed[:, h % 2, :], mx[2 + h][:, :], ACT.Square).then_inc(*n_sq.up())

                n_square(0)
                n_square(1)
                take(GATES + 4)
                rs(0)
                n_square(2)
                rs(1)
                n_square(3)
                take(GATES + 5)
                rs(2)
                rs(3)
                act.wait_ge(*blocks(l, 2 * (RET_OUT + 12)))
                y_split(0, zA[:, 0, :], 8)
                y_split(1, zA[:, 1, :], 9)
                take(GATES + 6)
                y_split(2, zA[:, 2, :], 10)
                y_split(3, zA[:, 3, :], 11)
                act.wait_ge(*act_took(l, TAKEN[BLOCK[GATES + 6]][1]))
                for i in range(2):
                    act.activation(gates[:, 2 * i:2 * i + 2, :], gates[:, 2 * i:2 * i + 2, :], ACT.Tanh, scale=0.5).then_inc(*g_tanh.up())
                take(GATES + 7)
                act.wait_ge(*act_took(l, TAKEN[BLOCK[GATES + 7]][1]))
                for i in range(2, 4):
                    act.activation(gates[:, 2 * i:2 * i + 2, :], gates[:, 2 * i:2 * i + 2, :], ACT.Tanh, scale=0.5).then_inc(*g_tanh.up())
                for g in range(4):
                    ahead(GDN_OUT + g)
                    for kb in (2 * g, 2 * g + 1):
                        act.wait_ge(*mrg_acc(l, 8 + kb + 1))
                        cp(hnh[:, kb, :], mrg[:, kb, :], scale=0.5).then_inc(*m_hi.up())
                act.preload_act_table_set(LN_EXP)
                for d in range(KB):
                    ahead(FIRST["wout"] + d)
                    act.wait_ge(*x_new(l, d + 1))
                    square(d)

            rms(DEPTH)

        @block.vector
        def _(dve):
            dve.memset(eps[:, :], EPS)
            dve.memset(abh[:, KB * 8:].bitcast(F32), 0.0)
            dve.memset(abl[:, KB * 8:].bitcast(F32), 0.0).then_inc(consts_up, 1)

            def norm_scale(l, g, kb):
                dve.scalar_tensor_tensor(out=sq[:, kb, :], in0=x[:, kb, :], scalar=g, in1=rstd,
                                         op0=ALU.mult, op1=ALU.mult).then_inc(*norm_t.up())

            def add_squares(l, kb):
                dve.wait_ge(*norm_sq(l, kb + 1))
                if kb == 1:
                    dve.tensor_tensor(ssq[:, :], sq[:, 0, :], sq[:, 1, :], ALU.add).then_inc(*norm_add.up())
                else:
                    dve.wait_ge(*norm_add(l, kb - 1))
                    dve.tensor_tensor(ssq[:, :], ssq[:, :], sq[:, kb, :], ALU.add).then_inc(*norm_add.up())

            for kb in range(1, KB - 1):
                add_squares(0, kb)

            with dve.Fori(0, DEPTH) as l:
                def came(t, b=0):
                    dve.wait_ge(*blocks(l, 2 * t + 2 if PLAN[t][0] != "branch" else 2 * t + 1 + b))
                    return pj[(BLOCK[t] + b) % 2]

                dve.wait_ge(*norm_rs(l, 1))
                dve.wait_ge(*params_in(l, 32))

                def hn_low(kb):
                    dve.wait_ge(*hn_hi(l, kb + 1))
                    dve.tensor_tensor(hnl[:, kb, :], sq[:, kb, :], hnh[:, kb, :], ALU.subtract).then_inc(*hn_lo.up())

                for kb in range(KB):
                    norm_scale(l, prm[:, PAR["norm"] + kb:PAR["norm"] + kb + 1], kb)
                    if kb - 1 in VECTOR_LOW:
                        hn_low(kb - 1)
                dve.wait_ge(*norm_t(l, KB))
                dve.memset(area(4096, 4096), 0.0).then_inc(*sb_zero.up())

                ab = blk(mx[5][:, :])

                def heads(ap):
                    return ap.rearrange("p (h t) -> p t h", h=GH)

                dve.wait_ge(*g_ab(l, 1))
                dve.tensor_tensor(heads(sm[:, 0, :]), ab[:, :, 4:8],
                                  heads(prm[:, PAR["dtb"]:PAR["dtb"] + 16]), ALU.add).then_inc(*g_s1.up())
                dve.tensor_scalar(heads(sm[:, 2, :]), ab[:, :, 0:4], -1.0, 80.0, ALU.mult, ALU.min).then_inc(*g_s1.up())
                dve.wait_ge(*g_s1(l, 1))
                dve.tensor_scalar(sm[:, 1, :], sm[:, 0, :], 40.0, None, ALU.min).then_inc(*g_s1.up())
                dve.wait_ge(*g_s2(l, 4))
                dve.tensor_tensor(sm[:, 6, :], sm[:, 3, :], sm[:, 0, :], ALU.max).then_inc(*g_s3.up())
                dve.tensor_scalar(sm[:, 4, :], sm[:, 4, :], 1.0, None, ALU.add).then_inc(*g_s3.up())
                dve.wait_ge(*g_s3(l, 1))
                dve.scalar_tensor_tensor(out=sm[:, 6, :], in0=sm[:, 6, :], scalar=-1.0, in1=sm[:, 5, :],
                                         op0=ALU.mult, op1=ALU.mult).then_inc(*g_s3.up())
                dve.wait_ge(*g_s3(l, 2))
                dve.reciprocal(sm[:, 7, :], sm[:, 4, :]).then_inc(*g_s3.up())
                dve.wait_ge(*g_gc(l, 1))
                dve.tensor_scalar(sm[:, 8, :], mx[5][:, 0:16], -1.0, None, ALU.mult).then_inc(*g_s5.up())
                dve.wait_ge(*g_s4(l, 1))
                dve.tensor_tensor(sm[:, 10, :], sm[:, 7, :], sm[:, 9, :], ALU.mult).then_inc(*g_s5.up())

                def take_z(t, dst):
                    bank = came(t)
                    dve.tensor_copy(dst[:, PLAN[t][1], :], bank[:, :]).then_inc(*dve_took.up())

                t = FIRST["rv"] + 3
                for tb in range(TB):
                    v = blk(mx[TOKEN_MAJOR["rv"][tb]][:, :])
                    col = slice(4 * tb, 4 * tb + 4)
                    dve.wait_ge(*blocks(l, 2 * t + 1 + tb // 2))
                    dve.tensor_reduce(sm[:, 12, col], v, mybir.AxisListType.X, ALU.add).then_inc(*rv_sum.up())
                    dve.wait_ge(*rv_sum(l, tb + 1))
                    dve.tensor_scalar(sm[:, 13, col], sm[:, 12, col], 1.0 / P, None, ALU.mult).then_inc(*rv_mean.up())
                    dve.wait_ge(*rv_mean(l, tb + 1))
                    dve.tensor_tensor(rv[:, :, tb * P:(tb + 1) * P], v,
                                      sm[:, 13, col].unsqueeze(2).broadcast_to((P, RH, P)), ALU.subtract).then_inc(*rv_tm.up())

                def sb_clamp(u):
                    j = u % 3
                    dve.wait_ge(*sb_z(l, u + 1))
                    n = len(UNITS[j])
                    diag = mx[u % 5][:, 0:P * n].rearrange("p (a b) -> p a b", a=n)
                    dve.tensor_tensor(diag, diag, const("negsb").unsqueeze(1).broadcast_to((P, n, P)), ALU.add)\
                       .then_inc(*sb_mask.up())
                    dve.wait_ge(*sb_mask(l, u + 1))
                    if u >= 2:
                        dve.wait_ge(*sb_sp(l, u - 1))
                    dve.tensor_scalar(sbe[:, u % 2, 0:UNIT_W[j]], mx[u % 5][:, 0:UNIT_W[j]], 40.0, None, ALU.min)\
                       .then_inc(*sb_min.up())

                def sb_softplus(u):
                    j, h = u % 3, u // 3
                    dve.wait_ge(*sb_l(l, u + 1))
                    e = sbe[:, u % 2, 0:UNIT_W[j]]
                    at = SP_AT[h % 2][UNITS[j][0][0]]
                    hi, lo = (v[:, at:at + UNIT_W[j]] for v in sp_parts)
                    dve.tensor_tensor(e, e, mx[u % 5][:, 0:UNIT_W[j]], ALU.max).then_inc(*sb_m.up())
                    if j == 2 and h:
                        dve.wait_ge(*sb_s(l, 3 * h))
                    elif h >= 2:
                        dve.wait_ge(*sb_s(l, 3 * (h - 1)))
                    dve.wait_ge(*sb_m(l, u + 1))
                    dve.tensor_copy(hi, e).then_inc(*sb_hi.up())
                    dve.wait_ge(*sb_hi(l, u + 1))
                    dve.tensor_tensor(lo, e, hi, ALU.subtract).then_inc(*sb_sp.up())

                def y_low(i, src, n):
                    dve.wait_ge(*y_hi(l, n + 1))
                    dve.tensor_tensor(yl[:, i, :], src, yh[:, i, :], ALU.subtract).then_inc(*y_lo.up())

                def rotary(i):
                    if i == 0:
                        dve.wait_ge(late_consts_in, 32)
                    dve.wait_ge(*r_swap(l, i + 1))
                    dve.tensor_tensor(rsw[:, i, :], rsw[:, i, :], sin, ALU.mult).then_inc(*rt1.up())
                    dve.wait_ge(*act_took(l, TAKEN[BLOCK[FIRST["rq"] + i]][1]))
                    dve.tensor_tensor(rrot[:, i, :], rrot[:, i, :], cos, ALU.mult).then_inc(*rt2.up())
                    dve.wait_ge(*rt1(l, i + 1))
                    dve.wait_ge(*rt2(l, i + 1))
                    dve.tensor_tensor(rrot[:, i, :], rrot[:, i, :], rsw[:, i, :], ALU.add).then_inc(*rrd.up())

                for u in range(NU + 2):
                    if u >= 9 and u % 6 == 3:
                        c = u // 6 - 1
                        dve.wait_ge(*sb_o(l, 6 * c + 6))
                        dve.tensor_copy(sby[:, c, :], mx[5][:, :]).then_inc(*sb_y.up())
                    if u < NU:
                        sb_clamp(u)
                    if 1 <= u <= NU:
                        sb_softplus(u - 1)
                    if u >= 2 and u % 2 == 0 and PLAN[16 + u // 2 - 1][0] in ("sbz", "rz"):
                        take_z(16 + u // 2 - 1, zA if u <= 8 else zB)
                    if u >= 15 and u % 2:
                        if u // 2 - 7 < 4:
                            rotary(u // 2 - 7)
                dve.wait_ge(*sb_o(l, NU))
                dve.tensor_copy(sby[:, 3, :], mx[5][:, :]).then_inc(*sb_y.up())

                def take_branch(t, b):
                    for i in range(2):
                        d = 2 * (PLAN[t][1] % 4) + i
                        bank = came(t, i)
                        gate = gates[:, d, :] if b == 2 else tg[:, i, :]
                        if b == 2:
                            dve.wait_ge(*g_tanh(l, d // 2 + 1))
                        else:
                            dve.wait_ge(*(tg_tanh(l, 1) if t == RET_OUT + 2 else act_took(l, TAKEN[BLOCK[t - 2 + i]][1])))
                        if b == 0:
                            dve.scalar_tensor_tensor(out=mrg[:, d, :], in0=tg[:, i, :], scalar=1.0, in1=bank[:, :],
                                                     op0=ALU.add, op1=ALU.mult).then_inc(*dve_took.up())
                            continue
                        dve.scalar_tensor_tensor(out=gate, in0=gate, scalar=1.0, in1=bank[:, :],
                                                 op0=ALU.add, op1=ALU.mult).then_inc(*dve_took.up())
                        dve.wait_ge(*dve_took(l, TAKEN[BLOCK[t] + i][1]))
                        dve.tensor_tensor(mrg[:, d, :], mrg[:, d, :], gate, ALU.add).then_inc(*mrg_acc.up())

                for h in range(RH):
                    dve.wait_ge(*r_dec(l, h + 1))
                    if h >= 2:
                        dve.wait_ge(*r_o(l, h - 1))
                    for j in range(3):
                        dve.wait_ge(*r_scores(l, 3 * h + j + 1))
                        for kb, at in UNITS[j]:
                            w = WIDTH[kb]
                            d = dve.tensor_tensor(rsc[:, h % 2, UNIT_AT[j] + at:UNIT_AT[j] + at + w],
                                                  mx[j][:, at:at + w], rdec[:, h % 2, 0:w], ALU.mult)
                        d.then_inc(*r_sc.up())
                    if h == 0:
                        dve.wait_ge(*silu_a(l, 1))
                        dve.wait_ge(*sb_y(l, 4))
                        for c in range(4):
                            dve.tensor_tensor(zA[:, c, :], sby[:, c, :], zA[:, c, :], ALU.mult).then_inc(*y_ready.up())
                    dve.wait_ge(*r_sq(l, h + 1))
                    dve.tensor_tensor(part[:, 1, :], rsq[:, h % 2, :], part[:, 0, :], ALU.subtract).then_inc(*r_sq_lo.up())
                    if h == 0:
                        for c in range(4):
                            y_low(c, zA[:, c, :], c)
                    take_branch(SB_OUT + 3 * h + 2, 0)
                    dve.wait_ge(*r_rs(l, h + 1))
                    dve.tensor_tensor(ro[:, h % 2, :], mx[3 + h % 2][:, :], rrs[:, h % 2, :], ALU.mult).then_inc(*r_y.up())
                    dve.wait_ge(*r_y(l, h + 1))
                    if h == 0:
                        dve.wait_ge(*silu_b(l, 1))
                    dve.tensor_tensor(zB[:, h, :], ro[:, h % 2, :], zB[:, h, :], ALU.mult).then_inc(*y_ready.up())
                dve.wait_ge(*y_ready(l, 8))
                dve.memset(cin[:, :, 0:3], 0.0).then_inc(*g_pad.up())
                for c in range(4):
                    y_low(c, zB[:, c, :], 4 + c)

                for i in range(12):
                    dve.wait_ge(*act_took(l, TAKEN[BLOCK[FIRST["gqkv"] + i]][1]))
                    if i >= 2:
                        dve.wait_ge(*g_silu(l, i - 1))
                    for j in range(4):
                        w = prm[:, PAR["conv"] + 4 * i + j:PAR["conv"] + 4 * i + j + 1]
                        if j == 0:
                            dve.tensor_scalar(cacc[:, i % 2, :], cin[:, i % 2, 0:T], w, None, ALU.mult).then_inc(*g_cv.up())
                        else:
                            dve.wait_ge(*g_cv(l, 4 * i + j))
                            dve.scalar_tensor_tensor(out=cacc[:, i % 2, :], in0=cin[:, i % 2, j:j + T], scalar=w,
                                                     in1=cacc[:, i % 2, :], op0=ALU.mult, op1=ALU.add).then_inc(*g_cv.up())
                    if 1 <= i <= QK_SPLIT:
                        dve.wait_ge(*g_sq(l, i))
                        dve.tensor_tensor(part[:, 1, :], ed[:, (i - 1) % 4, :], part[:, 0, :], ALU.subtract)\
                           .then_inc(*g_sq_lo.up())
                for n in range(8):
                    if n and n % 2 == 0:
                        take_z(FIRST["gz"] + n // 2 - 1, zA)
                    dve.wait_ge(*g_rs(l, n + 1))
                    dve.scalar_tensor_tensor(out=gqkv[:, n, :], in0=gqkv[:, n, :], scalar=P ** -0.5 if n < 4 else 1.0,
                                             in1=ed[:, n % 2, :], op0=ALU.mult, op1=ALU.mult).then_inc(*g_nrm.up())

                take_z(FIRST["gz"] + 3, zA)

                def wide(ap):
                    return ap.unsqueeze(2).broadcast_to((P, TB, P))

                def rep(ap):
                    return ap.unsqueeze(1).broadcast_to((P, TB, P))

                def turn(h):
                    dve.transpose(gX[:, h, :], gXT[:, h, :]).then_inc(*g_X.up())

                for h in range(GH):
                    col = slice(4 * h, 4 * h + 4)
                    E, dec = ed[:, h % 2, :], ed[:, 2 + h % 2, :]
                    dve.wait_ge(*g_x(l, h + 1))
                    dve.wait_ge(*g_E(l, h + 1))
                    dve.tensor_copy(sm[:, 13, col], blk(mx[0][:, :])[:, :, P - 1]).then_inc(*g_gl.up())
                    dve.wait_ge(*g_gl(l, h + 1))
                    dve.tensor_tensor(blk(mx[0][:, :]), blk(mx[0][:, :]), rep(const("neggdn")), ALU.add).then_inc(*g_xm.up())
                    dve.tensor_tensor(sm[:, 12, col], sm[:, 13, col], sm[:, 8, col], ALU.add).then_inc(*g_kd0.up())
                    dve.tensor_copy(gel[:, h, :], blk(E)[:, :, P - 1]).then_inc(*g_prep.up())
                    dve.wait_ge(*g_kt(l, h + 1))
                    dve.tensor_tensor(blk(kbg[:, h, :]), blk(mx[4][:, :]), wide(sm[:, 10, col]), ALU.mult).then_inc(*g_prep.up())
                    dve.wait_ge(*g_qk(l, h + 1))
                    dve.wait_ge(*g_kds(l, h + 1))
                    dve.tensor_tensor(blk(gk[:, h, :]), blk(mx[4][:, :]), wide(sm[:, 11, col]), ALU.mult).then_inc(*g_prep.up())
                    dve.wait_ge(*g_vt(l, h + 1))
                    dve.tensor_tensor(blk(gv[:, h, :]), blk(mx[5][:, :]), wide(sm[:, 7, col]), ALU.mult).then_inc(*g_prep.up())
                    dve.tensor_tensor(gq[:, h, :], gq[:, h, :], E, ALU.mult).then_inc(*g_prep.up())
                    dve.wait_ge(*g_dec(l, h + 1))
                    dve.tensor_tensor(gLT[:, h, :], mx[2][:, :], dec, ALU.mult).then_inc(*g_prep.up())
                    dve.tensor_tensor(gsc[:, h, :], mx[3][:, :], dec, ALU.mult).then_inc(*g_prep.up())
                    dve.wait_ge(*g_prep(l, 8 * h + 6))
                    dve.wait_ge(*g_bb(l, h + 1))
                    dve.tensor_tensor(gLT[:, h, :], gLT[:, h, :], mx[1][:, :], ALU.mult).then_inc(*g_prep.up())
                    dve.wait_ge(*g_prep(l, 8 * h + 8))
                    dve.tensor_tensor(blk(gXT[:, h, :]), blk(gLT[:, h, :]), rep(const("m1t")), ALU.mult).then_inc(*g_XT.up())
                    dve.wait_ge(*g_XT(l, 2 * h + 1))
                    dve.tensor_tensor(blk(gXT[:, h, :]), rep(ident), blk(gXT[:, h, :]), ALU.subtract).then_inc(*g_XT.up())
                    dve.wait_ge(*g_XT(l, 2 * h + 2))
                    turn(h)


                for step, n, h in INVERSE:
                    if step == "half" and h == 1 and PLAN[n][0] == "branch":
                        take_branch(n, 1)
                    elif step == "P":
                        mask = rep(late(C_LEVEL + P * (n - 1), P))
                        dve.wait_ge(*g_P(l, GH * (n - 1) + h + 1))
                        if n > 1 or h >= 2:
                            dve.wait_ge(*g_AB(l, GH * (n - 1) + h - 1))
                        dve.tensor_tensor(blk(ed[:, h % 2, :]), blk(mx[3 * (h % 2)][:, :]), mask, ALU.mult).then_inc(*g_Pm.up())
                    elif step == "AB":
                        dve.wait_ge(*g_AB(l, GH * (n - 1) + h + 1))
                        new = subs(gXT[:, h, :], n, 1)
                        dve.tensor_tensor(new, new, subs(mx[3 * (h % 2) + 2][:, :], n, 1), ALU.subtract).then_inc(*g_XT.up())
                        if n < WIDE:
                            dve.wait_ge(*g_XT(l, GH * (n + 1) + h + 1))
                            turn(h)
                for tb in range(TB - 1):
                    dve.wait_ge(*g_s(l, tb + 1))
                    if tb == 0:
                        dve.tensor_copy(gS[:, :, :], blk(mx[1][:, :])).then_inc(*g_su.up())
                    else:
                        dve.tensor_tensor(gS[:, :, :], gS[:, :, :], gel[:, :, tb].unsqueeze(2).broadcast_to((P, GH, P)),
                                          ALU.mult).then_inc(*g_s0.up())
                        dve.wait_ge(*g_s0(l, tb))
                        dve.tensor_tensor(gS[:, :, :], gS[:, :, :], blk(mx[1][:, :]), ALU.add).then_inc(*g_su.up())
                def n_low(h):
                    dve.wait_ge(*n_sq(l, h + 1))
                    dve.tensor_tensor(yl[:, h, :], ed[:, h % 2, :], yh[:, h, :], ALU.subtract).then_inc(*n_sq_lo.up())

                n_low(0)
                for h in range(GH):
                    if h + 1 < GH:
                        n_low(h + 1)
                    dve.wait_ge(*n_rs(l, h + 1))
                    dve.scalar_tensor_tensor(out=gXT[:, h, :], in0=mx[2 + h][:, :], scalar=prm[:, PAR["gain"]:PAR["gain"] + 1],
                                             in1=ed[:, 2 + h % 2, :], op0=ALU.mult, op1=ALU.mult).then_inc(*n_t.up())
                    dve.wait_ge(*n_t(l, h + 1))
                    if h == 0:
                        dve.wait_ge(*silu_a(l, 2))
                    dve.tensor_tensor(zA[:, h, :], gXT[:, h, :], zA[:, h, :], ALU.mult).then_inc(*y_ready.up())
                for h in range(GH):
                    y_low(h, zA[:, h, :], 8 + h)
                def merged_low(kb):
                    dve.wait_ge(*m_hi(l, kb + 1))
                    dve.scalar_tensor_tensor(out=hnl[:, kb, :], in0=mrg[:, kb, :], scalar=0.5, in1=hnh[:, kb, :],
                                             op0=ALU.mult, op1=ALU.subtract).then_inc(*m_lo.up())

                for g in range(4):
                    take_branch(GDN_OUT + g, 2)
                    if g:
                        merged_low(2 * g - 2)
                        merged_low(2 * g - 1)
                merged_low(6)
                merged_low(7)
                for d in range(KB):
                    bank = came(FIRST["wout"] + d)
                    dve.tensor_tensor(x[:, d, :], x[:, d, :], bank[:, :], ALU.add).then_inc(*x_new.up())
                    if d >= 2:
                        add_squares(l + 1, d - 1)

            dve.wait_ge(*norm_rs(DEPTH, 1))
            dve.wait_ge(late_consts_in, 32)
            for kb in range(KB):
                norm_scale(DEPTH, fing[:, kb:kb + 1], kb)

        @block.tensor
        def _(pe):
            def mm(o, w, a, start, stop):
                return pe.matmul(o, w, a, start=start, stop=stop, skip_group_check=True)

            def mm3(o, w, a, start, stop):
                mm(o, w[0], a[0], start, False)
                mm(o, w[0], a[1], False, False)
                return mm(o, w[1], a[0], False, stop)

            def mm3_split(o, w, a, start):
                mm(o, w[0], a[0], start, False)
                mm(o, w[1], a[0], False, False)

            def minus_sum(bank, parts):
                mm(bank[:, :], nones_r, parts[0], True, False)
                return mm(bank[:, :], nones_r, parts[1], False, True)

            def square_sum(l):
                pe.wait_ge(*norm_add(l, KB - 2))
                mm(mx[0][:, :], const("nones"), ssq[:, :], True, False)
                pe.wait_ge(*norm_sq(l, KB))
                mm(mx[0][:, :], const("nones"), sq[:, KB - 1, :], False, True).then_inc(*norm_sum.up())

            pe.wait_ge(consts_in, 32)
            pe.wait_ge(consts_up, 3)
            square_sum(0)
            with pe.Fori(0, DEPTH) as l:
                def wpair(t, a, b, kn, n):
                    s = t % 2
                    return [w[:, s, :].rearrange("p (k n) -> p k n", k=kn)[:, a, b:b + n] for w in (whi, wlo)]

                def hn(kb, c0=0, n=T):
                    return [hnh[:, kb, c0:c0 + n], hnl[:, kb, c0:c0 + n]]

                def free(n):
                    if n >= 2:
                        who, k = TAKEN[n - 2]
                        pe.wait_ge(*by(who)(l, k))

                def half(t, b):
                    what, i = PLAN[t]
                    n = BLOCK[t]
                    if b == 0:
                        pe.wait_ge(*w_hi(l, t + 1))
                        pe.wait_ge(*w_lo(l, t + 1))
                    if what == "branch":
                        free(n + b)
                        for c in range(4):
                            if i % 4 == 0 and b == 0:
                                pe.wait_ge(*y_lo(l, i + c + 1))
                            m = mm3(pj[(n + b) % 2][:, :], wpair(t, c, P * b, 4, P), [yh[:, c, :], yl[:, c, :]], c == 0, c == 3)
                        m.then_inc(*blocks.up())
                        return
                    if what in TOKEN_MAJOR:
                        w = wpair(t, slice(0, 2), 0, 2, T)
                        for tb in (2 * b, 2 * b + 1):
                            if what == "rv" and i == 0 and tb == 1:
                                pe.wait_ge(*g_s4(l, 1))
                            if what == "rv" and i == 0 and tb >= 2:
                                pe.wait_ge(*v_tm(l, tb + 1))
                            for k in range(2):
                                m = mm3(mx[TOKEN_MAJOR[what][tb]][:, :], hn(2 * i + k, tb * P, P), [v[:, k, :] for v in w],
                                        i == 0 and k == 0, i == 3 and k == 1)
                        m.then_inc(*blocks.up())
                        return
                    if b == 0:
                        free(n)
                    for kb in range(4 * b, 4 * b + 4):
                        if t == 0:
                            low = [k for k in range(kb + 1) if (k in VECTOR_LOW) == (kb in VECTOR_LOW)]
                            pe.wait_ge(*hn_hi(l, kb + 1))
                            mm3_split(pj[n % 2][:, :], wpair(t, kb, 0, KB, P), hn(kb), kb == 0)
                            if kb == 0:
                                pe.wait_ge(*ab_lo(l, 1))
                            wab_kb = [w[:, 8 * kb:8 * kb + P] for w in (abh, abl)]
                            mm3_split(mx[4][:, :], wab_kb, hn(kb), kb == 0)
                            pe.wait_ge(*(hn_lo if kb in VECTOR_LOW else hn_lo_p)(l, len(low)))
                            m = mm(pj[n % 2][:, :], wpair(t, kb, 0, KB, P)[0], hn(kb)[1], False, kb == KB - 1)
                            ab = mm(mx[4][:, :], wab_kb[0], hn(kb)[1], False, kb == KB - 1)
                            continue
                        if t == FIRST["wout"]:
                            pe.wait_ge(*m_lo(l, kb + 1))
                        m = mm3(pj[n % 2][:, :], wpair(t, kb, 0, KB, P), hn(kb), kb == 0, kb == KB - 1)
                    if b == 1:
                        m.then_inc(*blocks.up(2))
                    if t == 0 and b == 1:
                        ab.then_inc(*ab_cm.up())

                def tile(t):
                    half(t, 0)
                    half(t, 1)

                def four_turned(bank, src):
                    for tb in range(TB):
                        m = pe.transpose(bank[:, tb * P:(tb + 1) * P], src[:, tb * P:(tb + 1) * P], ident)
                    return m

                tile(0)
                tile(1)
                half(2, 0)
                pe.wait_ge(*ab_t(l, 1))
                four_turned(mx[5], abt).then_inc(*g_ab.up())
                half(2, 1)
                for t in range(3, 5):
                    tile(t)
                pe.wait_ge(*g_s3(l, 4))
                mm(mx[5][:, 0:16], const("triu"), sm[:, 6, :], True, True).then_inc(*g_gc.up())
                for t in range(5, 16):
                    tile(t)

                def sb_scores(u):
                    h, j = divmod(u, 3)
                    c, po = h // 2, SBD * (h % 2)
                    if u == 0:
                        pe.wait_ge(*v_tm(l, 4))
                    if u == 2:
                        pe.wait_ge(*rv_tm(l, 4))
                    if u >= 5:
                        pe.wait_ge(*sb_w(l, u - 4))
                    bank = mx[u % 5]
                    for n, (kb, at) in enumerate(UNITS[j]):
                        m = mm(bank[:, at:at + WIDTH[kb]], sbk[po:po + SBD, c, kb * P:(kb + 1) * P],
                               sbq[po:po + SBD, c, kb * P:T], n == 0, False)
                    m.then_inc(*sb_z.up())

                def sb_sums(u):
                    h, j = divmod(u, 3)
                    pe.wait_ge(*sb_sp(l, u + 1))
                    bank = mx[u % 5]
                    for kb, at in UNITS[j]:
                        for k2 in range(kb, TB):
                            lo = at + P * (k2 - kb)
                            for i in range(2):
                                m = mm(bank[:, lo:at + WIDTH[kb]], ntril_r if k2 == kb else nones_r,
                                       sp_parts[i][:, SP_AT[h % 2][k2]:SP_AT[h % 2][k2] + WIDTH[k2]], False,
                                       k2 == TB - 1 and i == 1)
                    m.then_inc(*sb_s.up())

                def sb_out(u):
                    h, j = divmod(u, 3)
                    pe.wait_ge(*sb_w(l, u + 1))
                    if u % 6 == 0 and u:
                        pe.wait_ge(*sb_y(l, u // 6))
                    for n, (kb, at) in enumerate(UNITS[j]):
                        m = mm(mx[5][:, kb * P:T], vpad[:, kb, h, :], sbw[:, u % 2, at:at + WIDTH[kb]],
                               u % 6 == 0 and n == 0, u % 6 == 5)
                    m.then_inc(*sb_o.up())

                for u in range(NU + 3):
                    if u < NU:
                        sb_scores(u)
                        half(16 + u // 2, u % 2)
                    if 2 <= u < NU + 2:
                        sb_sums(u - 2)
                    if u >= 3:
                        sb_out(u - 3)

                tile(SB_OUT)
                for h in range(RH):
                    c, po = h // 2, 64 * (h % 2)
                    t = SB_OUT + 3 * h
                    pe.wait_ge(*rrd(l, 4))
                    for j in range(3):
                        pe.wait_ge(*(r_sc(l, 3 * (h - 1) + j + 1) if h else sb_w(l, NU)))
                        for n, (kb, at) in enumerate(UNITS[j]):
                            m = mm(mx[j][:, at:at + WIDTH[kb]], rrot[po:po + 64, 2 + c, kb * P:(kb + 1) * P],
                                   rrot[po:po + 64, c, kb * P:T], n == 0, True)
                        m.then_inc(*r_scores.up())
                    half(t if h else t + 1, 0)
                    if h:
                        half(t, 1)
                    pe.wait_ge(*r_sc(l, 3 * h + 3))
                    if h >= 2:
                        pe.wait_ge(*r_y(l, h - 1))
                    for kb in range(TB):
                        m = mm(mx[3 + h % 2][:, kb * P:T], rv[:, h, kb * P:(kb + 1) * P],
                               rsc[:, h % 2, SC_AT[kb]:SC_AT[kb] + WIDTH[kb]], kb == 0, kb == TB - 1)
                    m.then_inc(*r_o.up())
                    if h:
                        half(t + 1, 0)
                    half(t + 1, 1)
                    pe.wait_ge(*r_sq_lo(l, h + 1))
                    pe.wait_ge(*(r_ln(l, h) if h else sb_y(l, 4)))
                    minus_sum(mx[5], (part[:, 0, :], part[:, 1, :])).then_inc(*r_var.up())
                    tile(t + 2)

                def qk_sum(n):
                    if n < QK_SPLIT:
                        pe.wait_ge(*g_sq_lo(l, n + 1))
                        minus_sum(mx[n], (part[:, 0, :], part[:, 1, :])).then_inc(*g_ss.up())
                        return
                    pe.wait_ge(*g_sq(l, n + 1))
                    pe.wait_ge(*g_ln(l, n - QK_SPLIT + 1))
                    mm(mx[n - QK_SPLIT][:, :], const("nones"), ed[:, n % 4, :], True, True).then_inc(*g_ss.up())

                for i in range(12):
                    tile(FIRST["gqkv"] + i)
                    if 2 <= i < 2 + QK_SPLIT:
                        qk_sum(i - 2)
                for i in range(4):
                    tile(FIRST["gz"] + i)
                    if i == 1:
                        qk_sum(6)
                        qk_sum(7)
                pe.wait_ge(*g_nrm(l, 8))
                pe.wait_ge(*g_s5(l, 2))
                for h in range(GH):
                    def four(bank, lhs, rhs):
                        for tb in range(TB):
                            m = mm(bank[:, tb * P:(tb + 1) * P], lhs(tb), rhs(tb), tb == 0, True)
                        return m

                    def tok(buf):
                        return lambda tb: buf[:, h, tb * P:(tb + 1) * P]

                    def spread(row):
                        return lambda tb: sm[:, row, 4 * h + tb:4 * h + tb + 1].broadcast_to((P, P))

                    if h:
                        pe.wait_ge(*g_dec(l, h))
                    four(mx[0], spread(6), lambda tb: const("triu")).then_inc(*g_x.up())
                    if h:
                        pe.wait_ge(*g_prep(l, 8 * h))
                    for tb in range(TB):
                        m = pe.transpose(mx[1][:, tb * P:(tb + 1) * P], spread(7)(tb), ident)
                    m.then_inc(*g_bb.up())
                    four(mx[2], tok(gk), tok(gk)).then_inc(*g_kk.up())
                    for tb in range(TB):
                        m = pe.transpose(mx[4][:, tb * P:(tb + 1) * P], gk[:, h, tb * P:(tb + 1) * P], ident)
                    m.then_inc(*g_kt.up())
                    four(mx[3], tok(gk), tok(gq)).then_inc(*g_qk.up())
                    for tb in range(TB):
                        m = pe.transpose(mx[5][:, tb * P:(tb + 1) * P], gv[:, h, tb * P:(tb + 1) * P], ident)
                    m.then_inc(*g_vt.up())
                    half(RET_OUT + h // 2, h % 2)

                def four_sub(bank, lhs, src, lv, odd):
                    for tb in range(TB):
                        m = mm(subs(bank[:, tb * P:(tb + 1) * P], lv, odd), lhs(tb),
                               subs(src[:, tb * P:(tb + 1) * P], lv, odd), tb == 0, True)
                    return m

                for step, n, h in INVERSE:
                    if step == "half":
                        half(n, h)
                        continue
                    lv, b = n, 3 * (h % 2)
                    tok_h = (lambda buf, h=h: lambda tb: buf[:, h, tb * P:(tb + 1) * P])
                    if step == "P":
                        if (lv, h) == (1, 0):
                            pe.wait_ge(*g_prep(l, 8 * GH))
                        pe.wait_ge(*g_X(l, GH * (lv - 1) + h + 1))
                        if lv > 1 or h >= 2:
                            pe.wait_ge(*g_Pm(l, GH * (lv - 1) + h - 1))
                        four_sub(mx[b], tok_h(gLT), gX[:, h, :], lv, 0).then_inc(*g_P.up())
                    elif step == "AB":
                        pe.wait_ge(*g_Pm(l, GH * (lv - 1) + h + 1))
                        pe.wait_ge(*g_XT(l, GH * lv + h + (3 if h < 2 else 1)))
                        if h >= 2:
                            pe.wait_ge(*g_XT(l, GH * (lv + 1) + h - 1))
                        pm = (lambda tb, h=h: ed[:, h % 2, tb * P:(tb + 1) * P])
                        four_sub(mx[b + 2], pm, gXT[:, h, :], lv, 1).then_inc(*g_AB.up())
                    else:
                        pe.wait_ge(*g_XT(l, GH * (lv + 1) + h + 1))
                        if h >= 2:
                            pe.wait_ge(*g_X(l, GH * lv + h - 1))
                        four_turned(mx[b + 1], gXT[:, h, :]).then_inc(*g_T.up())
                for h in range(GH):
                    pe.wait_ge(*g_XT(l, GH * LEVELS + h + 1))
                    if h < 2:
                        pe.wait_ge(*g_Pm(l, GH * (LEVELS - 1) - 1 + h))
                    tok_h = (lambda buf, h=h: lambda tb: buf[:, h, tb * P:(tb + 1) * P])
                    four(mx[WT_BANK[h]], tok_h(kbg), tok_h(gXT)).then_inc(*g_wt.up())
                pe.wait_ge(*g_wts(l, 1))
                for tb in range(TB):
                    s = slice(tb * P, (tb + 1) * P)
                    if tb:
                        pe.wait_ge(*g_vn(l, tb))
                        pe.wait_ge(*g_su(l, tb))
                    for h in range(GH):
                        hs = slice(h * P, (h + 1) * P)
                        m = mm(mx[0][:, hs], gXT[:, h, s], gv[:, h, s], True, tb == 0)
                        if tb:
                            m = mm(mx[0][:, hs], gLT[:, h, s], gS[:, h, :], False, True)
                    m.then_inc(*g_v.up())
                    half(GATES + tb, 0)
                    if tb == 0:
                        pe.wait_ge(*g_wts(l, GH))
                    if tb:
                        for h in range(GH):
                            mm(mx[2 + h][:, s], gS[:, h, :], gq[:, h, s], True, False)
                    pe.wait_ge(*g_vn(l, tb + 1))
                    if tb < TB - 1:
                        for h in range(GH):
                            m = mm(mx[1][:, h * P:(h + 1) * P], gk[:, h, s], ed[:, 2, h * P:(h + 1) * P], True, True)
                        m.then_inc(*g_s.up())
                    for h in range(GH):
                        m = mm(mx[2 + h][:, s], ed[:, 2, h * P:(h + 1) * P], gsc[:, h, s], tb == 0, True)
                    m.then_inc(*g_o.up())
                    half(GATES + tb, 1)
                tile(GATES + 4)
                for h in range(GH):
                    pe.wait_ge(*n_sq_lo(l, h + 1))
                    if h >= 2:
                        pe.wait_ge(*n_ln(l, h - 1))
                    minus_sum(mx[h % 2], (yh[:, h, :], yl[:, h, :])).then_inc(*n_ss.up())
                    half(GATES + 5 + h // 2, h % 2)
                tile(GATES + 7)
                for t in range(GDN_OUT, FIRST["wout"]):
                    tile(t)
                for t in range(FIRST["wout"], NTILES):
                    tile(t)
                square_sum(l + 1)

        for s in sigs:
            extra = {"norm_sq": KB, "norm_sum": 1, "norm_ln": 1, "norm_rs": 1, "norm_t": KB, "norm_add": KB - 2}.get(s.name, 0)
            want = {"w_lo": 0}.get(s.name, s.per_layer)
            assert s.n == want + extra, (s.name, s.n, s.per_layer)


def layout(inputs):
    a = {k: np.asarray(v) for k, v in inputs.items()}
    xin = np.ascontiguousarray(a["x"][0].T.reshape(KB, P, T).transpose(1, 0, 2))
    wt = np.empty((DEPTH, NTILES, P, TILE), np.float32)
    branches = (a["w_sb"], a["w_ret"], a["w_gdn"])
    for t, (what, i) in enumerate(PLAN):
        if what == "branch":
            src = branches[i // 4][:, :, 256 * (i % 4):256 * (i % 4) + 256]
        elif what == "wout":
            src = a["w_out"][:, :, P * i:P * (i + 1)]
        elif what in TOKEN_MAJOR:
            src = a["w_in"][:, 2 * P * i:2 * P * (i + 1), OFF[what]:OFF[what] + T]
        else:
            src = a["w_in"][:, :, OFF[what] + P * i:OFF[what] + P * (i + 1)]
        k = src.shape[1] // P
        wt[:, t] = src.reshape(DEPTH, k, P, -1).transpose(0, 2, 1, 3).reshape(DEPTH, P, TILE)
    wab = np.ascontiguousarray(a["w_in"][:, :, OFF["gab"]:OFF["gab"] + 8].reshape(DEPTH, KB, P, 8)
                               .transpose(0, 2, 1, 3).reshape(DEPTH, P, KB * 8))
    par = np.empty((DEPTH, P, PAR_END), np.float32)
    par[:, :, 0:8] = a["norm_g"].reshape(DEPTH, KB, P).transpose(0, 2, 1)
    par[:, :, 8:56] = a["conv_w"].reshape(DEPTH, 4, 12, P).transpose(0, 3, 2, 1).reshape(DEPTH, P, 48)
    par[:, :, 56] = a["gdn_norm_g"]
    par[:, :, 57:73] = np.repeat(a["dt_bias"], TB, axis=1)[:, None, :]
    par[:, :, 73:89] = np.repeat(a["a_log"], TB, axis=1)[:, None, :]
    return {"xin": xin, "wt": wt.reshape(DEPTH * NTILES // RAW, RAW, P, TILE), "wab": wab, "par": par,
            "fin": np.ascontiguousarray(a["final_g"].reshape(KB, P).T), "cst": constants()}


def kernel(**inputs):
    import concourse.bacc as _bacc
    from concourse.bass_utils import run_bass_kernel_spmd as _run

    arrays = layout(inputs)
    nc = _bacc.Bacc("TRN2", target_bir_lowering=False, num_devices=1)
    args = [nc.dram_tensor(n, v.shape, mybir.dt.float32, kind="ExternalInput").ap() for n, v in arrays.items()]
    args.append(nc.dram_tensor("out", (P, KB, T), mybir.dt.float32, kind="ExternalOutput").ap())
    trunk(nc, *args)
    r = _run(nc, [arrays], core_ids=[0])
    got = r.results[0]["out"]
    return np.ascontiguousarray(got.transpose(1, 0, 2).reshape(D, T).T)[None]
```
